# Optimizing a Trainium2 kernel written in Bass

```python
import jax, jax.numpy as jnp
from jax import lax
import numpy as np

D_MODEL = 1024
BATCH = 1
SEQ = 256
DEPTH = 1
DEC_BATCH = 1
DEC_SEQ = 2048
PAST_LEN = 512

GRID_W = 64
N_HEADS = 8
QK_NOPE = 64
QK_ROPE = 32
V_HEAD = 64
Q_LORA = 256
KV_LORA = 128
ATTN_W = N_HEADS * V_HEAD
FNET_GROUPS = 8
FNET_CH = 64
FNET_W = FNET_GROUPS * FNET_CH
MIX_W = ATTN_W + FNET_W
IN_W = Q_LORA + KV_LORA + QK_ROPE + FNET_W
N_EXPERTS = 16
CAP_FACTOR = 2
D_EXPERT = 512
ROPE_BASE = 10000.0
EPS = 1e-6
Q_BLOCK = 128

kernel_name = 'hybrid_mla_fnet_ecmoe_diffusion_step'

def rmsnorm(x, g):
    xf = x.astype(jnp.float32)
    out = xf * lax.rsqrt(jnp.mean(xf * xf, axis=-1, keepdims=True) + EPS)
    return (out * g.astype(jnp.float32)).astype(x.dtype)

def adaln(cvec, w_mod, b_mod):
    m = jax.nn.silu(cvec) @ w_mod + b_mod
    return [t[:, None, :] for t in jnp.split(m, 6, axis=-1)]

def modulate(h, shift, scale):
    return h * (1.0 + scale) + shift

def rope_angles(n_tokens):
    n_rows = n_tokens // GRID_W
    rows = jnp.repeat(jnp.arange(n_rows, dtype=jnp.float32), GRID_W)
    cols = jnp.tile(jnp.arange(GRID_W, dtype=jnp.float32), n_rows)
    n_freq = QK_ROPE // 4
    inv_freq = ROPE_BASE ** (-jnp.arange(n_freq, dtype=jnp.float32) / n_freq)
    return jnp.concatenate([rows[:, None] * inv_freq, cols[:, None] * inv_freq], axis=-1)

def apply_rope(x, ang):
    half = QK_ROPE // 2
    cos = jnp.cos(ang)[:, None, :]
    sin = jnp.sin(ang)[:, None, :]
    xf = x.astype(jnp.float32)
    x1, x2 = xf[..., :half], xf[..., half:]
    out = jnp.concatenate([x1 * cos - x2 * sin, x1 * sin + x2 * cos], axis=-1)
    return out.astype(x.dtype)

def mixing_inputs(h, w_in, q_norm_g, w_uq, kv_norm_g):
    B, T, _ = h.shape
    proj = h @ w_in
    q_lat = proj[..., :Q_LORA]
    kv_lat = proj[..., Q_LORA:Q_LORA + KV_LORA]
    k_pe = proj[..., Q_LORA + KV_LORA:Q_LORA + KV_LORA + QK_ROPE]
    f_in = proj[..., Q_LORA + KV_LORA + QK_ROPE:]
    q = (rmsnorm(q_lat, q_norm_g) @ w_uq).reshape(B, T, N_HEADS, QK_NOPE + QK_ROPE)
    ckv = rmsnorm(kv_lat, kv_norm_g)
    return q[..., :QK_NOPE], q[..., QK_NOPE:], ckv, k_pe, f_in

def decompress(ckv, w_ukv):
    B, T, _ = ckv.shape
    kv = (ckv @ w_ukv).reshape(B, T, N_HEADS, QK_NOPE + V_HEAD)
    return kv[..., :QK_NOPE], kv[..., QK_NOPE:]

def attend(q_nope, q_pe, k_nope, k_pe, v):
    B, T = q_nope.shape[:2]
    nb = T // Q_BLOCK
    qn = q_nope.reshape(B, nb, Q_BLOCK, N_HEADS, QK_NOPE).transpose(1, 0, 2, 3, 4)
    qp = q_pe.reshape(B, nb, Q_BLOCK, N_HEADS, QK_ROPE).transpose(1, 0, 2, 3, 4)
    scale = (QK_NOPE + QK_ROPE) ** -0.5

    def block(args):
        qn_b, qp_b = args
        s = jnp.einsum('bqhd,bkhd->bhqk', qn_b, k_nope) + jnp.einsum('bqhr,bkr->bhqk', qp_b, k_pe)
        p = jax.nn.softmax(s.astype(jnp.float32) * scale, axis=-1).astype(v.dtype)
        return jnp.einsum('bhqk,bkhd->bqhd', p, v)

    out = lax.map(block, (qn, qp))
    return out.transpose(1, 0, 2, 3, 4).reshape(B, T, ATTN_W)

def fourier_mix(f_in, w_fmix):
    B, T, _ = f_in.shape
    f = f_in.reshape(B, T, FNET_GROUPS, FNET_CH).astype(jnp.float32)
    fr = jnp.fft.fft2(f, axes=(1, 3), norm='ortho').real.astype(f_in.dtype)
    return jnp.einsum('btgc,gcd->btgd', fr, w_fmix).reshape(B, T, FNET_W)

def expert_choice(h, w_router, w_e_gate, w_e_up, w_e_down):
    B, n, _ = h.shape
    cap = CAP_FACTOR * n // N_EXPERTS
    aff = jax.nn.softmax((h @ w_router).astype(jnp.float32), axis=-1)
    g, idx = lax.top_k(aff.transpose(0, 2, 1), cap)
    b_idx = jnp.arange(B)[:, None, None]
    xs = h[b_idx, idx]
    hid = jax.nn.silu(jnp.einsum('becd,edf->becf', xs, w_e_gate)) * jnp.einsum('becd,edf->becf', xs, w_e_up)
    ys = jnp.einsum('becf,efd->becd', hid, w_e_down) * g[..., None].astype(h.dtype)
    return jnp.zeros_like(h).at[b_idx, idx].add(ys)

def context_layer(x, mods, lp):
    (norm1_g, w_in, q_norm_g, w_uq, kv_norm_g, w_ukv, w_fmix, w_out,
     norm2_g, w_router, w_e_gate, w_e_up, w_e_down) = lp
    shift1, scale1, gate1, shift2, scale2, gate2 = mods
    h = modulate(rmsnorm(x, norm1_g), shift1, scale1)
    q_nope, q_pe, ckv, k_pe, f_in = mixing_inputs(h, w_in, q_norm_g, w_uq, kv_norm_g)
    k_nope, v = decompress(ckv, w_ukv)
    attn = attend(q_nope, q_pe, k_nope, k_pe, v)
    fmix = fourier_mix(f_in, w_fmix)
    x = x + gate1 * (jnp.concatenate([attn, fmix], axis=-1) @ w_out)
    h2 = modulate(rmsnorm(x, norm2_g), shift2, scale2)
    x = x + gate2 * expert_choice(h2, w_router, w_e_gate, w_e_up, w_e_down)
    return x, ckv, k_pe

def latent_layer(x, mods, ckv_ctx, kpe_ctx, ang, lp):
    (norm1_g, w_in, q_norm_g, w_uq, kv_norm_g, w_ukv, w_fmix, w_out,
     norm2_g, w_router, w_e_gate, w_e_up, w_e_down) = lp
    shift1, scale1, gate1, shift2, scale2, gate2 = mods
    h = modulate(rmsnorm(x, norm1_g), shift1, scale1)
    q_nope, q_pe, ckv, k_pe, f_in = mixing_inputs(h, w_in, q_norm_g, w_uq, kv_norm_g)
    q_pe = apply_rope(q_pe, ang)
    k_pe = apply_rope(k_pe[:, :, None, :], ang)[:, :, 0, :]
    k_nope_l, v_l = decompress(ckv, w_ukv)
    k_nope_c, v_c = decompress(ckv_ctx, w_ukv)
    k_nope = jnp.concatenate([k_nope_c, k_nope_l], axis=1)
    k_pe_all = jnp.concatenate([kpe_ctx, k_pe], axis=1)
    v = jnp.concatenate([v_c, v_l], axis=1)
    attn = attend(q_nope, q_pe, k_nope, k_pe_all, v)
    fmix = fourier_mix(f_in, w_fmix)
    x = x + gate1 * (jnp.concatenate([attn, fmix], axis=-1) @ w_out)
    h2 = modulate(rmsnorm(x, norm2_g), shift2, scale2)
    x = x + gate2 * expert_choice(h2, w_router, w_e_gate, w_e_up, w_e_down)
    return x

def setup_inputs(seed: int = 0) -> dict:
    key = jax.random.key(seed)
    ks = jax.random.split(key, 32)
    f32 = jnp.float32

    def nrm(k, shape, scale):
        return jax.random.normal(k, shape, f32) * scale

    def gain(k, shape):
        return 1.0 + 0.02 * jax.random.normal(k, shape, f32)

    L = DEPTH
    return {
        'x_prompt': nrm(ks[0], (BATCH, SEQ, D_MODEL), 1.0),
        'x_sample': nrm(ks[1], (DEC_BATCH, DEC_SEQ, D_MODEL), 1.0),
        'cache_ckv': nrm(ks[2], (DEC_BATCH, DEPTH, PAST_LEN, KV_LORA), 1.0),
        'cache_kpe': nrm(ks[3], (DEC_BATCH, DEPTH, PAST_LEN, QK_ROPE), 1.0),
        'c': nrm(ks[4], (DEC_BATCH, D_MODEL), 1.0),
        'c_ctx': nrm(ks[5], (D_MODEL,), 1.0),
        'w_mod': nrm(ks[6], (L, D_MODEL, 6 * D_MODEL), 0.5 * D_MODEL ** -0.5),
        'b_mod': nrm(ks[7], (L, 6 * D_MODEL), 0.02),
        'norm1_g': gain(ks[8], (L, D_MODEL)),
        'w_in': nrm(ks[9], (L, D_MODEL, IN_W), D_MODEL ** -0.5),
        'q_norm_g': gain(ks[10], (L, Q_LORA)),
        'w_uq': nrm(ks[11], (L, Q_LORA, N_HEADS * (QK_NOPE + QK_ROPE)), Q_LORA ** -0.5),
        'kv_norm_g': gain(ks[12], (L, KV_LORA)),
        'w_ukv': nrm(ks[13], (L, KV_LORA, N_HEADS * (QK_NOPE + V_HEAD)), KV_LORA ** -0.5),
        'w_fmix': nrm(ks[14], (L, FNET_GROUPS, FNET_CH, FNET_CH), FNET_CH ** -0.5),
        'w_out': nrm(ks[15], (L, MIX_W, D_MODEL), MIX_W ** -0.5),
        'norm2_g': gain(ks[16], (L, D_MODEL)),
        'w_router': nrm(ks[17], (L, D_MODEL, N_EXPERTS), D_MODEL ** -0.5),
        'w_e_gate': nrm(ks[18], (L, N_EXPERTS, D_MODEL, D_EXPERT), D_MODEL ** -0.5),
        'w_e_up': nrm(ks[19], (L, N_EXPERTS, D_MODEL, D_EXPERT), D_MODEL ** -0.5),
        'w_e_down': nrm(ks[20], (L, N_EXPERTS, D_EXPERT, D_MODEL), D_EXPERT ** -0.5),
        'final_g': gain(ks[21], (D_MODEL,)),
    }

def reference(x_prompt, x_sample, cache_ckv, cache_kpe, c, c_ctx, w_mod, b_mod, norm1_g, w_in,
              q_norm_g, w_uq, kv_norm_g, w_ukv, w_fmix, w_out, norm2_g, w_router, w_e_gate,
              w_e_up, w_e_down, final_g):
    ang = rope_angles(x_sample.shape[1])
    xp = x_prompt
    xs = x_sample
    new_ckv = []
    new_kpe = []
    for l in range(DEPTH):
        lp = (norm1_g[l], w_in[l], q_norm_g[l], w_uq[l], kv_norm_g[l], w_ukv[l], w_fmix[l], w_out[l],
              norm2_g[l], w_router[l], w_e_gate[l], w_e_up[l], w_e_down[l])
        mods_ctx = adaln(c_ctx[None, :], w_mod[l], b_mod[l])
        mods_lat = adaln(c, w_mod[l], b_mod[l])
        xp, ckv, kpe = context_layer(xp, mods_ctx, lp)
        new_ckv.append(ckv)
        new_kpe.append(kpe)
        xs = latent_layer(xs, mods_lat, cache_ckv[:, l], cache_kpe[:, l], ang, lp)
    y_prompt = rmsnorm(xp, final_g)
    y_sample = rmsnorm(xs, final_g)
    state_ckv = jnp.stack(new_ckv, axis=1)
    state_kpe = jnp.stack(new_kpe, axis=1)
    return (y_prompt, y_sample, state_ckv, state_kpe)


_drawn_inputs = setup_inputs


def setup_inputs(seed=0):
    import zlib

    import numpy as np

    out = dict(_drawn_inputs(seed))
    spreads = {}
    factors = {'cache_ckv': 8.0,
     'cache_kpe': 8.0,
     'norm1_g': 3.114,
     'q_norm_g': 8.0,
     'kv_norm_g': 3.076,
     'norm2_g': 8.0,
     'final_g': 2.75}
    for name, (base, spread) in spreads.items():
        noise = np.random.default_rng([zlib.crc32(name.encode()), seed]).standard_normal(out[name].shape)
        drawn = base * np.exp(spread * noise) if base else spread * noise
        out[name] = __import__('jax').numpy.asarray(drawn.astype(out[name].dtype))
    for name, factor in factors.items():
        out[name] = (out[name] * factor).astype(out[name].dtype)
    return out
```

```python
import numpy as np
from contextlib import ExitStack

import concourse.bass as bass
from concourse import mybir

F32 = mybir.dt.float32
BF16 = mybir.dt.bfloat16
U32 = mybir.dt.uint32
ACT = mybir.ActivationFunctionType
ALU = mybir.AluOpType
AX = mybir.AxisListType

P = 128
D = 1024
DK = D // P
CTX, LAT, PAST = 256, 2048, 512
CT, LT, KC = CTX // P, LAT // P, PAST // P
NT = CT + LT
NTOK = CTX + LAT
KEYS = PAST + LAT + CTX
H = 8
NOPE, ROPE, VH = 64, 32, 64
QK = NOPE + ROPE
QL, KVL = 256, 128
FW = 512
LATW = QL + KVL + ROPE
NE = 16
CAP_L, CAP_C = 2 * LAT // NE, 2 * CTX // NE
DE = 512
EPS = 1e-6
SCALE = float(QK) ** -0.5
ROWW = D + NE


def is_int(n):
    return isinstance(n, int)


def active(n, first, last):
    return not is_int(n) or first <= n <= last


def wait_slot(eng, sem, m, per, depth):
    if not is_int(m) or m >= depth:
        eng.wait_ge(sem, (m - depth + 1) * per)


class Chain:

    def __init__(self, eng, sem, per, m):
        self.eng, self.sem, self.base, self.n, self.per = eng, sem, m * per, 0, per

    def link(self, ins):
        self.n += 1
        assert self.n <= self.per
        ins.then_inc(self.sem, 1)
        self.eng.wait_ge(self.sem, self.base + self.n)


class PoolWaits:

    def __init__(self, pool, passed):
        self.pool, self.passed = pool, passed

    def wait_ge(self, sem, value):
        self.pool.wait_ge(sem, value)
        if not is_int(value):
            self.pool.sem_inc(self.passed, 1)

    def Fori(self, *args):
        return self.pool.Fori(*args)


def run_steps(eng, step, loop_from, loop_to, last):
    for n in range(2 * loop_from):
        step(n, n % 2, n // 2)
    with eng.Fori(loop_from, loop_to) as j:
        step(2 * j, 0, j)
        step(2 * j + 1, 1, j)
    for n in range(2 * loop_to, last + 1):
        step(n, n % 2, n // 2)


def at(v, m):
    if is_int(m):
        return v[:, m]
    names = "abcd"[:len(v.shape) - 2]
    return v[:, bass.ds(m, 1)].rearrange(f"p o {' '.join(names)} -> p (o {names[0]}) {' '.join(names[1:])}")


def program(nc, a):
    with ExitStack() as ctx:
        sb = lambda name, shape, dt=F32: ctx.enter_context(nc.sbuf_tensor(name, shape, dt))
        pers = {
            "ident": sb("ident", [P, P]),
            "mods": sb("mods", [P, 6 * DK, 2]),
            "gs1": sb("gs1", [P, DK, 2]),
            "gs2": sb("gs2", [P, DK, 2]),
            "neg_half": sb("neg_half", [P, 1]),
            "AFF": sb("aff", [P, NT, NE]),
            "IDX": sb("slot_row", [P, NE, 3], U32),
            "sems": [],
        }
        modulation(nc, a, pers)
        with ExitStack() as mid:
            sbm = lambda name, shape, dt=F32: mid.enter_context(nc.sbuf_tensor(name, shape, dt))
            pers["ckvT"] = sbm("ckvT", [P, KEYS])
            pers["kpeT"] = sbm("kpeT", [QK, KEYS])
            fmix = mid.enter_context(nc.sbuf_tensor("fmixT", [P, FW // P, NTOK], F32))
            pers["fmixT"] = fmix
            with ExitStack() as fs:
                pers["F"] = fs.enter_context(nc.sbuf_tensor("f_in", [P, NT, FW], F32))
                mixing_in(nc, a, pers)
                clear_semaphores(nc, pers["sems"])
                fourier(nc, a, pers)
            pers["O"] = mid.enter_context(nc.sbuf_tensor("attn_out", [P, NT, H * VH], F32))
            attention(nc, a, pers)
            mixing_out(nc, a, pers)
        routing(nc, a, pers)
        experts(nc, a, pers)
        final_norm(nc, a, pers)


def clear_semaphores(nc, sems):
    nums = [s.num for s in sems]
    assert nums == list(range(nums[0], nums[0] + len(nums)))
    with nc.Block() as block:
        @block.gpsimd
        def _(pool):
            pool.sem_clear(range(nums[0], nums[0] + len(nums)))


def modulation(nc, a, t):
    NB, BC, NS = 12, 512, 3
    QT = BC // P
    with ExitStack() as x:
        sb = lambda name, shape, dt=F32: x.enter_context(nc.sbuf_tensor(name, shape, dt))
        sem = lambda name: t["sems"].append(x.enter_context(nc.semaphore(name))) or t["sems"][-1]
        wm = [sb(f"wm{s}", [P, DK, BC]) for s in range(NS)]
        NROW = 10 * DK
        vrow, vcol = sb("vec_rows", [NROW, P]), sb("vec_cols", [P, NROW])
        scol = sb("silu_cols", [P, 2, DK])
        gate_col, gate_row = sb("gate_cols", [P, 2, 2, DK]), sb("gate_rows", [4 * DK, P])
        v_ps = x.enter_context(nc.psum_tensor("vec_ps", [P, 512], F32))
        mp = [x.enter_context(nc.psum_tensor(f"mod_ps{s}", [P, 512], F32)) for s in range(NS)]
        w_loaded = [sem(f"mod_w_loaded{s}") for s in range(NS)]
        vec_loaded, vecT_done, vecT_copied = sem("mod_vec_loaded"), sem("mod_vecT"), sem("mod_vecT_copied")
        gates_ready, gateT_done, gateT_copied = sem("mod_gates"), sem("mod_gateT"), sem("mod_gateT_copied")
        silu_done, block_done, block_read = sem("mod_silu"), sem("mod_block_done"), sem("mod_block_read")
        gates_stored, chain = sem("mod_gates_stored"), sem("mod_chain")
        mods, gs1, gs2, ident = t["mods"], t["gs1"], t["gs2"], t["ident"]
        w_v = a["w_mod"][0].rearrange("(k p) n -> p k n", p=P)
        block = x.enter_context(nc.Block())

        @block.sync
        def _(sp):
            def load(n, s, i):
                if not is_int(i) or i >= 1:
                    sp.wait_ge(block_done, n - NS + 1)
                sp.dma_start(wm[s][:], w_v[:, :, bass.ds(n * BC, BC)]).then_inc(w_loaded[s], 16)

            for s in range(NS):
                load(s, s, 0)
            with sp.Fori(1, NB // NS) as i:
                for s in range(NS):
                    load(i * NS + s, s, i)

        @block.tensor
        def _(pe):
            pe.wait_ge(vec_loaded, 96)
            nc.tensor.transpose(v_ps[:, 0:NROW], vrow[:], ident[0:NROW, 0:NROW]).then_inc(vecT_done, 1)
            pe.wait_ge(silu_done, 1)

            def block_of(n, s, i):
                pe.wait_ge(w_loaded[s], 16 * (i + 1))
                if not is_int(i) or i >= 1:
                    pe.wait_ge(block_read, n - NS + 1)
                for q in range(QT):
                    for k in range(DK):
                        last = nc.tensor.matmul(mp[s][:, 2 * q:2 * q + 2], wm[s][:, k, q * P:(q + 1) * P],
                                                scol[:, :, k], start=(k == 0), stop=(k == DK - 1))
                last.then_inc(block_done, 1)

            for s in range(NS):
                block_of(s, s, 0)
            with pe.Fori(1, NB // NS) as i:
                for s in range(NS):
                    block_of(i * NS + s, s, i)
            pe.wait_ge(gates_ready, 4)
            nc.tensor.transpose(v_ps[0:4 * DK, 0:P], gate_col[:].rearrange("p g k j -> p (g k j)"), ident[:])\
                .then_inc(gateT_done, 1)

        @block.scalar
        def _(act):
            act.dma_start(ident[:], a["k_ident"]).then_inc(vec_loaded, 16)
            rows = (("c_ctx", a["c_ctx"]), ("c", a["c"][0]), ("norm1_g", a["norm1_g"][0]),
                    ("norm2_g", a["norm2_g"][0]), ("b_mod", a["b_mod"][0]))
            r = 0
            for _, src in rows:
                n = src.shape[0] // P
                act.dma_start(vrow[r:r + n, :], src.rearrange("(k p) -> k p", p=P)).then_inc(vec_loaded, 16)
                r += n
            act.wait_ge(vecT_copied, 1)
            nc.scalar.activation(scol[:], vcol[:, 0:2 * DK].rearrange("p (c k) -> p c k", c=2), ACT.Silu)\
                .then_inc(silu_done, 1)
            act.wait_ge(gateT_copied, 1)
            act.dma_start(a["s_gates"].rearrange("g k (j p) -> (g k j) p", p=P), gate_row[:]).then_inc(gates_stored, 16)
            act.wait_ge(gates_stored, 16)

        @block.vector
        def _(dve):
            nc.vector.memset(t["neg_half"][:], -0.5)
            dve.wait_ge(vecT_done, 1)
            nc.vector.tensor_copy(vcol[:], v_ps[:, 0:NROW]).then_inc(vecT_copied, 1)
            dve.wait_ge(vecT_copied, 1)
            bcol = vcol[:, 4 * DK:]

            def add_bias(n, s):
                dve.wait_ge(block_done, n + 1)
                bias = bcol[:, bass.ds(n * QT, QT)].unsqueeze(2).to_broadcast([P, QT, 2])
                nc.vector.tensor_tensor(mods[:, bass.ds(n * QT, QT), :],
                                        mp[s][:, 0:2 * QT].rearrange("p (q k) -> p q k", k=2), bias,
                                        ALU.add).then_inc(block_read, 1)

            for s in range(NS):
                add_bias(s, s)
            with dve.Fori(1, NB // NS) as i:
                for s in range(NS):
                    add_bias(i * NS + s, s)
            dve.wait_ge(block_read, NB)
            link = Chain(dve, chain, 4, 0).link
            for g, (gs, seg) in enumerate(((gs1, 1), (gs2, 4))):
                link(nc.vector.tensor_scalar(gs[:], mods[:, seg * DK:(seg + 1) * DK, :], 1.0, None, ALU.add))
                gcol = vcol[:, (2 + g) * DK:(3 + g) * DK].unsqueeze(2).to_broadcast([P, DK, 2])
                link(nc.vector.tensor_tensor(gs[:], gs[:], gcol, ALU.mult))
                for kind in range(2):
                    nc.vector.tensor_copy(gate_col[:, g, kind, :],
                                          mods[:, (2 + 3 * g) * DK:(3 + 3 * g) * DK, kind]).then_inc(gates_ready, 1)
            dve.wait_ge(gateT_done, 1)
            nc.vector.tensor_copy(gate_row[:], v_ps[0:4 * DK, 0:P]).then_inc(gateT_copied, 1)


def mixing_in(nc, a, t):
    with ExitStack() as x:
        sb = lambda name, shape, dt=F32: x.enter_context(nc.sbuf_tensor(name, shape, dt))
        sem = lambda name: t["sems"].append(x.enter_context(nc.semaphore(name))) or t["sems"][-1]
        ps = lambda name: x.enter_context(nc.psum_tensor(name, [P, 512], F32))
        two = range(2)
        w_in = sb("w_in_sb", [P, DK, LATW + FW])
        w_uq = sb("w_uq_sb", [P, QL // P, H * QK])
        qg = sb("qg", [P, QL])
        kvg = sb("kvg", [P, KVL])
        cs, sn = sb("rope_cos", [P, NT, ROPE]), sb("rope_sin", [P, NT, ROPE])
        ckv_c, kpe_c = sb("ckv_cache", [P, KC, KVL]), sb("kpe_cache", [P, KC, P])
        xt = [sb(f"x{s}", [P, D]) for s in two]
        xn = [sb(f"xn{s}", [P, D]) for s in two]
        junk, junk_p = sb("junk", [P, D]), sb("junk_p", [P, QL + KVL])
        ssx = [sb(f"ssx{s}", [P, 1]) for s in two]
        msx, rsx = sb("msx", [P, 1]), [sb(f"rsx{s}", [P, 1]) for s in two]
        hT = [sb(f"hT{s}", [P, DK, P]) for s in two]
        pa = [sb(f"pa{s}", [P, LATW]) for s in two]
        ssp = [sb(f"ssp{s}", [P, 2]) for s in two]
        msp, rsp = sb("msp", [P, 2]), [sb(f"rsp{s}", [P, 2]) for s in two]
        rt = sb("rope_t", [P, 2, ROPE])
        tm = [sb(f"tm{s}", [P, 4 * P]) for s in two]
        KPE0 = QL + KVL + NOPE
        qnT = [sb(f"qnT{s}", [P, QL // P, P]) for s in two]
        q_sb = [sb(f"q_sb{s}", [P, H, QK]) for s in two]
        qt_ = sb("q_rope_t", [P, 2, H, ROPE])
        qT = [sb(f"qT{s}", [QK, H, P]) for s in two]
        xT_ps = [ps("xT_ps0"), ps("xT_ps1")]
        pa_ps, pf_ps, sT_ps = ps("pa_ps"), ps("pf_ps"), ps("sT_ps")
        q_ps, qT_ps = [ps("q_ps0"), ps("q_ps1")], ps("qT_ps")
        HH = H // 2

        w_loaded, rows_loaded, cache_loaded = sem("in_w_loaded"), sem("in_rows_loaded"), sem("in_cache_loaded")
        x_loaded = [sem(f"in_x_loaded{s}") for s in two]
        st_stored = [sem(f"in_state_stored{s}") for s in two]
        q_stored = [sem(f"in_q_stored{s}") for s in two]
        ssx_done, rsx_done, xn_done, xT_done = sem("in_ssx"), sem("in_rsx"), sem("in_xn"), sem("in_xT")
        hTa, hTv = sem("in_hT_act"), sem("in_hT_dve")
        pa_done, pf_done, pa_copied, f_copied = sem("in_pa"), sem("in_pf"), sem("in_pa_copied"), sem("in_f_copied")
        ssp_done, rsp_done, norm_done, kpe_done = sem("in_ssp"), sem("in_rsp"), sem("in_norms"), sem("in_kpe")
        sT_done, sT_read = sem("in_sT"), sem("in_sT_read")
        q_done, qa_copied, qv_copied, q_roped = sem("in_q"), sem("in_qa"), sem("in_qv"), sem("in_q_roped")
        qT_done, qTa, qTv = sem("in_qT"), sem("in_qTa"), sem("in_qTv")
        passed = sem("in_pool_waits_passed")
        px, pp, pq, zeroed = sem("in_pool_x"), sem("in_pool_p"), sem("in_pool_q"), sem("in_zeroed")
        cT_done, cT_read, final_st = sem("in_cacheT"), sem("in_cacheT_read"), sem("in_states_out")
        mods, gs1, F, ckvT, kpeT, ident = (t[k] for k in ("mods", "gs1", "F", "ckvT", "kpeT", "ident"))
        xp, xs = a["x_prompt"][0], a["x_sample"][0]
        LAST = NT + 1
        block = x.enter_context(nc.Block())

        def key_col(m):
            if is_int(m) and m < CT:
                return PAST + LAT + m * P
            return PAST + (m - CT) * P

        @block.sync
        def _(sp):
            def load_x(n, s):
                wait_slot(sp, xn_done, n, 1, 2)
                src = xp[n * P:(n + 1) * P, :] if is_int(n) and n < CT else xs[bass.ds((n - CT) * P, P), :]
                sp.dma_start(xt[s][:], src).then_inc(x_loaded[s], 16)

            for n in two:
                load_x(n, n)
            sp.dma_start(w_in[:, :, 0:LATW], a["w_in"][0].rearrange("(k p) n -> p k n", p=P)[:, :, 0:LATW])\
                .then_inc(w_loaded, 16)
            sp.dma_start(w_in[:, :, LATW:], a["w_in"][0].rearrange("(k p) n -> p k n", p=P)[:, :, LATW:])\
                .then_inc(w_loaded, 16)
            sp.dma_start(w_uq[:], a["w_uq"][0].rearrange("(k p) n -> p k n", p=P)).then_inc(w_loaded, 16)

            def step(n, s, j):
                if active(n, 2, NT - 1):
                    load_x(n, s)
                if active(n, 1, NT):
                    m = n - 1
                    sp.wait_ge(norm_done, 2 * (m + 1))
                    sp.wait_ge(kpe_done, m + 1)
                    sp.dma_start(a["s_state"][bass.ds(m * P, P), 0:KVL], tm[1 - s][:, QL:QL + KVL])\
                        .then_inc(st_stored[1 - s], 16)
                    sp.dma_start(a["s_state"][bass.ds(m * P, P), KVL:], tm[1 - s][:, KPE0:KPE0 + ROPE])\
                        .then_inc(st_stored[1 - s], 16)
                if active(n, 2, LAST):
                    m = n - 2
                    sp.wait_ge(qTa, m + 1)
                    sp.wait_ge(qTv, m + 1)
                    sp.dma_start(a["s_q"][m] if is_int(m) else a["s_q"][bass.ds(m, 1)].rearrange("o p h q -> (o p) h q"), qT[s][:])\
                        .then_inc(q_stored[s], 16)

            run_steps(sp, step, 2, NT // 2, LAST)
            for s in two:
                sp.wait_ge(st_stored[s], 32 * (NT // 2))
                sp.wait_ge(q_stored[s], 16 * (NT // 2))
            sp.dma_start(a["state_ckv"][0, 0], a["s_state"][0:CTX, 0:KVL]).then_inc(final_st, 16)
            sp.dma_start(a["state_kpe"][0, 0], a["s_state"][0:CTX, KVL:]).then_inc(final_st, 16)
            sp.wait_ge(final_st, 32)

        @block.scalar
        def _(act):
            act.dma_start(qg[:], a["q_norm_g"].partition_broadcast(P)).then_inc(rows_loaded, 16)
            act.dma_start(kvg[:], a["kv_norm_g"].partition_broadcast(P)).then_inc(rows_loaded, 16)
            act.dma_start(cs[:], a["k_rope_cos"].rearrange("(n p) r -> p n r", p=P)).then_inc(rows_loaded, 16)
            act.dma_start(sn[:], a["k_rope_sin"].rearrange("(n p) r -> p n r", p=P)).then_inc(rows_loaded, 16)
            act.wait_ge(zeroed, 3)
            act.dma_start(ckv_c[:], a["cache_ckv"][0, 0].rearrange("(n p) r -> p n r", p=P)).then_inc(cache_loaded, 16)
            act.dma_start(kpe_c[:, :, NOPE:QK], a["cache_kpe"][0, 0].rearrange("(n p) r -> p n r", p=P))\
                .then_inc(cache_loaded, 16)
            act.wait_ge(cT_done, 1)
            nc.scalar.copy(ckvT[:, 0:PAST], sT_ps[:]).then_inc(cT_read, 1)

            def step(n, s, j):
                o = 1 - s
                if active(n, 0, NT - 1):
                    act.wait_ge(x_loaded[s], 16 * (j + 1))
                    wait_slot(act, rsx_done, n, 1, 2)
                    act.wait_ge(ssx_done, n)
                    nc.scalar.activation(junk[:], xt[s][:], ACT.Square, accum_out=ssx[s][:]).then_inc(ssx_done, 1)
                if active(n, 1, NT):
                    m = n - 1
                    act.wait_ge(pa_done, m + 1)
                    wait_slot(act, norm_done, m, 2, 2)
                    wait_slot(act, kpe_done, m, 1, 2)
                    nc.scalar.copy(pa[o][:], pa_ps[:, 0:LATW]).then_inc(pa_copied, 1)
                    act.wait_ge(pa_copied, m + 1)
                    wait_slot(act, rsp_done, m, 1, 2)
                    act.wait_ge(ssp_done, 2 * m)
                    nc.scalar.activation(junk_p[:, 0:QL], pa[o][:, 0:QL], ACT.Square, accum_out=ssp[o][:, 0:1])\
                        .then_inc(ssp_done, 1)
                    nc.scalar.activation(junk_p[:, QL:], pa[o][:, QL:QL + KVL], ACT.Square,
                                         accum_out=ssp[o][:, 1:2]).then_inc(ssp_done, 1)
                if active(n, 2, LAST):
                    m = n - 2
                    act.wait_ge(q_done, 2 * m + 1)
                    wait_slot(act, qT_done, m, 2, 2)
                    nc.scalar.copy(q_sb[s][:, 0:HH, :], q_ps[0][:, 0:HH * QK]).then_inc(qa_copied, 1)
                if active(n, 0, NT - 1):
                    kind = 0 if is_int(n) and n < CT else 1
                    act.wait_ge(xT_done, 2 * n + 1)
                    wait_slot(act, pf_done, n, 1, 2)
                    for k in range(DK // 2):
                        nc.scalar.activation(hT[s][:, k, :], xT_ps[0][:, k * P:(k + 1) * P], ACT.Identity,
                                             scale=gs1[:, k, kind:kind + 1], bias=mods[:, k, kind:kind + 1])\
                            .then_inc(hTa, 1)
                if active(n, 1, NT):
                    m = n - 1
                    act.wait_ge(pf_done, m + 1)
                    nc.scalar.copy(at(F, m), pf_ps[:]).then_inc(f_copied, 1)
                if active(n, 2, LAST):
                    m = n - 2
                    act.wait_ge(qT_done, 2 * m + 1)
                    wait_slot(act, q_stored[s], j - 1, 16, 1)
                    nc.scalar.copy(qT[s][:, 0:HH, :], qT_ps[0:QK, :]).then_inc(qTa, 1)

            run_steps(act, step, 2, NT // 2, LAST)

        @block.gpsimd
        def _(pool):
            nc.gpsimd.memset(kpe_c[:], 0.0).then_inc(zeroed, 1)
            for s in two:
                nc.gpsimd.memset(tm[s][:], 0.0).then_inc(zeroed, 1)
            pool.wait_ge(zeroed, 3)
            pool.wait_ge(rows_loaded, 64)
            pool = PoolWaits(pool, passed)

            def step(n, s, j):
                o = 1 - s
                if active(n, 0, NT - 1):
                    pool.wait_ge(ssx_done, n + 1)
                    c = Chain(pool, px, 1, n)
                    c.link(nc.gpsimd.tensor_scalar(msx[:], ssx[s][:], 1.0 / D, EPS, ALU.mult, ALU.add))
                    wait_slot(pool, xn_done, n, 1, 2)
                    nc.gpsimd.tensor_tensor(rsx[s][:], msx[:], t["neg_half"][:], ALU.pow).then_inc(rsx_done, 1)
                if active(n, 1, NT):
                    m = n - 1
                    pool.wait_ge(ssp_done, 2 * (m + 1))
                    c = Chain(pool, pp, 4, m)
                    nc.gpsimd.tensor_scalar(msp[:, 0:1], ssp[o][:, 0:1], 1.0 / QL, EPS, ALU.mult, ALU.add)
                    c.link(nc.gpsimd.tensor_scalar(msp[:, 1:2], ssp[o][:, 1:2], 1.0 / KVL, EPS, ALU.mult, ALU.add))
                    wait_slot(pool, norm_done, m, 2, 2)
                    nc.gpsimd.tensor_tensor(rsp[o][:], msp[:], t["neg_half"][:].to_broadcast([P, 2]), ALU.pow)\
                        .then_inc(rsp_done, 1)
                    kp = pa[o][:, QL + KVL:LATW]
                    R = ROPE // 2
                    csm, snm = at(cs, m), at(sn, m)
                    c.link(nc.gpsimd.tensor_tensor(rt[:, 0, :], kp, csm, ALU.mult))
                    c.link(nc.gpsimd.tensor_tensor(rt[:, 1, 0:R], kp[:, R:], snm[:, 0:R], ALU.mult))
                    c.link(nc.gpsimd.tensor_tensor(rt[:, 1, R:], kp[:, 0:R], snm[:, R:], ALU.mult))
                    wait_slot(pool, sT_done, m, 1, 2)
                    wait_slot(pool, st_stored[o], j - o, 32, 1)
                    nc.gpsimd.tensor_tensor(tm[o][:, KPE0:KPE0 + ROPE], rt[:, 0, :], rt[:, 1, :], ALU.add)\
                        .then_inc(kpe_done, 1)
                if active(n, 2, LAST):
                    m = n - 2
                    pool.wait_ge(qa_copied, m + 1)
                    pool.wait_ge(qv_copied, m + 1)
                    c = Chain(pool, pq, 3, m)
                    R = ROPE // 2
                    wide = lambda v: v.unsqueeze(1).to_broadcast([P, H, v.shape[-1]])
                    csm, snm = at(cs, m), at(sn, m)
                    qp = q_sb[s][:, :, NOPE:QK]
                    c.link(nc.gpsimd.tensor_tensor(qt_[:, 0], qp, wide(csm), ALU.mult))
                    c.link(nc.gpsimd.tensor_tensor(qt_[:, 1, :, 0:R], qp[:, :, R:], wide(snm[:, 0:R]), ALU.mult))
                    c.link(nc.gpsimd.tensor_tensor(qt_[:, 1, :, R:], qp[:, :, 0:R], wide(snm[:, R:]), ALU.mult))
                    nc.gpsimd.tensor_tensor(qp, qt_[:, 0], qt_[:, 1], ALU.add).then_inc(q_roped, 1)

            run_steps(pool, step, 2, NT // 2, LAST)

        @block.vector
        def _(dve):
            dve.wait_ge(rows_loaded, 64)
            dve.wait_ge(cT_done, 2)
            nc.vector.tensor_copy(kpeT[NOPE:QK, 0:PAST], qT_ps[NOPE:QK, :]).then_inc(cT_read, 1)

            def step(n, s, j):
                o = 1 - s
                if active(n, 0, NT - 1):
                    dve.wait_ge(rsx_done, n + 1)
                    wait_slot(dve, xT_done, n, 2, 2)
                    nc.vector.tensor_scalar(xn[s][:], xt[s][:], rsx[s][:], None, ALU.mult).then_inc(xn_done, 1)
                if active(n, 2, LAST):
                    m = n - 2
                    dve.wait_ge(sT_done, m + 1)
                    col = key_col(m)
                    wait_slot(dve, q_done, m, 2, 2)
                    nc.vector.tensor_copy(qnT[s][:], sT_ps[:, 0:QL])
                    nc.vector.tensor_copy(ckvT[:, bass.ds(col, P)], sT_ps[:, QL:QL + P])
                    nc.vector.tensor_copy(kpeT[NOPE:QK, bass.ds(col, P)], sT_ps[NOPE:QK, QL + P:QL + 2 * P])\
                        .then_inc(sT_read, 1)
                if active(n, 1, NT):
                    m = n - 1
                    dve.wait_ge(rsp_done, m + 1)
                    wait_slot(dve, sT_done, m, 1, 2)
                    wait_slot(dve, st_stored[o], j - o, 32, 1)
                    nc.vector.scalar_tensor_tensor(tm[o][:, 0:QL], pa[o][:, 0:QL], rsp[o][:, 0:1], qg[:],
                                                   ALU.mult, ALU.mult).then_inc(norm_done, 1)
                    nc.vector.scalar_tensor_tensor(tm[o][:, QL:QL + KVL], pa[o][:, QL:QL + KVL], rsp[o][:, 1:2],
                                                   kvg[:], ALU.mult, ALU.mult).then_inc(norm_done, 1)
                if active(n, 2, LAST):
                    m = n - 2
                    dve.wait_ge(q_done, 2 * m + 2)
                    wait_slot(dve, qT_done, m, 2, 2)
                    nc.vector.tensor_copy(q_sb[s][:, HH:, :], q_ps[1][:, 0:HH * QK]).then_inc(qv_copied, 1)
                if active(n, 0, NT - 1):
                    kind = 0 if is_int(n) and n < CT else 1
                    dve.wait_ge(xT_done, 2 * n + 2)
                    wait_slot(dve, pf_done, n, 1, 2)
                    for k in range(DK // 2, DK):
                        nc.vector.tensor_scalar(hT[s][:, k, :], xT_ps[1][:, (k - DK // 2) * P:(k - DK // 2 + 1) * P],
                                                gs1[:, k, kind:kind + 1], mods[:, k, kind:kind + 1],
                                                ALU.mult, ALU.add).then_inc(hTv, 1)
                if active(n, 2, LAST):
                    m = n - 2
                    dve.wait_ge(qT_done, 2 * m + 2)
                    wait_slot(dve, q_stored[s], j - 1, 16, 1)
                    nc.vector.tensor_copy(qT[s][:, HH:, :], q_ps[0][0:QK, :]).then_inc(qTv, 1)

            run_steps(dve, step, 2, NT // 2, LAST)

        @block.tensor
        def _(pe):
            pe.wait_ge(cache_loaded, 32)
            for n in range(KC):
                last = nc.tensor.transpose(sT_ps[:, n * P:(n + 1) * P], ckv_c[:, n, :], ident[:])
            last.then_inc(cT_done, 1)
            for n in range(KC):
                last = nc.tensor.transpose(qT_ps[:, n * P:(n + 1) * P], kpe_c[:, n, :], ident[:])
            last.then_inc(cT_done, 1)
            pe.wait_ge(cT_read, 2)

            def step(n, s, j):
                o = 1 - s
                if active(n, 2, LAST):
                    m = n - 2
                    pe.wait_ge(norm_done, 2 * (m + 1))
                    pe.wait_ge(kpe_done, m + 1)
                    wait_slot(pe, sT_read, m, 1, 1)
                    for k in range(4):
                        last = nc.tensor.transpose(sT_ps[:, k * P:(k + 1) * P], tm[s][:, k * P:(k + 1) * P], ident[:])
                    last.then_inc(sT_done, 1)
                if active(n, 1, NT):
                    m = n - 1
                    if is_int(m) and m == 0:
                        pe.wait_ge(w_loaded, 48)
                    wait_slot(pe, pa_copied, m, 1, 1)
                    for k in range(DK):
                        wait_hT(pe, m, k)
                        last = nc.tensor.matmul(pa_ps[:, 0:LATW], hT[o][:, k, :], w_in[:, k, 0:LATW],
                                                start=(k == 0), stop=(k == DK - 1))
                    last.then_inc(pa_done, 1)
                if active(n, 2, LAST):
                    m = n - 2
                    pe.wait_ge(sT_read, m + 1)
                    for h in range(2):
                        wait_slot(pe, (qTv, qv_copied)[h], m, 1, 1)
                        for k in range(QL // P):
                            last = nc.tensor.matmul(q_ps[h][:, 0:HH * QK], qnT[s][:, k, :],
                                                    w_uq[:, k, h * HH * QK:(h + 1) * HH * QK],
                                                    start=(k == 0), stop=(k == QL // P - 1))
                        last.then_inc(q_done, 1)
                if active(n, 0, NT - 1):
                    pe.wait_ge(xn_done, n + 1)
                    for b in range(2):
                        wait_slot(pe, (hTa, hTv)[b], n, DK // 2, 1)
                        for k in range(DK // 2):
                            c0 = (b * (DK // 2) + k) * P
                            last = nc.tensor.transpose(xT_ps[b][:, k * P:(k + 1) * P], xn[s][:, c0:c0 + P], ident[:])
                        last.then_inc(xT_done, 1)
                if active(n, 1, NT):
                    m = n - 1
                    wait_slot(pe, f_copied, m, 1, 1)
                    for k in range(DK):
                        last = nc.tensor.matmul(pf_ps[:], hT[o][:, k, :], w_in[:, k, LATW:],
                                                start=(k == 0), stop=(k == DK - 1))
                    last.then_inc(pf_done, 1)
                if active(n, 2, LAST):
                    m = n - 2
                    pe.wait_ge(q_roped, m + 1)
                    wait_slot(pe, qTa, m, 1, 1)
                    for h in range(H):
                        dst = (qT_ps, q_ps[0])[h // HH][0:QK, (h % HH) * P:(h % HH + 1) * P]
                        last = nc.tensor.transpose(dst, q_sb[s][:, h, :], ident[:])
                        if h % HH == HH - 1:
                            last.then_inc(qT_done, 1)

            def wait_hT(pe, m, k):
                half_k = DK // 2
                pe.wait_ge((hTa, hTv)[k // half_k], m * half_k + k % half_k + 1)

            run_steps(pe, step, 2, NT // 2, LAST)


def fourier(nc, a, t):
    with ExitStack() as x:
        sb = lambda name, shape, dt=F32: x.enter_context(nc.sbuf_tensor(name, shape, dt))
        sem = lambda name: x.enter_context(nc.semaphore(name))
        two = range(2)
        FT, HT, QT = FW // P, LT // 2, LT // 4
        NO, N0, N2 = LAT // 4, LAT // 8 + 1, LAT // 8
        tab = {
            "odd": [sb(f"tab_odd{q}", [P, HT, NO]) for q in two],
            "r0": [sb(f"tab_r0{q}", [P, QT, N0]) for q in two],
            "r2": [sb(f"tab_r2{q}", [P, QT, N2]) for q in two],
        }
        G = sb("half_sums", [P, HT, FW])
        chan = sb("chan", [P, 2, 2, P])
        wblk = sb("w_fmix_blocks", [P, FT, P])
        M = sb("chan_mix", [P, 2, 2, FT, P])
        PQ = [[sb(f"{'PQ'[q]}{s}", [P, 512]) for s in two] for q in two]
        R2 = [sb(f"R2_{s}", [P, 512]) for s in two]
        pq_ps = [[x.enter_context(nc.psum_tensor(f"fps_{'PQ'[q]}{s}", [P, 512], F32)) for s in two] for q in two]
        r_ps = [[x.enter_context(nc.psum_tensor(f"fps_R{q}{s}", [P, 512], F32)) for s in two] for q in two]
        r0_loaded, odd_loaded, r2_loaded = sem("f_r0_loaded"), sem("f_odd_loaded"), sem("f_r2_loaded")
        chan_loaded, zeroed = sem("f_chan_loaded"), sem("f_zeroed")
        M_done, M_copied = sem("f_M_done"), sem("f_M_copied")
        g_done, d_done, u_done = sem("f_half_sums"), sem("f_half_diffs"), sem("f_quarters")
        pq_done = [sem(f"f_{'PQ'[q]}_done") for q in two]
        pq_copied = [sem(f"f_{'PQ'[q]}_copied") for q in two]
        r_done, r2_copied, mixed = sem("f_R_done"), sem("f_R2_copied"), sem("f_mixed")
        F, out = t["F"], t["fmixT"]
        lat = lambda lo, hi, step: out[:, :, CTX + lo:CTX + hi:step]
        jobs = []
        for c in range(FT):
            jobs.append(("ctx", [F[:, i, c * P:(c + 1) * P] for i in range(CT)], CTX // 2 + 1,
                         out[:, c, 0:CTX // 2 + 1], out[:, c, CTX - 1:CTX // 2:-1], (1, CTX // 2), None))
        T = LAT
        lo = lambda c, k0, step: out[:, c, CTX + k0:CTX + T // 2 + 1:step]
        hi = lambda c, k0, step: out[:, c, CTX + T - k0:CTX + T // 2:-step]
        for c in range(FT):
            cc = slice(c * P, (c + 1) * P)
            jobs.append(("odd", [F[:, CT + HT + i, cc] for i in range(HT)], NO, lo(c, 1, 2), hi(c, 1, 2), (0, NO), "d"))
        for c in range(FT):
            cc = slice(c * P, (c + 1) * P)
            jobs.append(("r0", [F[:, CT + i, cc] for i in range(QT)], N0, lo(c, 0, 4), hi(c, 4, 4), (1, N0 - 1), "u"))
        for c in range(FT):
            cc = slice(c * P, (c + 1) * P)
            jobs.append(("r2", [F[:, CT + QT + i, cc] for i in range(QT)], N2, lo(c, 2, 4), hi(c, 2, 4), (0, N2), "u"))
        NJ = len(jobs)
        block = x.enter_context(nc.Block())

        @block.sync
        def _(sp):
            sp.dma_start(chan[:], a["k_chan"]).then_inc(chan_loaded, 16)
            for name, s in (("r0", r0_loaded), ("odd", odd_loaded), ("r2", r2_loaded)):
                for q, f in enumerate(("cos", "sin")):
                    sp.dma_start(tab[name][q][:], a[f"k_{f}_{name}"].rearrange("(k p) f -> p k f", p=P)).then_inc(s, 16)

        @block.gpsimd
        def _(pool):
            nc.gpsimd.memset(wblk[:], 0.0).then_inc(zeroed, 1)
            for i in range(HT):
                pool.wait_ge(g_done, i + 1)
                nc.gpsimd.tensor_tensor(F[:, CT + HT + i, :], F[:, CT + i, :], F[:, CT + HT + i, :], ALU.subtract)\
                    .then_inc(d_done, 1)

        @block.vector
        def _(dve):
            for i in range(HT):
                nc.vector.tensor_tensor(G[:, i, :], F[:, CT + i, :], F[:, CT + HT + i, :], ALU.add).then_inc(g_done, 1)
            dve.wait_ge(M_done, 1)
            for q in two:
                nc.vector.tensor_copy(M[:, 1, q], r_ps[q][1][:].rearrange("p (c d) -> p c d", c=FT)).then_inc(M_copied, 1)
            dve.wait_ge(d_done, HT)
            dve.wait_ge(g_done, HT)
            for i in range(QT):
                nc.vector.tensor_tensor(F[:, CT + i, :], G[:, i, :], G[:, QT + i, :], ALU.add).then_inc(u_done, 1)
            for i in range(QT):
                nc.vector.tensor_tensor(F[:, CT + QT + i, :], G[:, i, :], G[:, QT + i, :], ALU.subtract).then_inc(u_done, 1)

            def copy_q(i):
                s, n = i % 2, jobs[i][2]
                dve.wait_ge(pq_done[1], i + 1)
                if i >= 2:
                    dve.wait_ge(r_done, i - 1)
                nc.vector.tensor_copy(PQ[1][s][:, 0:n], pq_ps[1][s][:, 0:n]).then_inc(pq_copied[1], 1)

            def combine(i):
                s, (_, _, n, direct, mirror, (m0, m1), _) = i % 2, jobs[i]
                dve.wait_ge(r_done, i + 1)
                dve.wait_ge(r2_copied, i + 1)
                nc.vector.tensor_tensor(direct, r_ps[0][s][:, 0:n], R2[s][:, 0:n], ALU.subtract)
                nc.vector.tensor_tensor(mirror, r_ps[0][s][:, m0:m1], R2[s][:, m0:m1], ALU.add).then_inc(mixed, 1)

            for i in range(NJ + 1):
                if i < NJ:
                    copy_q(i)
                if i >= 1:
                    combine(i - 1)

        @block.scalar
        def _(act):
            act.wait_ge(zeroed, 1)
            for b in two:
                src = a["w_fmix"][0].rearrange("(c b) i d -> b i c d", b=2)[b]
                act.dma_start(wblk[b * 64:(b + 1) * 64, :, b * 64:(b + 1) * 64], src).then_inc(chan_loaded, 16)
            act.wait_ge(M_done, 1)
            for q in two:
                nc.scalar.copy(M[:, 0, q], r_ps[q][0][:].rearrange("p (c d) -> p c d", c=FT)).then_inc(M_copied, 1)
            for i in range(NJ + 1):
                if i < NJ:
                    s, n = i % 2, jobs[i][2]
                    act.wait_ge(pq_done[0], i + 1)
                    if i >= 2:
                        act.wait_ge(r_done, i - 1)
                    nc.scalar.copy(PQ[0][s][:, 0:n], pq_ps[0][s][:, 0:n]).then_inc(pq_copied[0], 1)
                if i >= 1:
                    s, n = (i - 1) % 2, jobs[i - 1][2]
                    act.wait_ge(r_done, i)
                    if i >= 3:
                        act.wait_ge(mixed, i - 2)
                    nc.scalar.copy(R2[s][:, 0:n], r_ps[1][s][:, 0:n]).then_inc(r2_copied, 1)

        @block.tensor
        def _(pe):
            pe.wait_ge(chan_loaded, 48)
            for kind in two:
                for q in two:
                    for c in range(FT):
                        last = nc.tensor.matmul(r_ps[q][kind][:, c * P:(c + 1) * P], chan[:, kind, q, :], wblk[:, c, :],
                                                start=True, stop=True)
            last.then_inc(M_done, 1)

            def mix(i):
                s, kind, n, c = i % 2, 0 if i < FT else 1, jobs[i][2], i % FT
                if i == 0:
                    pe.wait_ge(M_copied, 4)
                if i >= 2:
                    pe.wait_ge(mixed, i - 1)
                for q in two:
                    pe.wait_ge(pq_copied[q], i + 1)
                    last = nc.tensor.matmul(r_ps[q][s][:, 0:n], M[:, kind, q, c, :], PQ[q][s][:, 0:n],
                                            start=True, stop=True)
                last.then_inc(r_done, 1)

            for i, (name, src, n, _, _, _, need) in enumerate(jobs):
                s = i % 2
                if i == 0:
                    pe.wait_ge(r0_loaded, 32)
                if name == "odd":
                    pe.wait_ge(odd_loaded, 32)
                if name == "r2":
                    pe.wait_ge(r2_loaded, 32)
                for q in two:
                    if i >= 2:
                        pe.wait_ge(pq_copied[q], i - 1)
                for k in range(len(src)):
                    if need == "d":
                        pe.wait_ge(d_done, k + 1)
                    if need == "u":
                        pe.wait_ge(u_done, k + 1 + (QT if name == "r2" else 0))
                    for q in two:
                        rhs = tab["r0"][q][:, k, 0:2 * n - 1:2] if name == "ctx" else tab[name][q][:, k, :]
                        last = nc.tensor.matmul(pq_ps[q][s][:, 0:n], src[k], rhs, start=(k == 0),
                                                stop=(k == len(src) - 1))
                        if k == len(src) - 1:
                            last.then_inc(pq_done[q], 1)
                if i >= 1:
                    mix(i - 1)
            mix(NJ - 1)


def attention(nc, a, t):
    with ExitStack() as x:
        sb = lambda name, shape, dt=F32: x.enter_context(nc.sbuf_tensor(name, shape, dt))
        sem = lambda name: x.enter_context(nc.semaphore(name))
        two = range(2)
        CH = 512
        KL = PAST + LAT
        NCH, KT = KL // CH, KEYS // P
        chunks = {1: [(c * CH, CH) for c in range(NCH)], 0: [(KL, CTX)]}
        w_h = sb("w_ukv_head", [P, NOPE + VH])
        V = sb("values", [P, KT, VH])
        qT = [sb(f"a_qT{s}", [QK, P]) for s in two]
        prob = [sb(f"prob{s}", [P, KL]) for s in two]
        PT = [sb(f"probT{c}", [P, CH]) for c in range(NCH)]
        mx, nmt = sb("chunk_max", [P, NCH]), sb("neg_max_t", [P, 1])
        nm = [sb(f"neg_max{s}", [P, 1]) for s in two]
        rs = [sb(f"row_sums{s}", [P, NCH]) for s in two]
        rst, rinv = sb("row_sum", [P, 1]), sb("row_inv", [P, 1])
        S_ps = [x.enter_context(nc.psum_tensor(f"S_ps{c}", [P, CH], F32)) for c in range(NCH)]
        PT_ps = [x.enter_context(nc.psum_tensor(f"PT_ps{b}", [P, CH], F32)) for b in two]
        O_ps = x.enter_context(nc.psum_tensor("O_ps", [P, CH], F32))
        w_loaded = sem("a_w_loaded")
        q_loaded = [sem(f"a_q_loaded{s}") for s in two]
        k_done, k_copied, v_done, v_copied = sem("a_k_done"), sem("a_k_copied"), sem("a_v_done"), sem("a_v_copied")
        s_done, mx_done, nm_done, exp_done = sem("a_scores"), sem("a_chunk_max"), sem("a_neg_max"), sem("a_exp")
        t_done, t_copied, pv_done, o_done = sem("a_probT"), sem("a_probT_copied"), sem("a_pv"), sem("a_out")
        chain, sums_done = sem("a_dve_chain"), sem("a_row_sums")
        kT, ckvT, O = t["kpeT"], t["ckvT"], t["O"]
        KJ = len(chunks[1]) + 1
        VG, VPB = 3, CH // VH
        k_banks = S_ps + [PT_ps[0]]
        v_banks = [PT_ps[1], O_ps, S_ps[0]]

        def cnt(h, i, per_lat=1, per_ctx=1):
            head = LT * per_lat + CT * per_ctx
            if is_int(i) and i > LT:
                return h * head + LT * per_lat + (i - LT) * per_ctx
            return h * head + i * per_lat

        def chunk_cnt(h, i):
            return cnt(h, i, NCH, 1)

        def kind(i):
            return 0 if is_int(i) and i >= LT else 1

        def before(i, depth):
            return i - depth + 1 if not is_int(i) or i >= depth - 1 else 0

        def steps(eng, step):
            for i in two:
                step(i, i, 0)
            with eng.Fori(1, LT // 2) as j:
                step(2 * j, 0, j)
                step(2 * j + 1, 1, j)
            for i in range(LT, NT + 1):
                step(i, i % 2, i // 2)

        PRIMED = 1
        block = x.enter_context(nc.Block())

        @block.sync
        def _(sp):
            with sp.Fori(0, H) as h:
                sp.wait_ge(v_done, PRIMED + VG * h)
                sp.dma_start(w_h[:], a["w_ukv"][0][:, bass.ds(h * (NOPE + VH), NOPE + VH)]).then_inc(w_loaded, 16)

                def step(i, s, j):
                    if is_int(i) and i == NT:
                        return
                    sp.wait_ge(s_done, PRIMED + chunk_cnt(h, before(i, 2)))
                    n = i - LT if is_int(i) and i >= LT else i + CT
                    src = a["s_q"][bass.ds(n, 1), :, bass.ds(h, 1), :].rearrange("n p h q -> (n p) (h q)")
                    sp.dma_start(qT[s][:], src).then_inc(q_loaded[s], 16)

                steps(sp, step)

        @block.tensor
        def _(pe):
            for done in (s_done, t_done, v_done):
                pe.sem_inc(done, PRIMED)
            with pe.Fori(0, H) as h:
                pe.wait_ge(w_loaded, 16 * (h + 1))
                pe.wait_ge(exp_done, PRIMED + chunk_cnt(h, 0))
                pe.wait_ge(o_done, PRIMED + cnt(h, 0))
                for c in range(KJ):
                    w = min(CH, KEYS - c * CH)
                    nc.tensor.matmul(k_banks[c][0:NOPE, 0:w], w_h[:, 0:NOPE], ckvT[:, c * CH:c * CH + w],
                                     start=True, stop=True).then_inc(k_done, 1)
                for g in range(VG):
                    if v_banks[g] is S_ps[0]:
                        pe.wait_ge(k_copied, KJ * h + 1)
                    for n in range(g * VPB, min((g + 1) * VPB, KT)):
                        last = nc.tensor.matmul(v_banks[g][:, (n % VPB) * VH:(n % VPB + 1) * VH],
                                                ckvT[:, n * P:(n + 1) * P], w_h[:, NOPE:], start=True, stop=True)
                    last.then_inc(v_done, 1)

                def step(i, s, j):
                    if not is_int(i) or i < NT:
                        pe.wait_ge(q_loaded[s], 16 * ((NT // 2) * h + j + 1))
                        for c, (k0, w) in enumerate(chunks[kind(i)]):
                            if is_int(i) and i == 0:
                                pe.wait_ge(k_copied, KJ * h + c + 1)
                                if c == 0:
                                    pe.wait_ge(v_copied, VG * (h + 1))
                            else:
                                pe.wait_ge(exp_done, PRIMED + chunk_cnt(h, i - 1) + min(c + 1, NCH))
                            if kind(i) == 0 and i == LT:
                                pe.wait_ge(k_copied, KJ * (h + 1))
                            nc.tensor.matmul(S_ps[c][:, 0:w], qT[s][:], kT[:, k0:k0 + w], start=True, stop=True)\
                                .then_inc(s_done, 1)
                    if not is_int(i) or i >= 1:
                        m, o = i - 1, 1 - s
                        ch = chunks[kind(m)]
                        if is_int(m) and m == 0:
                            pe.wait_ge(v_copied, VG * (h + 1))

                        def pv(c):
                            k0, w = ch[c]
                            pe.wait_ge(t_copied, PRIMED + chunk_cnt(h, m) + c + 1)
                            if c == 0:
                                pe.wait_ge(o_done, PRIMED + cnt(h, m))
                            for q in range(w // P):
                                last = nc.tensor.matmul(O_ps[:, 0:VH], PT[c][:, q * P:(q + 1) * P],
                                                        V[:, k0 // P + q, :], start=(c == 0 and q == 0),
                                                        stop=(c == len(ch) - 1 and q == w // P - 1))
                            if c == len(ch) - 1:
                                last.then_inc(pv_done, 1)

                        for c, (k0, w) in enumerate(ch):
                            pe.wait_ge(exp_done, PRIMED + chunk_cnt(h, m) + c + 1)
                            pe.wait_ge(t_copied, PRIMED + chunk_cnt(h, m) + max(c - 1, 0))
                            for q in range(w // P):
                                off = k0 - ch[0][0] + q * P
                                last = nc.tensor.transpose(PT_ps[c % 2][:, q * P:(q + 1) * P],
                                                           prob[o][:, off:off + P], t["ident"][:])
                            last.then_inc(t_done, 1)
                            if c >= 1:
                                pv(c - 1)
                        pv(len(ch) - 1)

                steps(pe, step)

        @block.scalar
        def _(act):
            act.sem_inc(exp_done, PRIMED)
            with act.Fori(0, H) as h:
                for c in range(KJ):
                    w = min(CH, KEYS - c * CH)
                    act.wait_ge(k_done, KJ * h + c + 1)
                    nc.scalar.copy(kT[0:NOPE, c * CH:c * CH + w], k_banks[c][0:NOPE, 0:w]).then_inc(k_copied, 1)

                def step(i, s, j):
                    if is_int(i) and i == NT:
                        return
                    act.wait_ge(nm_done, cnt(h, i) + 1)
                    act.wait_ge(t_done, PRIMED + chunk_cnt(h, before(i, 2)))
                    act.wait_ge(o_done, PRIMED + cnt(h, before(i, 2)))
                    for c, (k0, w) in enumerate(chunks[kind(i)]):
                        nc.scalar.activation(prob[s][:, c * CH:c * CH + w], S_ps[c][:, 0:w], ACT.Exp,
                                             bias=nm[s][:], scale=SCALE, accum_out=rs[s][:, c:c + 1])\
                            .then_inc(exp_done, 1)

                steps(act, step)

        @block.vector
        def _(dve):
            for done in (t_copied, o_done):
                dve.sem_inc(done, PRIMED)
            with dve.Fori(0, H) as h:
                for g in range(VG):
                    dve.wait_ge(v_done, PRIMED + VG * h + g + 1)
                    lo, hi = g * VPB, min((g + 1) * VPB, KT)
                    nc.vector.tensor_copy(V[:, lo:hi, :], v_banks[g][:, 0:(hi - lo) * VH]).then_inc(v_copied, 1)

                def step(i, s, j):
                    if not is_int(i) or i < NT:
                        ch = chunks[kind(i)]
                        for c, (k0, w) in enumerate(ch):
                            dve.wait_ge(s_done, PRIMED + chunk_cnt(h, i) + c + 1)
                            nc.vector.reduce_max(mx[:, c:c + 1], S_ps[c][:, 0:w], AX.X).then_inc(mx_done, 1)
                        dve.wait_ge(mx_done, chunk_cnt(h, i) + len(ch))
                        link = Chain(dve, chain, 1, cnt(h, i))
                        link.link(nc.vector.tensor_reduce(nmt[:], mx[:, 0:len(ch)], AX.X, ALU.max, negate=True))
                        nc.vector.tensor_scalar(nm[s][:], nmt[:], SCALE, None, ALU.mult).then_inc(nm_done, 1)
                    if not is_int(i) or i >= 1:
                        m, o = i - 1, 1 - s
                        ch = chunks[kind(m)]
                        for c, (k0, w) in enumerate(ch):
                            dve.wait_ge(t_done, PRIMED + chunk_cnt(h, m) + c + 1)
                            nc.vector.tensor_copy(PT[c][:, 0:w], PT_ps[c % 2][:, 0:w]).then_inc(t_copied, 1)
                        nc.vector.tensor_reduce(rst[:], rs[o][:, 0:len(ch)], AX.X, ALU.add).then_inc(sums_done, 1)
                        dve.wait_ge(sums_done, cnt(h, m) * 2 + 1)
                        nc.vector.reciprocal(rinv[:], rst[:]).then_inc(sums_done, 1)
                        dve.wait_ge(sums_done, cnt(h, m) * 2 + 2)
                        dve.wait_ge(pv_done, cnt(h, m) + 1)
                        n = m - LT if is_int(m) and m >= LT else m + CT
                        dst = O[:, bass.ds(n, 1), bass.ds(h * VH, VH)].rearrange("p n d -> p (n d)")
                        nc.vector.tensor_scalar(dst, O_ps[:, 0:VH], rinv[:], None, ALU.mult).then_inc(o_done, 1)

                steps(dve, step)


def mixing_out(nc, a, t):
    with ExitStack() as x:
        sb = lambda name, shape, dt=F32: x.enter_context(nc.sbuf_tensor(name, shape, dt))
        sem = lambda name: x.enter_context(nc.semaphore(name))
        ps = lambda name: x.enter_context(nc.psum_tensor(name, [P, 512], F32))
        two = range(2)
        FT, HD = FW // P, D // 2
        w_out = sb("w_out_sb", [P, DK, D])
        w_r = sb("w_router_sb", [P, DK, NE])
        gate = sb("gate1_rows", [P, 2, D])
        xt = [sb(f"o_x{s}", [P, D]) for s in two]
        o_st = [sb(f"o_attn{s}", [P, FW]) for s in two]
        fT = [sb(f"o_fmixT{s}", [P, FT, P]) for s in two]
        aT = [sb(f"o_attnT{s}", [P, FT, P]) for s in two]
        yg = [sb(f"gated{s}", [P, D]) for s in two]
        x2 = [sb(f"x2_{s}", [P, D]) for s in two]
        row = [sb(f"row{s}", [P, ROWW]) for s in two]
        hT = [sb(f"h2T{s}", [P, DK, P]) for s in two]
        ex = [sb(f"aff_exp{s}", [P, NE]) for s in two]
        ss, rs = [sb(f"o_ss{s}", [P, 1]) for s in two], [sb(f"o_rs{s}", [P, 1]) for s in two]
        ms, nm, se = sb("o_ms", [P, 1]), sb("o_nm", [P, 1]), [sb(f"o_se{s}", [P, 1]) for s in two]
        ri = sb("o_ri", [P, 1])
        aT_ps, l_ps = ps("o_aT_ps"), ps("o_logit_ps")
        y_ps = [[ps(f"o_y_ps{s}{h}") for h in two] for s in two]
        xT_ps = [ps(f"o_xT_ps{h}") for h in two]
        w_loaded = sem("o_w_loaded")
        x_loaded = [sem(f"o_x_loaded{s}") for s in two]
        acc_stored, row_stored = [sem(f"o_acc_st{s}") for s in two], [sem(f"o_row_st{s}") for s in two]
        staged, aT_done, aT_copied, y_done = sem("o_staged"), sem("o_aT"), sem("o_aT_copied"), sem("o_y")
        gated, added, ss_done, rs_done = sem("o_gated"), sem("o_added"), sem("o_ss_done"), sem("o_rs_done")
        xn_done, xT_done, hTa, hTv = sem("o_xn"), sem("o_xT"), sem("o_hTa"), sem("o_hTv")
        l_done, nm_done, ex_done, aff_done = sem("o_logits"), sem("o_nm_done"), sem("o_ex"), sem("o_aff")
        pchain, vchain, passed = sem("o_pool_chain"), sem("o_dve_chain"), sem("o_pool_waits_passed")
        mods, gs2, O, fmixT, AFF, ident = (t[k] for k in ("mods", "gs2", "O", "fmixT", "AFF", "ident"))
        SH = 3 * DK
        xp, xs = a["x_prompt"][0], a["x_sample"][0]
        block = x.enter_context(nc.Block())

        def kind(n):
            return 0 if is_int(n) and n < CT else 1

        def run(eng, step):
            run_steps(eng, step, 2, NT // 2, NT)

        @block.sync
        def _(sp):
            def step(n, s, j):
                if active(n, 0, NT - 1):
                    wait_slot(sp, added, n, 1, 2)
                    src = xp[n * P:(n + 1) * P, :] if kind(n) == 0 else xs[bass.ds((n - CT) * P, P), :]
                    sp.dma_start(xt[s][:], src).then_inc(x_loaded[s], 16)
                    if is_int(n) and n == 0:
                        w_v = a["w_out"][0].rearrange("(k p) n -> p k n", p=P)
                        sp.dma_start(w_out[:, FT:, :], w_v[:, FT:, :]).then_inc(w_loaded, 16)
                        sp.dma_start(w_out[:, 0:FT, :], w_v[:, 0:FT, :]).then_inc(w_loaded, 16)
                        sp.dma_start(gate[:], a["s_gates"][0].partition_broadcast(P)).then_inc(w_loaded, 16)
                        sp.dma_start(w_r[:], a["w_router"][0].rearrange("(k p) n -> p k n", p=P)).then_inc(w_loaded, 16)
                if active(n, 1, NT):
                    m, o, jm = n - 1, 1 - s, j - (1 - s)
                    sp.wait_ge(added, m + 1)
                    sp.dma_start(a["s_acc"][bass.ds(m * P, P), :], x2[o][:]).then_inc(acc_stored[o], 16)
                    sp.wait_ge(aff_done, 2 * (m + 1))
                    sp.dma_start(a["s_rows"][bass.ds(m * P, P), :], row[o][:]).then_inc(row_stored[o], 16)

            run(sp, step)
            for s in two:
                sp.wait_ge(acc_stored[s], 16 * (NT // 2))
                sp.wait_ge(row_stored[s], 16 * (NT // 2))

        @block.gpsimd
        def _(pool):
            pool = PoolWaits(pool, passed)

            def step(n, s, j):
                if active(n, 0, NT - 1):
                    wait_slot(pool, y_done, n, 1, 2)
                    nc.gpsimd.tensor_copy(fT[s][:], fmixT[:, :, bass.ds(n * P, P)]).then_inc(staged, 1)
                    nc.gpsimd.tensor_copy(o_st[s][:], at(O, n)).then_inc(staged, 1)
                if active(n, 1, NT):
                    m, o, jm = n - 1, 1 - s, j - (1 - s)
                    pool.wait_ge(ss_done, m + 1)
                    c = Chain(pool, pchain, 1, m)
                    c.link(nc.gpsimd.tensor_scalar(ms[:], ss[o][:], 1.0 / D, EPS, ALU.mult, ALU.add))
                    nc.gpsimd.tensor_tensor(rs[o][:], ms[:], t["neg_half"][:], ALU.pow).then_inc(rs_done, 1)
                if active(n, 0, NT - 1):
                    pool.wait_ge(gated, 2 * (n + 1))
                    pool.wait_ge(x_loaded[s], 16 * (j + 1))
                    wait_slot(pool, acc_stored[s], j, 16, 1)
                    wait_slot(pool, xn_done, n, 1, 2)
                    nc.gpsimd.tensor_tensor(x2[s][:], yg[s][:], xt[s][:], ALU.add).then_inc(added, 1)

            run(pool, step)

        @block.scalar
        def _(act):
            def step(n, s, j):
                if active(n, 0, NT - 1):
                    act.wait_ge(aT_done, n + 1)
                    nc.scalar.copy(aT[s][:], aT_ps[:]).then_inc(aT_copied, 1)
                if active(n, 1, NT):
                    m, o = n - 1, 1 - s
                    act.wait_ge(xT_done, 2 * m + 1)
                    wait_slot(act, l_done, m, 1, 2)
                    for k in range(DK // 2):
                        nc.scalar.activation(hT[o][:, k, :], xT_ps[0][:, k * P:(k + 1) * P], ACT.Identity,
                                             scale=gs2[:, k, kind(m):kind(m) + 1],
                                             bias=mods[:, SH + k, kind(m):kind(m) + 1]).then_inc(hTa, 1)
                    act.wait_ge(nm_done, m + 1)
                    wait_slot(act, aff_done, m, 2, 2)
                    nc.scalar.activation(ex[o][:], l_ps[:, 0:NE], ACT.Exp, bias=nm[:], accum_out=se[o][:])\
                        .then_inc(ex_done, 1)
                if active(n, 0, NT - 1):
                    act.wait_ge(added, n + 1)
                    wait_slot(act, rs_done, n, 1, 2)
                    wait_slot(act, row_stored[s], j, 16, 1)
                    wait_slot(act, xT_done, n, 2, 2)
                    nc.scalar.activation(row[s][:, 0:D], x2[s][:], ACT.Square, accum_out=ss[s][:]).then_inc(ss_done, 1)

            run(act, step)

        @block.vector
        def _(dve):
            dve.wait_ge(w_loaded, 64)

            def step(n, s, j):
                if active(n, 1, NT):
                    m, o, jm = n - 1, 1 - s, j - (1 - s)
                    dve.wait_ge(rs_done, m + 1)
                    nc.vector.tensor_scalar(row[o][:, 0:D], x2[o][:], rs[o][:], None, ALU.mult).then_inc(xn_done, 1)
                if active(n, 0, NT - 1):
                    dve.wait_ge(y_done, n + 1)
                    for h in two:
                        nc.vector.tensor_tensor(yg[s][:, h * HD:(h + 1) * HD], y_ps[s][h][:],
                                                gate[:, kind(n), h * HD:(h + 1) * HD], ALU.mult).then_inc(gated, 1)
                if active(n, 1, NT):
                    dve.wait_ge(xT_done, 2 * m + 2)
                    wait_slot(dve, l_done, m, 1, 2)
                    for k in range(DK // 2, DK):
                        nc.vector.tensor_scalar(hT[o][:, k, :], xT_ps[1][:, (k - DK // 2) * P:(k - DK // 2 + 1) * P],
                                                gs2[:, k, kind(m):kind(m) + 1], mods[:, SH + k, kind(m):kind(m) + 1],
                                                ALU.mult, ALU.add).then_inc(hTv, 1)
                    dve.wait_ge(l_done, m + 1)
                    nc.vector.tensor_reduce(nm[:], l_ps[:, 0:NE], AX.X, ALU.max, negate=True).then_inc(nm_done, 1)
                    dve.wait_ge(ex_done, m + 1)
                    Chain(dve, vchain, 1, m).link(nc.vector.reciprocal(ri[:], se[o][:]))
                    nc.vector.tensor_scalar(row[o][:, D:], ex[o][:], ri[:], None, ALU.mult).then_inc(aff_done, 1)
                    nc.vector.tensor_scalar(at(AFF, m), ex[o][:], ri[:], None, ALU.mult).then_inc(aff_done, 1)

            run(dve, step)

        @block.tensor
        def _(pe):
            pe.wait_ge(w_loaded, 64)

            def step(n, s, j):
                if active(n, 0, NT - 1):
                    pe.wait_ge(staged, 2 * (n + 1))
                    wait_slot(pe, aT_copied, n, 1, 1)
                    for k in range(FT):
                        last = nc.tensor.transpose(aT_ps[:, k * P:(k + 1) * P], o_st[s][:, k * P:(k + 1) * P], ident[:])
                    last.then_inc(aT_done, 1)
                    wait_slot(pe, gated, n, 2, 2)
                    for k in range(FT):
                        for h in two:
                            nc.tensor.matmul(y_ps[s][h][:], fT[s][:, k, :], w_out[:, FT + k, h * HD:(h + 1) * HD],
                                             start=(k == 0), stop=False)
                    pe.wait_ge(aT_copied, n + 1)
                    for k in range(FT):
                        for h in two:
                            last = nc.tensor.matmul(y_ps[s][h][:], aT[s][:, k, :], w_out[:, k, h * HD:(h + 1) * HD],
                                                    start=False, stop=(k == FT - 1))
                    last.then_inc(y_done, 1)
                if active(n, 1, NT):
                    m, o = n - 1, 1 - s
                    pe.wait_ge(xn_done, m + 1)
                    for b in two:
                        wait_slot(pe, (hTa, hTv)[b], m, DK // 2, 1)
                        for k in range(DK // 2):
                            c0 = (b * (DK // 2) + k) * P
                            last = nc.tensor.transpose(xT_ps[b][:, k * P:(k + 1) * P], row[o][:, c0:c0 + P], ident[:])
                        last.then_inc(xT_done, 1)
                    wait_slot(pe, ex_done, m, 1, 1)
                    for k in range(DK):
                        pe.wait_ge((hTa, hTv)[k // (DK // 2)], m * (DK // 2) + k % (DK // 2) + 1)
                        last = nc.tensor.matmul(l_ps[:, 0:NE], hT[o][:, k, :], w_r[:, k, :], start=(k == 0),
                                                stop=(k == DK - 1))
                    last.then_inc(l_done, 1)

            run(pe, step)


def routing(nc, a, t):
    with ExitStack() as x:
        sb = lambda name, shape, dt=F32: x.enter_context(nc.sbuf_tensor(name, shape, dt))
        sem = lambda name: x.enter_context(nc.semaphore(name))
        ps = lambda name: x.enter_context(nc.psum_tensor(name, [P, 512], F32))
        two = range(2)
        BITS = 30
        NONE = 512.0
        tri_f, tri, ones = sb("tri_f", [P, P]), sb("tri", [P, P], BF16), sb("ones_bf", [P, P], BF16)
        iota_f, iota = sb("iota_f", [P, CAP_L]), sb("iota", [P, CAP_L], BF16)
        pay_f, pay = sb("pay_f", [P, NT, 2]), sb("pay", [P, NT, 2], BF16)
        bit, cur, cand = (sb(n, [P, 2, NE], U32) for n in ("bit", "cur", "cand"))
        keep = sb("keep", [P, 2, NE])
        ge, cnt = sb("reaches", [P, NT, NE], BF16), sb("counts", [P, 2, NE], BF16)
        mk = sb("above_at", [P, NT, 2, NE], BF16)
        run = sb("tiles_before", [P, NT, 2, NE], BF16)
        total = sb("total", [P, 2, NE], BF16)
        above = sb("n_above", [P, 2, NE])
        pe_, pg = sb("pos_at", [P, NT, NE]), sb("pos_above", [P, NT, NE])
        pos = sb("pos", [P, NT, NE], BF16)
        hot = [sb(f"one_hot{s}", [P, LT, CAP_L], BF16) for s in two]
        hot_c = [sb(f"one_hot_ctx{s}", [P, CT, CAP_C], BF16) for s in two]
        ids = [sb(f"ids{s}", [P, 3, 2]) for s in two]
        n_ps, l_ps, c_ps = ps("count_ps"), ps("prefix_lat_ps"), ps("prefix_ctx_ps")
        id_ps = [ps(f"ids_ps{s}") for s in two]
        loaded, counted, totalled = sem("r_loaded"), sem("r_counted"), sem("r_totalled")
        v, pre_ready, pre_done = sem("r_dve"), sem("r_prefix_ready"), sem("r_prefix_done")
        hot_done, ids_done, ids_read, id_chain = sem("r_one_hot"), sem("r_ids"), sem("r_ids_read"), sem("r_ids_chain")
        setup = sem("r_setup")
        AFF, IDX = t["AFF"], t["IDX"]
        groups = ((0, 0, CT), (1, CT, NT))
        PRIMED = 1
        block = x.enter_context(nc.Block())

        @block.sync
        def _(sp):
            sp.dma_start(tri_f[:], a["k_before"]).then_inc(loaded, 16)
            sp.dma_start(iota_f[:], a["k_slots"].partition_broadcast(P)).then_inc(loaded, 16)
            sp.dma_start(pay_f[:], a["k_tile_part"].rearrange("(n p) q -> p n q", p=P)).then_inc(loaded, 16)

        @block.gpsimd
        def _(pool):
            pool.wait_ge(loaded, 48)
            nc.gpsimd.memset(ones[:], 1.0).then_inc(setup, 1)
            nc.gpsimd.tensor_copy(tri[:], tri_f[:]).then_inc(setup, 1)
            nc.gpsimd.tensor_copy(iota[:], iota_f[:]).then_inc(setup, 1)
            nc.gpsimd.tensor_copy(pay[:], pay_f[:]).then_inc(setup, 1)

        @block.vector
        def _(dve):
            dve.sem_inc(id_chain, PRIMED)
            nc.vector.memset(bit[:], 1 << (BITS - 1))
            Chain(dve, v, 1, 0).link(nc.vector.memset(cur[:], 0))
            PER = 5
            with dve.Fori(0, BITS) as b:
                c = Chain(dve, v, PER, b)
                c.base = b * PER + 1
                c.link(nc.vector.tensor_tensor(cand[:], cur[:], bit[:], ALU.bitwise_or))
                for k, n0, n1 in groups:
                    ins = nc.vector.tensor_tensor(
                        ge[:, n0:n1], AFF[:, n0:n1],
                        cand[:, k].bitcast(F32).unsqueeze(1).to_broadcast([P, n1 - n0, NE]), ALU.is_ge)
                c.link(ins)
                with nc.allow_low_precision(reason="counts up to 16 are exact in bfloat16"):
                    for k, n0, n1 in groups:
                        ins = nc.vector.tensor_reduce(cnt[:, k], ge[:, n0:n1].rearrange("p n e -> p e n"), AX.X, ALU.add)
                ins.then_inc(counted, 1)
                c.link(nc.vector.tensor_scalar(bit[:], bit[:], 1, None, ALU.logical_shift_right))
                dve.wait_ge(totalled, b + 1)
                for k, capacity in ((0, CAP_C), (1, CAP_L)):
                    ins = nc.vector.scalar_tensor_tensor(keep[:, k], n_ps[:, k * NE:(k + 1) * NE], float(capacity),
                                                         cand[:, k].bitcast(F32), ALU.is_ge, ALU.mult)
                c.link(ins)
                c.link(nc.vector.tensor_tensor(cur[:].bitcast(F32), cur[:].bitcast(F32), keep[:], ALU.max))
            c = Chain(dve, v, 99, 0)
            c.base = BITS * PER + 1
            for k, n0, n1 in groups:
                thr = cur[:, k].bitcast(F32).unsqueeze(1).to_broadcast([P, n1 - n0, NE])
                nc.vector.tensor_tensor(mk[:, n0:n1, 0], AFF[:, n0:n1], thr, ALU.is_gt)
                nc.vector.tensor_tensor(mk[:, n0:n1, 1], AFF[:, n0:n1], thr, ALU.is_equal)
                ins = nc.vector.memset(run[:, n0], 0.0)
            c.link(ins)
            for k, n0, n1 in groups:
                for n in range(n0 + 1, n1):
                    c.link(nc.vector.tensor_tensor(run[:, n], run[:, n - 1], mk[:, n - 1], ALU.add))
                ins = nc.vector.tensor_tensor(total[:, k], run[:, n1 - 1, 0], mk[:, n1 - 1, 0], ALU.add)
            ins.then_inc(pre_ready, 1)
            dve.wait_ge(pre_done, 1)
            c.link(nc.vector.tensor_copy(above[:], n_ps[:, 0:2 * NE]))
            for k, n0, n1 in groups:
                src = (c_ps, l_ps)[k][:, 0:(n1 - n0) * 2 * NE].rearrange("p (n q e) -> p n q e", q=2, e=NE)
                nc.vector.tensor_tensor(pe_[:, n0:n1], src[:, :, 1], above[:, k].unsqueeze(1)
                                        .to_broadcast([P, n1 - n0, NE]), ALU.add)
                ins = nc.vector.tensor_scalar(pg[:, n0:n1], src[:, :, 0], -NONE, None, ALU.add)
            c.link(ins)
            c.link(nc.vector.tensor_scalar(pe_[:], pe_[:], -NONE, None, ALU.add))
            c.link(nc.vector.tensor_tensor(pe_[:], pe_[:], mk[:, :, 1], ALU.mult))
            c.link(nc.vector.tensor_tensor(pg[:], pg[:], mk[:, :, 0], ALU.mult))
            c.link(nc.vector.tensor_tensor(pg[:], pg[:], pe_[:], ALU.add))
            c.link(nc.vector.tensor_scalar(pos[:], pg[:], NONE, None, ALU.add))
            dve.wait_ge(setup, 4)

            def index(e, s):
                dve.wait_ge(ids_done, PRIMED + e + 1)
                nc.vector.tensor_copy(ids[s][:, 0:2, :], id_ps[s][:, 0:4])
                nc.vector.tensor_copy(ids[s][0:CAP_C, 2, :], id_ps[s][0:CAP_C, 4:6]).then_inc(ids_read, 1)
                dve.wait_ge(ids_read, e + 1)
                for lo, hi, rows in ((0, 2, P), (2, 3, CAP_C)):
                    dst = IDX[0:rows, bass.ds(e, 1), lo:hi].rearrange("p e h -> p (e h)")
                    ins = nc.vector.scalar_tensor_tensor(dst, ids[s][0:rows, lo:hi, 0], float(P),
                                                         ids[s][0:rows, lo:hi, 1], ALU.mult, ALU.add)
                ins.then_inc(id_chain, 1)

            with dve.Fori(0, NE // 2) as j:
                for s in two:
                    dve.wait_ge(ids_done, PRIMED + 2 * j)
                    for dst, n0, n1, w in ((hot_c[s], 0, CT, CAP_C), (hot[s], CT, NT, CAP_L)):
                        ins = nc.vector.tensor_tensor(
                            dst[:], iota[:, 0:w].unsqueeze(1).to_broadcast([P, n1 - n0, w]),
                            pos[:, n0:n1, bass.ds(2 * j + s, 1)].to_broadcast([P, n1 - n0, w]), ALU.is_equal)
                    ins.then_inc(hot_done, 1)
                for s in two:
                    index(2 * j + s, s)
            dve.wait_ge(id_chain, PRIMED + NE)

        @block.tensor
        def _(pe):
            pe.sem_inc(ids_done, PRIMED)
            pe.wait_ge(setup, 4)
            with pe.Fori(0, BITS) as b:
                pe.wait_ge(counted, b + 1)
                nc.tensor.matmul(n_ps[:, 0:2 * NE], ones[:], cnt[:].rearrange("p k e -> p (k e)"), start=True, stop=True)\
                    .then_inc(totalled, 1)
            pe.wait_ge(pre_ready, 1)
            flat = lambda z, n0, n1: z[:, n0:n1].rearrange("p n q e -> p (n q e)")
            for k, n0, n1 in groups:
                w = (n1 - n0) * 2 * NE
                dst = (c_ps, l_ps)[k][:, 0:w]
                nc.tensor.matmul(dst, tri[:], flat(mk, n0, n1), start=True, stop=False)
                nc.tensor.matmul(dst, ones[:], flat(run, n0, n1), start=False, stop=True)
            nc.tensor.matmul(n_ps[:, 0:2 * NE], ones[:], total[:].rearrange("p k e -> p (k e)"), start=True, stop=True)\
                .then_inc(pre_done, 1)
            with pe.Fori(0, NE // 2) as j:
                for s in two:
                    pe.wait_ge(hot_done, 2 * j + s + 1)
                    pe.wait_ge(id_chain, PRIMED + 2 * j)
                    for hh in two:
                        for n in range(LT):
                            nc.tensor.matmul(id_ps[s][:, 2 * hh:2 * hh + 2], hot[s][:, n, hh * P:(hh + 1) * P],
                                             pay[:, CT + n, :], start=(n == 0), stop=(n == LT - 1))
                    for n in range(CT):
                        last = nc.tensor.matmul(id_ps[s][0:CAP_C, 4:6], hot_c[s][:, n, :], pay[:, n, :],
                                                start=(n == 0), stop=(n == CT - 1))
                    last.then_inc(ids_done, 1)


def experts(nc, a, t):
    with ExitStack() as x:
        sb = lambda name, shape, dt=F32: x.enter_context(nc.sbuf_tensor(name, shape, dt))
        sem = lambda name: x.enter_context(nc.semaphore(name))
        ps = lambda name: x.enter_context(nc.psum_tensor(name, [P, 512], F32))
        two = range(2)
        C = CAP_L + CAP_C
        parts = ((0, P, 1), (P, P, 1), (CAP_L, CAP_C, 0))
        NF, HD = DE // P, D // 2
        wg = [sb(f"w_gate{s}", [P, DK, DE]) for s in two]
        wu = [sb(f"w_up{s}", [P, DK, DE]) for s in two]
        wd = [sb(f"w_down{s}", [P, NF, D]) for s in two]
        gate = sb("gate2_rows", [P, 2, D])
        idx = [[sb(f"idx{s}{i}", [P, 1], U32) for i in range(3)] for s in two]
        rows = [sb(f"rows{s}", [P, 3, ROWW]) for s in two]
        aff = [sb(f"slot_aff{s}", [P, 3]) for s in two]
        xT = sb("xsT", [P, DK, C])
        act_g = [sb(f"silu_gate{b}", [P, C]) for b in two]
        hid = sb("hidT", [P, NF, C])
        ys = [sb(f"ys{i}", [P, D]) for i in range(3)]
        xT_ps = [ps(f"e_xT_ps{b}") for b in two]
        g_ps, u_ps = [ps(f"e_g_ps{b}") for b in two], [ps(f"e_u_ps{b}") for b in two]
        y_ps = [ps(f"e_y_ps{b}") for b in two]
        gate_loaded = sem("e_gate2_loaded")
        gu_loaded, d_loaded = [sem(f"e_gu_loaded{s}") for s in two], [sem(f"e_d_loaded{s}") for s in two]
        gathered = [sem(f"e_gathered{s}") for s in two]
        idx_ready, aff_done = sem("e_idx"), sem("e_slot_aff")
        xT_done, xTa, xTv = sem("e_xT"), sem("e_xTa"), sem("e_xTv")
        gu_done, silu_done, hid_done, y_done = sem("e_gate_up"), sem("e_silu"), sem("e_hid"), sem("e_y")
        ys_done, added = sem("e_ys"), sem("e_added")
        mods, gs2, IDX, ident = (t[k] for k in ("mods", "gs2", "IDX", "ident"))
        SH = 3 * DK
        block = x.enter_context(nc.Block())

        def pairs(eng, step):
            for s in two:
                step(s, s, 0)
            with eng.Fori(1, NE // 2) as j:
                for s in two:
                    step(2 * j + s, s, j)

        @block.sync
        def _(sp):
            sp.dma_start(gate[:], a["s_gates"][1].partition_broadcast(P)).then_inc(gate_loaded, 16)

            def load(e, s, j):
                wait_slot(sp, gu_done, e, NF, 2)
                for name, w in (("w_e_gate", wg), ("w_e_up", wu)):
                    src = a[name][0][bass.ds(e, 1)].rearrange("e (k p) f -> p (e k) f", p=P)
                    sp.dma_start(w[s][:], src).then_inc(gu_loaded[s], 16)
                wait_slot(sp, y_done, e, 6, 2)
                src = a["w_e_down"][0][bass.ds(e, 1)].rearrange("e (k p) f -> p (e k) f", p=P)
                sp.dma_start(wd[s][:], src).then_inc(d_loaded[s], 16)

            pairs(sp, load)

        @block.gpsimd
        def _(pool):
            passed = x.enter_context(nc.semaphore("e_pool_waits_passed"))
            pool = PoolWaits(pool, passed)

            def gather(e, s, j):
                pool.wait_ge(idx_ready, e + 1)
                wait_slot(pool, xT_done, e, DK, 2)
                wait_slot(pool, aff_done, e, 1, 2)
                for i, (_, n, _) in enumerate(parts):
                    nc.gpsimd.indirect_dma_start(
                        out=rows[s][0:n, i, :], out_offset=None, in_=a["s_rows"],
                        in_offset=bass.IndirectOffsetOnAxis(ap=idx[s][i][0:n, :], axis=0)).then_inc(gathered[s], 16)

            def scatter(e, s, j):
                pool.wait_ge(added, 48 * e)
                for i, (_, n, _) in enumerate(parts):
                    pool.wait_ge(ys_done, 6 * e + 2 * (i + 1))
                    nc.gpsimd.indirect_dma_start(
                        out=a["s_acc"], out_offset=bass.IndirectOffsetOnAxis(ap=idx[s][i][0:n, :], axis=0),
                        in_=ys[i][0:n, :], in_offset=None, compute_op=ALU.add).then_inc(added, 16)

            gather(0, 0, 0)
            gather(1, 1, 0)
            scatter(0, 0, 0)
            with pool.Fori(1, NE // 2) as j:
                gather(2 * j, 0, j)
                scatter(2 * j - 1, 1, j)
                gather(2 * j + 1, 1, j)
                scatter(2 * j, 0, j)
            scatter(NE - 1, 1, 0)
            pool.wait_ge(added, 48 * NE)

        @block.scalar
        def _(act):
            def step(e, s, j):
                for k in range(0, DK, 2):
                    act.wait_ge(xT_done, DK * e + k + 1)
                    wait_slot(act, gu_done, e, NF, 1)
                    for lo, hi, kind in ((0, CAP_L, 1), (CAP_L, C, 0)):
                        ins = nc.scalar.activation(xT[:, k, lo:hi], xT_ps[0][:, lo:hi], ACT.Identity,
                                                   scale=gs2[:, k, kind:kind + 1], bias=mods[:, SH + k, kind:kind + 1])
                    ins.then_inc(xTa, 1)
                for f in range(NF):
                    act.wait_ge(gu_done, NF * e + f + 1)
                    if not is_int(e) or NF * e + f >= 2:
                        act.wait_ge(hid_done, NF * e + f - 1)
                    nc.scalar.activation(act_g[f % 2][:], g_ps[f % 2][:, 0:C], ACT.Silu).then_inc(silu_done, 1)

            pairs(act, step)

        @block.vector
        def _(dve):
            dve.wait_ge(gate_loaded, 16)

            def stage_idx(e, s):
                for i, (_, n, _) in enumerate(parts):
                    src = IDX[0:n, bass.ds(e, 1), i:i + 1].rearrange("p e i -> p (e i)")
                    ins = nc.vector.tensor_copy(idx[s][i][0:n, :], src)
                ins.then_inc(idx_ready, 1)

            def step(e, s, j, stage_next=True):
                if stage_next:
                    dve.wait_ge(added, 48 * (e - 1) if not is_int(e) else 48 * max(e - 1, 0))
                    if not is_int(e) or e >= 1:
                        dve.wait_ge(added, 48 * e)
                    stage_idx(e + 1, 1 - s)
                for k in range(1, DK, 2):
                    dve.wait_ge(xT_done, DK * e + k + 1)
                    wait_slot(dve, gu_done, e, NF, 1)
                    for lo, hi, kind in ((0, CAP_L, 1), (CAP_L, C, 0)):
                        ins = nc.vector.tensor_scalar(xT[:, k, lo:hi], xT_ps[1][:, lo:hi], gs2[:, k, kind:kind + 1],
                                                      mods[:, SH + k, kind:kind + 1], ALU.mult, ALU.add)
                    ins.then_inc(xTv, 1)
                dve.wait_ge(gathered[s], 48 * (j + 1))
                for i, (_, n, _) in enumerate(parts):
                    ins = nc.vector.tensor_copy(aff[s][0:n, i:i + 1], rows[s][0:n, i, bass.ds(D + e, 1)])
                ins.then_inc(aff_done, 1)
                for f in range(NF):
                    dve.wait_ge(silu_done, NF * e + f + 1)
                    wait_slot(dve, y_done, e, 6, 1)
                    nc.vector.tensor_tensor(hid[:, f, :], act_g[f % 2][:], u_ps[f % 2][:, 0:C], ALU.mult)\
                        .then_inc(hid_done, 1)
                dve.wait_ge(aff_done, e + 1)
                wait_slot(dve, added, e, 48, 1)
                for i, (_, n, kind) in enumerate(parts):
                    for h in two:
                        dve.wait_ge(y_done, 6 * e + 2 * i + h + 1)
                        nc.vector.scalar_tensor_tensor(ys[i][0:n, h * HD:(h + 1) * HD], y_ps[h][0:n, :],
                                                       aff[s][0:n, i:i + 1], gate[0:n, kind, h * HD:(h + 1) * HD],
                                                       ALU.mult, ALU.mult).then_inc(ys_done, 1)

            stage_idx(0, 0)
            step(0, 0, 0)
            step(1, 1, 0)
            with dve.Fori(1, NE // 2 - 1) as j:
                step(2 * j, 0, j)
                step(2 * j + 1, 1, j)
            step(NE - 2, 0, NE // 2 - 1)
            step(NE - 1, 1, NE // 2 - 1, stage_next=False)

        @block.tensor
        def _(pe):
            def step(e, s, j):
                pe.wait_ge(gathered[s], 48 * (j + 1))
                for k in range(DK):
                    b = k % 2
                    pe.wait_ge((xTa, xTv)[b], (DK // 2) * e + k // 2)
                    for i, (c0, n, _) in enumerate(parts):
                        last = nc.tensor.transpose(xT_ps[b][:, c0:c0 + n], rows[s][0:n, i, k * P:(k + 1) * P],
                                                   ident[0:n, 0:n])
                    last.then_inc(xT_done, 1)
                pe.wait_ge(gu_loaded[s], 32 * (j + 1))
                for f in range(NF):
                    if not is_int(e) or NF * e + f >= 2:
                        pe.wait_ge(hid_done, NF * e + f - 1)
                    for w, dst in ((wg, g_ps), (wu, u_ps)):
                        for k in range(DK):
                            if f == 0:
                                pe.wait_ge((xTa, xTv)[k % 2], (DK // 2) * e + k // 2 + 1)
                            last = nc.tensor.matmul(dst[f % 2][:, 0:C], w[s][:, k, f * P:(f + 1) * P], xT[:, k, :],
                                                    start=(k == 0), stop=(k == DK - 1))
                    last.then_inc(gu_done, 1)
                pe.wait_ge(d_loaded[s], 16 * (j + 1))
                for i, (c0, n, _) in enumerate(parts):
                    for h in two:
                        m = 6 * e + 2 * i + h
                        if not is_int(m) or m >= 2:
                            pe.wait_ge(ys_done, m - 1)
                        for f in range(NF):
                            if i == 0 and h == 0:
                                pe.wait_ge(hid_done, NF * e + f + 1)
                            last = nc.tensor.matmul(y_ps[h][0:n, :], hid[:, f, c0:c0 + n],
                                                    wd[s][:, f, h * HD:(h + 1) * HD], start=(f == 0), stop=(f == NF - 1))
                        last.then_inc(y_done, 1)

            pairs(pe, step)


def final_norm(nc, a, t):
    with ExitStack() as x:
        sb = lambda name, shape, dt=F32: x.enter_context(nc.sbuf_tensor(name, shape, dt))
        sem = lambda name: x.enter_context(nc.semaphore(name))
        NS = 6
        fg = sb("final_g_rows", [P, D])
        xt = [sb(f"z{s}", [P, D]) for s in range(NS)]
        sq = [sb(f"z_sq{s}", [P, D]) for s in range(2)]
        yt = [sb(f"y{s}", [P, D]) for s in range(NS)]
        ss, rs = [sb(f"z_ss{s}", [P, 1]) for s in range(NS)], [sb(f"z_rs{s}", [P, 1]) for s in range(NS)]
        ms = [sb(f"z_ms{s}", [P, 1]) for s in range(NS)]
        g_loaded = sem("z_g_loaded")
        loaded, stored = [sem(f"z_loaded{s}") for s in range(NS)], [sem(f"z_stored{s}") for s in range(NS)]
        ss_done, ms_done, rs_done, y_done = sem("z_ss"), sem("z_ms"), sem("z_rs"), sem("z_y")
        passed = sem("z_pool_waits_passed")
        yp, ysm = a["y_prompt"][0], a["y_sample"][0]
        block = x.enter_context(nc.Block())

        def tiles(eng, step):
            for s in range(NS):
                step(s, s, 0)
            with eng.Fori(1, NT // NS) as r:
                for s in range(NS):
                    step(r * NS + s, s, r)

        @block.sync
        def _(sp):
            sp.dma_start(fg[:], a["final_g"].partition_broadcast(P)).then_inc(g_loaded, 16)

            def step(n, s, r):
                wait_slot(sp, y_done, n, 1, NS)
                sp.dma_start(xt[s][:], a["s_acc"][bass.ds(n * P, P), :]).then_inc(loaded[s], 16)

            tiles(sp, step)

        @block.scalar
        def _(act):
            def square(n, s, r):
                act.wait_ge(loaded[s], 16 * (r + 1))
                wait_slot(act, ms_done, n, 1, NS)
                wait_slot(act, ss_done, n, 1, 2)
                nc.scalar.activation(sq[s % 2][:], xt[s][:], ACT.Square, accum_out=ss[s][:]).then_inc(ss_done, 1)

            def store(n, s, r):
                act.wait_ge(y_done, n + 1)
                dst = yp[n * P:(n + 1) * P, :] if is_int(n) and n < CT else ysm[bass.ds((n - CT) * P, P), :]
                act.dma_start(dst, yt[s][:]).then_inc(stored[s], 16)

            for s in range(NS):
                square(s, s, 0)
            for s in range(NS):
                store(s, s, 0)
            with act.Fori(1, NT // NS) as r:
                for s in range(NS):
                    square(r * NS + s, s, r)
                for s in range(NS):
                    store(r * NS + s, s, r)
            for s in range(NS):
                act.wait_ge(stored[s], 16 * (NT // NS))

        @block.gpsimd
        def _(pool):
            pool = PoolWaits(pool, passed)

            def step(n, s, r):
                pool.wait_ge(ss_done, n + 1)
                nc.gpsimd.tensor_scalar(ms[s][:], ss[s][:], 1.0 / D, EPS, ALU.mult, ALU.add).then_inc(ms_done, 1)
                pool.wait_ge(ms_done, n + 1)
                wait_slot(pool, y_done, n, 1, NS)
                nc.gpsimd.tensor_tensor(rs[s][:], ms[s][:], t["neg_half"][:], ALU.pow).then_inc(rs_done, 1)

            tiles(pool, step)

        @block.vector
        def _(dve):
            dve.wait_ge(g_loaded, 16)

            def step(n, s, r):
                dve.wait_ge(rs_done, n + 1)
                wait_slot(dve, stored[s], r, 16, 1)
                nc.vector.scalar_tensor_tensor(yt[s][:], xt[s][:], rs[s][:], fg[:], ALU.mult, ALU.mult)\
                    .then_inc(y_done, 1)

            tiles(dve, step)


_INS = ['x_prompt', 'x_sample', 'cache_ckv', 'cache_kpe', 'c', 'c_ctx', 'w_mod', 'b_mod', 'norm1_g', 'w_in',
        'q_norm_g', 'w_uq', 'kv_norm_g', 'w_ukv', 'w_fmix', 'w_out', 'norm2_g', 'w_router', 'w_e_gate',
        'w_e_up', 'w_e_down', 'final_g']
_OUTS = [('y_prompt', (1, CTX, D)), ('y_sample', (1, LAT, D)), ('state_ckv', (1, 1, CTX, KVL)),
         ('state_kpe', (1, 1, CTX, ROPE))]
_SCRATCH = [('s_gates', (2, 2, D)), ('s_state', (NTOK, KVL + ROPE)), ('s_q', (NT, QK, H, P)),
            ('s_acc', (NTOK, D)), ('s_rows', (NTOK, ROWW))]


def constants():
    f32 = np.float32
    k = {'k_ident': np.eye(P, dtype=f32)}
    nf = ROPE // 4
    inv = (f32(10000.0) ** (-np.arange(nf, dtype=f32) / f32(nf))).astype(f32)
    rows = np.repeat(np.arange(LAT // 64, dtype=f32), 64)
    cols = np.tile(np.arange(64, dtype=f32), LAT // 64)
    ang = np.concatenate([rows[:, None] * inv, cols[:, None] * inv], axis=-1).astype(f32)
    ang = np.concatenate([np.zeros((CTX, 2 * nf), f32), ang]).astype(np.float64)
    cos, sin = np.cos(ang).astype(f32), np.sin(ang).astype(f32)
    k['k_rope_cos'] = np.concatenate([cos, cos], axis=1)
    k['k_rope_sin'] = np.concatenate([-sin, sin], axis=1)
    def dft(t, f):
        ang = 2 * np.pi * ((np.arange(t)[:, None] * np.asarray(f)[None, :]) % LAT) / LAT
        return np.cos(ang).astype(f32), np.sin(ang).astype(f32)

    k['k_cos_odd'], k['k_sin_odd'] = dft(LAT // 2, np.arange(1, LAT // 2, 2))
    k['k_cos_r0'], k['k_sin_r0'] = dft(LAT // 4, np.arange(0, LAT // 2 + 1, 4))
    k['k_cos_r2'], k['k_sin_r2'] = dft(LAT // 4, np.arange(2, LAT // 2, 4))
    g = 64
    ang = 2 * np.pi * ((np.arange(g)[:, None] * np.arange(g)[None, :]) % g) / g
    blk = np.zeros((P, 2, 2, P))
    for kind, n in enumerate((CTX, LAT)):
        for q, m in enumerate((np.cos(ang), np.sin(ang))):
            for b in range(2):
                blk[b * g:(b + 1) * g, kind, q, b * g:(b + 1) * g] = m / np.sqrt(float(n) * g)
    k['k_chan'] = blk.astype(f32)
    k['k_before'] = np.triu(np.ones((P, P), f32), 1)
    k['k_slots'] = np.arange(CAP_L, dtype=f32)
    k['k_tile_part'] = np.stack([np.arange(NTOK) // P, np.arange(NTOK) % P], axis=1).astype(f32)
    return k


def kernel(**inputs):
    import concourse.bacc as _bacc
    from concourse.bass_utils import run_bass_kernel_spmd as _run

    nc = _bacc.Bacc("TRN2", target_bir_lowering=False, num_devices=1)
    arrays, aps = {}, {}
    host = {name: np.ascontiguousarray(inputs[name]) for name in _INS}
    host.update(constants())
    for name, v in host.items():
        arrays[f"in_{name}"] = v
        aps[name] = nc.dram_tensor(f"in_{name}", v.shape, mybir.dt.from_np(v.dtype), kind="ExternalInput").ap()
    for name, shape in _OUTS:
        aps[name] = nc.dram_tensor(f"out_{name}", shape, F32, kind="ExternalOutput").ap()
    for name, shape in _SCRATCH:
        aps[name] = nc.dram_tensor(name, shape, F32, kind="Internal").ap()
    program(nc, aps)
    r = _run(nc, [arrays], core_ids=[0])
    return tuple(r.results[0][f"out_{name}"] for name, _ in _OUTS)
```

```python
import numpy as np
from contextlib import ExitStack

import concourse.bass as bass
from concourse import mybir

F32 = mybir.dt.float32
BF16 = mybir.dt.bfloat16
F32R = mybir.dt.float32r
U32 = mybir.dt.uint32
ACT = mybir.ActivationFunctionType
ALU = mybir.AluOpType
AX = mybir.AxisListType

P = 128
D = 1024
DK = D // P
CTX, LAT, PAST = 256, 2048, 512
CT, LT, KC = CTX // P, LAT // P, PAST // P
NT = CT + LT
NTOK = CTX + LAT
KEYS = PAST + LAT + CTX
H = 8
NOPE, ROPE, VH = 64, 32, 64
QK = NOPE + ROPE
QL, KVL = 256, 128
FW = 512
LATW = QL + KVL + ROPE
NE = 16
CAP_L, CAP_C = 2 * LAT // NE, 2 * CTX // NE
DE = 512
EPS = 1e-6
SCALE = float(QK) ** -0.5
VEC_BIAS, VEC_ROWS = 4 * DK, 10 * DK
ROWW = D + NE


def is_int(n):
    return isinstance(n, int)


def active(n, first, last):
    return not is_int(n) or first <= n <= last


def wait_slot(eng, sem, m, per, depth):
    if not is_int(m) or m >= depth:
        eng.wait_ge(sem, (m - depth + 1) * per)


class Chain:

    def __init__(self, eng, sem, per, m):
        self.eng, self.sem, self.base, self.n, self.per = eng, sem, m * per, 0, per

    def link(self, ins):
        self.n += 1
        assert self.n <= self.per
        ins.then_inc(self.sem, 1)
        self.eng.wait_ge(self.sem, self.base + self.n)


class PlainWaits:

    def __init__(self, eng, passed):
        self.eng, self.passed = eng, passed

    def wait_ge(self, sem, value):
        self.eng.wait_ge(sem, value)
        if not is_int(value):
            self.eng.sem_inc(self.passed, 1)

    def Fori(self, *args):
        return self.eng.Fori(*args)


def run_steps(eng, step, loop_from, loop_to, last):
    for n in range(2 * loop_from):
        step(n, n % 2, n // 2)
    with eng.Fori(loop_from, loop_to) as j:
        step(2 * j, 0, j)
        step(2 * j + 1, 1, j)
    for n in range(2 * loop_to, last + 1):
        step(n, n % 2, n // 2)


def at(v, m):
    if is_int(m):
        return v[:, m]
    names = "abcd"[:len(v.shape) - 2]
    return v[:, bass.ds(m, 1)].rearrange(f"p o {' '.join(names)} -> p (o {names[0]}) {' '.join(names[1:])}")


def split_hi(dve, hi, src):
    return dve.tensor_copy(hi, src)


def split_lo(eng, lo, src, hi):
    return eng.tensor_tensor(lo, src, hi.bitcast(F32), ALU.subtract)


def program(nc, a):
    with ExitStack() as ctx:
        sb = lambda name, shape, dt=F32: ctx.enter_context(nc.sbuf_tensor(name, shape, dt))
        pers = {
            "ident": sb("ident", [P, P]),
            "mods": sb("mods", [P, 6 * DK, 2]),
            "gs1": sb("gs1", [P, DK, 2]),
            "gs2": sb("gs2", [P, DK, 2]),
            "neg_half": sb("neg_half", [P, 1]),
            "vec_cols": sb("vec_cols", [P, VEC_ROWS]),
            "silu_cols": sb("silu_cols", [P, 2, DK]),
            "AFF": sb("aff", [P, NT, NE]),
            "IDX": sb("slot_row", [P, NE, 3], U32),
            "sems": [],
        }
        modulation(nc, a, pers)
        with ExitStack() as mid:
            sbm = lambda name, shape, dt=F32: mid.enter_context(nc.sbuf_tensor(name, shape, dt))
            pers["F"] = pers["O"] = sbm("f_in_attn_out", [P, NT, FW])
            pers["ckvT"], pers["kpeT"] = sbm("ckvT", [P, KEYS]), sbm("kpeT", [P, KEYS])
            mixing_in(nc, a, pers)
            clear_semaphores(nc, pers["sems"])
            pers["fmixT"] = sbm("fmixT", [P, FW // P, NTOK])
            fourier(nc, a, pers)
            context_attention(nc, a, pers)
            attention(nc, a, pers)
            clear_semaphores(nc, pers["sems"])
            mixing_out(nc, a, pers)
        with ExitStack() as ex:
            pers["expert_weights"] = ExpertWeights(nc, a, ex)
            routing(nc, a, pers)
            experts(nc, a, pers)
        final_norm(nc, a, pers)


def clear_semaphores(nc, sems):
    nums = sorted(s.num for s in sems)
    runs = []
    for n in nums:
        if runs and runs[-1][1] == n:
            runs[-1][1] = n + 1
        else:
            runs.append([n, n + 1])
    with nc.Block() as block:
        @block.gpsimd
        def _(pool):
            for first, end in runs:
                pool.sem_clear(range(first, end))
    sems.clear()


def modulation(nc, a, t):
    SEGS = 2
    BC = 256
    NB, NPS = SEGS * D // BC, 4
    with ExitStack() as x:
        sb = lambda name, shape, dt=F32: x.enter_context(nc.sbuf_tensor(name, shape, dt))
        sem = lambda name: t["sems"].append(x.enter_context(nc.semaphore(name))) or t["sems"][-1]
        wm = [sb(f"wm{n}", [P, DK, BC]) for n in range(NB)]
        vrow, mrow = sb("vec_rows", [VEC_ROWS, P]), sb("mod_rows", [2, SEGS * D])
        v_ps = x.enter_context(nc.psum_tensor("vec_ps", [P, 512], F32))
        mp = [x.enter_context(nc.psum_tensor(f"mod_ps{s}", [P, 512], F32)) for s in range(NPS)]
        w_loaded = [sem(f"mod_w_loaded{n}") for n in range(NB)]
        vec_loaded, vecT_done, vecT_copied = sem("mod_vec_loaded"), sem("mod_vecT"), sem("mod_vecT_copied")
        silu_done, block_done, block_read = sem("mod_silu"), sem("mod_block_done"), sem("mod_block_read")
        chain, modT_done, biased = sem("mod_chain"), sem("mod_transposed"), sem("mod_biased")
        mods, gs1, ident, vcol, scol = (t[k] for k in ("mods", "gs1", "ident", "vec_cols", "silu_cols"))
        w_v = a["w_mod"][0].rearrange("(k p) n -> p k n", p=P)
        block = x.enter_context(nc.Block())

        @block.sync
        def _(sp):
            sp.dma_start(ident[:], a["k_ident"]).then_inc(vec_loaded, 16)
            rows = (("c_ctx", a["c_ctx"]), ("c", a["c"][0]), ("norm1_g", a["norm1_g"][0]),
                    ("norm2_g", a["norm2_g"][0]), ("b_mod", a["b_mod"][0]))
            r = 0
            for _, src in rows:
                n = src.shape[0] // P
                sp.dma_start(vrow[r:r + n, :], src.rearrange("(k p) -> k p", p=P)).then_inc(vec_loaded, 16)
                r += n
            for n in range(NB):
                sp.dma_start(wm[n][:], w_v[:, :, n * BC:(n + 1) * BC]).then_inc(w_loaded[n], 16)

        @block.tensor
        def _(pe):
            pe.wait_ge(vec_loaded, 96)
            nc.tensor.transpose(v_ps[:, 0:VEC_ROWS], vrow[:], ident[0:VEC_ROWS, 0:VEC_ROWS]).then_inc(vecT_done, 1)
            pe.wait_ge(silu_done, 1)
            for n in range(NB):
                pe.wait_ge(w_loaded[n], 16)
                if n >= NPS:
                    pe.wait_ge(block_read, n - NPS + 1)
                for k in range(DK):
                    last = nc.tensor.matmul(mp[n % NPS][0:2, 0:BC], scol[:, :, k], wm[n][:, k, :],
                                            start=(k == 0), stop=(k == DK - 1))
                last.then_inc(block_done, 1)
            pe.wait_ge(block_read, NB)
            for q in range(SEGS * DK):
                last = nc.tensor.transpose(v_ps[:, 2 * q:2 * q + 2], mrow[:, q * P:(q + 1) * P], ident[0:2, 0:2])
            last.then_inc(modT_done, 1)

        @block.scalar
        def _(act):
            act.wait_ge(vecT_copied, 1)
            nc.scalar.activation(scol[:], vcol[:, 0:2 * DK].rearrange("p (c k) -> p c k", c=2), ACT.Silu)\
                .then_inc(silu_done, 1)

        @block.vector
        def _(dve):
            nc.vector.memset(t["neg_half"][:], -0.5)
            dve.wait_ge(vecT_done, 1)
            nc.vector.tensor_copy(vcol[:], v_ps[:, 0:VEC_ROWS]).then_inc(vecT_copied, 1)
            dve.wait_ge(vecT_copied, 1)
            for n in range(NB):
                dve.wait_ge(block_done, n + 1)
                nc.vector.tensor_copy(mrow[:, n * BC:(n + 1) * BC], mp[n % NPS][0:2, 0:BC]).then_inc(block_read, 1)
            dve.wait_ge(modT_done, 1)
            bias = vcol[:, VEC_BIAS:VEC_BIAS + SEGS * DK].unsqueeze(2).to_broadcast([P, SEGS * DK, 2])
            nc.vector.tensor_tensor(mods[:, 0:SEGS * DK, :],
                                    v_ps[:, 0:2 * SEGS * DK].rearrange("p (q k) -> p q k", k=2), bias, ALU.add)\
                .then_inc(biased, 1)
            dve.wait_ge(biased, 1)
            link = Chain(dve, chain, 2, 0).link
            scaled_gain(nc.vector, link, gs1, mods, vcol, 1, 2)


def scaled_gain(dve, link, out, mods, vcol, seg, vec):
    link(dve.tensor_scalar(out[:], mods[:, seg * DK:(seg + 1) * DK, :], 1.0, None, ALU.add))
    gain = vcol[:, vec * DK:(vec + 1) * DK].unsqueeze(2).to_broadcast([P, DK, 2])
    link(dve.tensor_tensor(out[:], out[:], gain, ALU.mult))


def mixing_in(nc, a, t):
    with ExitStack() as x:
        sb = lambda name, shape, dt=F32: x.enter_context(nc.sbuf_tensor(name, shape, dt))
        sem = lambda name: t["sems"].append(x.enter_context(nc.semaphore(name))) or t["sems"][-1]
        ps = lambda name: x.enter_context(nc.psum_tensor(name, [P, 512], F32))
        two = range(2)
        IN_W, HK, KQ = LATW + FW, DK // 2, QL // P
        WR, EARLY = 4, 3
        raw = [sb(f"w_raw{s}", [P, IN_W]) for s in range(WR)]
        w_hi = sb("w_in_hi", [P, DK, IN_W], F32R)
        w_lo = sb("w_in_lo", [P, DK, IN_W], F32R)
        uq_hi, uq_lo = sb("w_uq_hi", [P, KQ, H * QK], F32R), sb("w_uq_lo", [P, KQ, H * QK], F32R)
        qg, kvg = sb("qg", [P, QL]), sb("kvg", [P, KVL])
        cs, sn = sb("rope_cos", [P, NT, ROPE]), sb("rope_sin", [P, NT, ROPE])
        ckv_c, kpe_c = sb("ckv_cache", [P, KC, KVL]), sb("kpe_cache", [P, KC, P])
        xt, xn = sb("x_tile", [P, D]), sb("xn", [P, D])
        junk, junk_p = sb("junk", [P, D], BF16), sb("junk_p", [P, QL + KVL], BF16)
        ssx, msx, rsx = sb("ssx", [P, 1]), sb("msx", [P, 1]), sb("rsx", [P, 1])
        hT, h_hi, h_lo = sb("hT", [P, DK, P]), sb("hT_hi", [P, DK, P], F32R), sb("hT_lo", [P, DK, P], F32R)
        pa = sb("latents", [P, LATW])
        ssp, msp, rsp = sb("ssp", [P, 2]), sb("msp", [P, 2]), sb("rsp", [P, 2])
        rt = sb("rope_t", [P, 2, ROPE])
        tm = sb("normed", [P, 4 * P])
        KPE0 = QL + KVL + NOPE
        qn_hi, qn_lo = sb("qnT_hi", [P, KQ, P], F32R), sb("qnT_lo", [P, KQ, P], F32R)
        q_sb, qt_ = sb("q_sb", [P, H, QK]), sb("q_rope_t", [P, 2, H, ROPE])
        qT = sb("qT", [QK, H, P])
        xT_ps = [ps("xT_ps0"), ps("xT_ps1")]
        pa_ps, pf_ps, sT_ps = ps("pa_ps"), ps("pf_ps"), ps("sT_ps")
        q_ps, qT_ps = [ps("q_ps0"), ps("q_ps1")], ps("qT_ps")
        HH = H // 2
        pieces = [(k, IN_W, w_hi, w_lo) for k in range(DK)] + [(k, H * QK, uq_hi, uq_lo) for k in range(KQ)]

        w_loaded = [sem(f"in_w_loaded{s}") for s in range(WR)]
        whi_done, wlo_done = sem("in_w_hi"), sem("in_w_lo")
        rows_loaded, cache_loaded = sem("in_rows_loaded"), sem("in_cache_loaded")
        x_loaded, st_stored, q_stored = sem("in_x_loaded"), sem("in_state_stored"), sem("in_q_stored")
        ssx_done, rsx_done, xn_done, xT_done = sem("in_ssx"), sem("in_rsx"), sem("in_xn"), sem("in_xT")
        hTa, hTv, hhi_done, hlo_done = sem("in_hT_act"), sem("in_hT_dve"), sem("in_h_hi"), sem("in_h_lo")
        pa_done, pf_done, pa_copied, f_copied = sem("in_pa"), sem("in_pf"), sem("in_pa_copied"), sem("in_f_copied")
        ssp_done, rsp_done, norm_done, kpe_done = sem("in_ssp"), sem("in_rsp"), sem("in_norms"), sem("in_kpe")
        sT_done, qn_rounded, sT_read = sem("in_sT"), sem("in_qn_hi"), sem("in_sT_read")
        q_done, qa_copied, qv_copied, q_roped = sem("in_q"), sem("in_qa"), sem("in_qv"), sem("in_q_roped")
        qT_done, qTa, qTv = sem("in_qT"), sem("in_qTa"), sem("in_qTv")
        passed = sem("in_pool_waits_passed")
        px, pp, pq, zeroed = sem("in_pool_x"), sem("in_pool_p"), sem("in_pool_q"), sem("in_zeroed")
        cT_done, cT_read, final_st = sem("in_cacheT"), sem("in_cacheT_read"), sem("in_states_out")
        mods, gs1, F, ckvT, kpeT, ident = (t[k] for k in ("mods", "gs1", "F", "ckvT", "kpeT", "ident"))
        xp, xs = a["x_prompt"][0], a["x_sample"][0]
        LAST = NT + 1
        block = x.enter_context(nc.Block())

        def key_col(m):
            if is_int(m) and m < CT:
                return PAST + LAT + m * P
            return PAST + (m - CT) * P

        def last_done(eng, sem, m, per=1):
            wait_slot(eng, sem, m, per, 1)

        def steps(eng, step):
            for n in range(CT + 1):
                step(n)
            with eng.Fori(CT + 1, NT - 1) as n:
                step(n)
            for n in range(NT - 1, LAST + 1):
                step(n)

        @block.sync
        def _(sp):
            def load_x(n):
                last_done(sp, xn_done, n)
                src = xp[n * P:(n + 1) * P, :] if is_int(n) and n < CT else xs[bass.ds((n - CT) * P, P), :]
                sp.dma_start(xt[:], src).then_inc(x_loaded, 16)

            load_x(0)
            w_v = a["w_in"][0].rearrange("(k p) n -> p k n", p=P)
            uq_v = a["w_uq"][0].rearrange("(k p) n -> p k n", p=P)
            for i, (k, w, hi, _) in enumerate(pieces):
                if i >= WR:
                    sp.wait_ge(whi_done, i - WR + 1)
                    sp.wait_ge(wlo_done, i - WR + 1)
                sp.dma_start(raw[i % WR][:, 0:w], (uq_v if hi is uq_hi else w_v)[:, k, :]).then_inc(w_loaded[i % WR], 16)

            def step(n):
                if active(n, 0, NT - 2):
                    load_x(n + 1)
                if active(n, 1, NT):
                    m = n - 1
                    sp.wait_ge(norm_done, 2 * (m + 1))
                    sp.wait_ge(kpe_done, m + 1)
                    sp.dma_start(a["s_state"][bass.ds(m * P, P), 0:KVL], tm[:, QL:QL + KVL]).then_inc(st_stored, 16)
                    sp.dma_start(a["s_state"][bass.ds(m * P, P), KVL:], tm[:, KPE0:KPE0 + ROPE]).then_inc(st_stored, 16)
                if active(n, 2, LAST):
                    m = n - 2
                    sp.wait_ge(qTa, m + 1)
                    sp.wait_ge(qTv, m + 1)
                    dst = a["s_q"][m] if is_int(m) else a["s_q"][bass.ds(m, 1)].rearrange("o p h q -> (o p) h q")
                    sp.dma_start(dst, qT[:]).then_inc(q_stored, 16)

            steps(sp, step)
            sp.wait_ge(st_stored, 32 * NT)
            sp.wait_ge(q_stored, 16 * NT)
            sp.dma_start(a["state_ckv"][0, 0], a["s_state"][0:CTX, 0:KVL]).then_inc(final_st, 16)
            sp.dma_start(a["state_kpe"][0, 0], a["s_state"][0:CTX, KVL:]).then_inc(final_st, 16)
            sp.wait_ge(final_st, 32)

        @block.scalar
        def _(act):
            act.wait_ge(zeroed, 2)
            act.dma_start(ckv_c[:], a["cache_ckv"][0, 0].rearrange("(n p) r -> p n r", p=P)).then_inc(cache_loaded, 16)
            act.dma_start(kpe_c[:, :, NOPE:QK], a["cache_kpe"][0, 0].rearrange("(n p) r -> p n r", p=P))\
                .then_inc(cache_loaded, 16)
            act.dma_start(qg[:], a["q_norm_g"].partition_broadcast(P)).then_inc(rows_loaded, 16)
            act.dma_start(kvg[:], a["kv_norm_g"].partition_broadcast(P)).then_inc(rows_loaded, 16)
            act.dma_start(cs[:], a["k_rope_cos"].rearrange("(n p) r -> p n r", p=P)).then_inc(rows_loaded, 16)
            act.dma_start(sn[:], a["k_rope_sin"].rearrange("(n p) r -> p n r", p=P)).then_inc(rows_loaded, 16)

            def squares(n):
                act.wait_ge(x_loaded, 16 * (n + 1))
                last_done(act, rsx_done, n)
                last_done(act, ssx_done, n)
                nc.scalar.activation(junk[:], xt[:], ACT.Square, accum_out=ssx[:]).then_inc(ssx_done, 1)

            def modulate(n):
                kind = 0 if is_int(n) and n < CT else 1
                act.wait_ge(xT_done, 2 * n + 1)
                last_done(act, hlo_done, n, 2)
                last_done(act, pf_done, n)
                for k in range(HK):
                    nc.scalar.activation(hT[:, k, :], xT_ps[0][:, k * P:(k + 1) * P], ACT.Identity,
                                         scale=gs1[:, k, kind:kind + 1], bias=mods[:, k, kind:kind + 1]).then_inc(hTa, 1)
                for b in two:
                    act.wait_ge((hTa, hTv)[b], HK * (n + 1))
                    nc.scalar.copy(h_hi[:, b * HK:(b + 1) * HK, :], hT[:, b * HK:(b + 1) * HK, :]).then_inc(hhi_done, 1)

            squares(0)
            act.wait_ge(cT_done, 1)
            nc.scalar.copy(ckvT[:, 0:PAST], sT_ps[:]).then_inc(cT_read, 1)
            for i, (k, w, hi, _) in enumerate(pieces):
                if i == EARLY:
                    modulate(0)
                act.wait_ge(w_loaded[i % WR], 16 * (i // WR + 1))
                nc.scalar.copy(hi[:, k, :], raw[i % WR][:, 0:w]).then_inc(whi_done, 1)

            def step(n):
                if active(n, 2, LAST):
                    m = n - 2
                    act.wait_ge(q_done, 2 * m + 1)
                    last_done(act, qT_done, m, 2)
                    nc.scalar.copy(q_sb[:, 0:HH, :], q_ps[0][:, 0:HH * QK]).then_inc(qa_copied, 1)
                if active(n, 1, NT - 1):
                    squares(n)
                if active(n, 1, NT):
                    m = n - 1
                    act.wait_ge(pa_done, m + 1)
                    last_done(act, norm_done, m, 2)
                    last_done(act, kpe_done, m)
                    nc.scalar.copy(pa[:], pa_ps[:, 0:LATW]).then_inc(pa_copied, 1)
                    act.wait_ge(pa_copied, m + 1)
                    last_done(act, rsp_done, m)
                    last_done(act, ssp_done, m, 2)
                    nc.scalar.activation(junk_p[:, 0:QL], pa[:, 0:QL], ACT.Square, accum_out=ssp[:, 0:1])\
                        .then_inc(ssp_done, 1)
                    nc.scalar.activation(junk_p[:, QL:], pa[:, QL:QL + KVL], ACT.Square, accum_out=ssp[:, 1:2])\
                        .then_inc(ssp_done, 1)
                    act.wait_ge(pf_done, m + 1)
                    nc.scalar.copy(at(F, m), pf_ps[:]).then_inc(f_copied, 1)
                if active(n, 1, NT - 1):
                    modulate(n)
                if active(n, 2, LAST):
                    m = n - 2
                    act.wait_ge(qT_done, 2 * m + 1)
                    last_done(act, q_stored, m, 16)
                    nc.scalar.copy(qT[:, 0:HH, :], qT_ps[0:QK, :]).then_inc(qTa, 1)

            steps(act, step)

        @block.gpsimd
        def _(pool):
            nc.gpsimd.memset(kpe_c[:], 0.0).then_inc(zeroed, 1)
            nc.gpsimd.memset(tm[:], 0.0).then_inc(zeroed, 1)
            pool.wait_ge(zeroed, 2)
            pool = PlainWaits(pool, passed)

            def rms(n):
                pool.wait_ge(ssx_done, n + 1)
                c = Chain(pool, px, 1, n)
                c.link(nc.gpsimd.tensor_scalar(msx[:], ssx[:], 1.0 / D, EPS, ALU.mult, ALU.add))
                last_done(pool, xn_done, n)
                nc.gpsimd.tensor_tensor(rsx[:], msx[:], t["neg_half"][:], ALU.pow).then_inc(rsx_done, 1)

            rms(0)
            pool.wait_ge(rows_loaded, 64)

            def step(n):
                R = ROPE // 2
                if active(n, 1, NT - 1):
                    rms(n)
                if active(n, 2, LAST):
                    m = n - 2
                    pool.wait_ge(qa_copied, m + 1)
                    pool.wait_ge(qv_copied, m + 1)
                    c = Chain(pool, pq, 3, m)
                    wide = lambda v: v.unsqueeze(1).to_broadcast([P, H, v.shape[-1]])
                    csm, snm = at(cs, m), at(sn, m)
                    qp = q_sb[:, :, NOPE:QK]
                    last_done(pool, q_roped, m)
                    c.link(nc.gpsimd.tensor_tensor(qt_[:, 0], qp, wide(csm), ALU.mult))
                    c.link(nc.gpsimd.tensor_tensor(qt_[:, 1, :, 0:R], qp[:, :, R:], wide(snm[:, 0:R]), ALU.mult))
                    c.link(nc.gpsimd.tensor_tensor(qt_[:, 1, :, R:], qp[:, :, 0:R], wide(snm[:, R:]), ALU.mult))
                    nc.gpsimd.tensor_tensor(qp, qt_[:, 0], qt_[:, 1], ALU.add).then_inc(q_roped, 1)
                if active(n, 1, NT):
                    m = n - 1
                    pool.wait_ge(ssp_done, 2 * (m + 1))
                    c = Chain(pool, pp, 4, m)
                    last_done(pool, rsp_done, m)
                    nc.gpsimd.tensor_scalar(msp[:, 0:1], ssp[:, 0:1], 1.0 / QL, EPS, ALU.mult, ALU.add)
                    c.link(nc.gpsimd.tensor_scalar(msp[:, 1:2], ssp[:, 1:2], 1.0 / KVL, EPS, ALU.mult, ALU.add))
                    last_done(pool, norm_done, m, 2)
                    nc.gpsimd.tensor_tensor(rsp[:], msp[:], t["neg_half"][:].to_broadcast([P, 2]), ALU.pow)\
                        .then_inc(rsp_done, 1)
                    kp = pa[:, QL + KVL:LATW]
                    csm, snm = at(cs, m), at(sn, m)
                    last_done(pool, kpe_done, m)
                    c.link(nc.gpsimd.tensor_tensor(rt[:, 0, :], kp, csm, ALU.mult))
                    c.link(nc.gpsimd.tensor_tensor(rt[:, 1, 0:R], kp[:, R:], snm[:, 0:R], ALU.mult))
                    c.link(nc.gpsimd.tensor_tensor(rt[:, 1, R:], kp[:, 0:R], snm[:, R:], ALU.mult))
                    last_done(pool, sT_done, m)
                    last_done(pool, st_stored, m, 32)
                    nc.gpsimd.tensor_tensor(tm[:, KPE0:KPE0 + ROPE], rt[:, 0, :], rt[:, 1, :], ALU.add)\
                        .then_inc(kpe_done, 1)

            steps(pool, step)

        @block.vector
        def _(dve):
            def scale(n):
                dve.wait_ge(rsx_done, n + 1)
                last_done(dve, xT_done, n, 2)
                nc.vector.tensor_scalar(xn[:], xt[:], rsx[:], None, ALU.mult).then_inc(xn_done, 1)

            def modulate(n):
                kind = 0 if is_int(n) and n < CT else 1
                dve.wait_ge(xT_done, 2 * n + 2)
                last_done(dve, hlo_done, n, 2)
                last_done(dve, pf_done, n)
                for k in range(HK, DK):
                    nc.vector.tensor_scalar(hT[:, k, :], xT_ps[1][:, (k - HK) * P:(k - HK + 1) * P],
                                            gs1[:, k, kind:kind + 1], mods[:, k, kind:kind + 1],
                                            ALU.mult, ALU.add).then_inc(hTv, 1)
                for b in two:
                    half = slice(b * HK, (b + 1) * HK)
                    dve.wait_ge(hhi_done, 2 * n + b + 1)
                    split_lo(nc.vector, h_lo[:, half, :], hT[:, half, :], h_hi[:, half, :]).then_inc(hlo_done, 1)

            scale(0)
            dve.wait_ge(cT_done, 2)
            nc.vector.tensor_copy(kpeT[NOPE:QK, 0:PAST], qT_ps[NOPE:QK, :]).then_inc(cT_read, 1)
            for i, (k, w, hi, lo) in enumerate(pieces):
                if i == EARLY:
                    modulate(0)
                dve.wait_ge(whi_done, i + 1)
                split_lo(nc.vector, lo[:, k, :], raw[i % WR][:, 0:w], hi[:, k, :]).then_inc(wlo_done, 1)
            dve.wait_ge(rows_loaded, 64)

            def step(n):
                if active(n, 2, LAST):
                    m = n - 2
                    dve.wait_ge(q_done, 2 * m + 2)
                    last_done(dve, qT_done, m, 2)
                    nc.vector.tensor_copy(q_sb[:, HH:, :], q_ps[1][:, 0:HH * QK]).then_inc(qv_copied, 1)
                if active(n, 1, NT - 1):
                    scale(n)
                if active(n, 1, NT):
                    m = n - 1
                    dve.wait_ge(rsp_done, m + 1)
                    last_done(dve, sT_done, m)
                    last_done(dve, st_stored, m, 32)
                    nc.vector.scalar_tensor_tensor(tm[:, 0:QL], pa[:, 0:QL], rsp[:, 0:1], qg[:],
                                                   ALU.mult, ALU.mult).then_inc(norm_done, 1)
                    nc.vector.scalar_tensor_tensor(tm[:, QL:QL + KVL], pa[:, QL:QL + KVL], rsp[:, 1:2],
                                                   kvg[:], ALU.mult, ALU.mult).then_inc(norm_done, 1)
                    dve.wait_ge(sT_done, m + 1)
                    col = key_col(m)
                    last_done(dve, q_done, m, 2)
                    split_hi(nc.vector, qn_hi[:], sT_ps[:, 0:QL]).then_inc(qn_rounded, 1)
                    nc.vector.tensor_copy(ckvT[:, bass.ds(col, P)], sT_ps[:, QL:QL + P])
                    nc.vector.tensor_copy(kpeT[NOPE:QK, bass.ds(col, P)], sT_ps[NOPE:QK, QL + P:QL + 2 * P])
                    dve.wait_ge(qn_rounded, m + 1)
                    split_lo(nc.vector, qn_lo[:], sT_ps[:, 0:QL], qn_hi[:].rearrange("p k n -> p (k n)"))\
                        .then_inc(sT_read, 1)
                if active(n, 1, NT - 1):
                    modulate(n)
                if active(n, 2, LAST):
                    m = n - 2
                    dve.wait_ge(qT_done, 2 * m + 2)
                    last_done(dve, q_stored, m, 16)
                    nc.vector.tensor_copy(qT[:, HH:, :], pf_ps[0:QK, :]).then_inc(qTv, 1)

            steps(dve, step)

        @block.tensor
        def _(pe):
            def transpose_x(n):
                pe.wait_ge(xn_done, n + 1)
                for b in two:
                    last_done(pe, (hTa, hTv)[b], n, HK)
                    for k in range(HK):
                        c0 = (b * HK + k) * P
                        last = nc.tensor.transpose(xT_ps[b][:, k * P:(k + 1) * P], xn[:, c0:c0 + P], ident[:])
                    last.then_inc(xT_done, 1)

            def three(dst, k, st_hi, st_lo, mv_hi, mv_lo, cols, n):
                nc.tensor.matmul(dst, st_hi[:, k, :], mv_hi[:, k, cols], start=(k == 0), stop=False)
                nc.tensor.matmul(dst, st_hi[:, k, :], mv_lo[:, k, cols], start=False, stop=False)
                return nc.tensor.matmul(dst, st_lo[:, k, :], mv_hi[:, k, cols], start=False, stop=(k == n - 1))

            pe.wait_ge(cache_loaded, 32)
            for n in range(KC):
                last = nc.tensor.transpose(sT_ps[:, n * P:(n + 1) * P], ckv_c[:, n, :], ident[:])
            last.then_inc(cT_done, 1)
            for n in range(KC):
                last = nc.tensor.transpose(qT_ps[:, n * P:(n + 1) * P], kpe_c[:, n, :], ident[:])
            last.then_inc(cT_done, 1)
            pe.wait_ge(cT_read, 2)

            def step(n):
                if active(n, 1, NT):
                    m = n - 1
                    last_done(pe, pa_copied, m)
                    for k in range(DK):
                        if is_int(m) and m == 0:
                            pe.wait_ge(wlo_done, k + 1)
                        pe.wait_ge(hlo_done, 2 * m + k // HK + 1)
                        last = three(pa_ps[:, 0:LATW], k, h_hi, h_lo, w_hi, w_lo, slice(0, LATW), DK)
                    last.then_inc(pa_done, 1)
                    if not is_int(m) or m >= 2:
                        pe.wait_ge(qTv, m - 1)
                    last_done(pe, f_copied, m)
                    for k in range(DK):
                        last = three(pf_ps[:], k, h_hi, h_lo, w_hi, w_lo, slice(LATW, IN_W), DK)
                    last.then_inc(pf_done, 1)
                    pe.wait_ge(norm_done, 2 * (m + 1))
                    pe.wait_ge(kpe_done, m + 1)
                    last_done(pe, sT_read, m)
                    for k in range(4):
                        last = nc.tensor.transpose(sT_ps[:, k * P:(k + 1) * P], tm[:, k * P:(k + 1) * P], ident[:])
                    last.then_inc(sT_done, 1)
                if active(n, 0, NT - 1):
                    transpose_x(n)
                if active(n, 2, LAST):
                    m = n - 2
                    pe.wait_ge(q_roped, m + 1)
                    last_done(pe, qTa, m)
                    pe.wait_ge(f_copied, min(n, NT) if is_int(n) else n)
                    for h in range(H):
                        dst = (qT_ps, pf_ps)[h // HH][0:QK, (h % HH) * P:(h % HH + 1) * P]
                        last = nc.tensor.transpose(dst, q_sb[:, h, :], ident[:])
                        if h % HH == HH - 1:
                            last.then_inc(qT_done, 1)
                if active(n, 1, NT):
                    m = n - 1
                    pe.wait_ge(sT_read, m + 1)
                    if is_int(m) and m == 0:
                        pe.wait_ge(wlo_done, DK + KQ)
                    for h in two:
                        last_done(pe, (qa_copied, qv_copied)[h], m)
                        for k in range(KQ):
                            last = three(q_ps[h][:, 0:HH * QK], k, qn_hi, qn_lo, uq_hi, uq_lo,
                                         slice(h * HH * QK, (h + 1) * HH * QK), KQ)
                        last.then_inc(q_done, 1)

            steps(pe, step)


def fourier(nc, a, t):
    with ExitStack() as x:
        sb = lambda name, shape, dt=F32: x.enter_context(nc.sbuf_tensor(name, shape, dt))
        sem = lambda name: t["sems"].append(x.enter_context(nc.semaphore(name))) or t["sems"][-1]
        two = range(2)
        FT, HT, QT = FW // P, LT // 2, LT // 4
        NO, N0, N2 = LAT // 4, LAT // 8 + 1, LAT // 8
        tab = {
            "odd": [sb(f"tab_odd{q}", [P, HT, NO]) for q in two],
            "r0": [sb(f"tab_r0{q}", [P, QT, N0]) for q in two],
            "r2": [sb(f"tab_r2{q}", [P, QT, N2]) for q in two],
        }
        G = sb("half_sums", [P, HT, FW])
        chan = sb("chan", [P, 2, 2, P])
        wblk = sb("w_fmix_blocks", [P, FT, P])
        M = sb("chan_mix", [P, 2, 2, FT, P])
        PQ = [[sb(f"{'PQ'[q]}{s}", [P, 512]) for s in two] for q in two]
        R2 = [sb(f"R2_{s}", [P, 512]) for s in two]
        pq_ps = [[x.enter_context(nc.psum_tensor(f"fps_{'PQ'[q]}{s}", [P, 512], F32)) for s in two] for q in two]
        r_ps = [[x.enter_context(nc.psum_tensor(f"fps_R{q}{s}", [P, 512], F32)) for s in two] for q in two]
        r0_loaded, odd_loaded, r2_loaded = sem("f_r0_loaded"), sem("f_odd_loaded"), sem("f_r2_loaded")
        chan_loaded, zeroed = sem("f_chan_loaded"), sem("f_zeroed")
        M_done, M_copied = sem("f_M_done"), sem("f_M_copied")
        g_done, d_done, u_done = sem("f_half_sums"), sem("f_half_diffs"), sem("f_quarters")
        pq_done = [sem(f"f_{'PQ'[q]}_done") for q in two]
        pq_copied = [sem(f"f_{'PQ'[q]}_copied") for q in two]
        r_done, r2_copied, mixed = sem("f_R_done"), sem("f_R2_copied"), sem("f_mixed")
        F, out = t["F"], t["fmixT"]
        lat = lambda lo, hi, step: out[:, :, CTX + lo:CTX + hi:step]
        jobs = []
        for c in range(FT):
            jobs.append(("ctx", [F[:, i, c * P:(c + 1) * P] for i in range(CT)], CTX // 2 + 1,
                         out[:, c, 0:CTX // 2 + 1], out[:, c, CTX - 1:CTX // 2:-1], (1, CTX // 2), None))
        T = LAT
        lo = lambda c, k0, step: out[:, c, CTX + k0:CTX + T // 2 + 1:step]
        hi = lambda c, k0, step: out[:, c, CTX + T - k0:CTX + T // 2:-step]
        for c in range(FT):
            cc = slice(c * P, (c + 1) * P)
            jobs.append(("odd", [F[:, CT + HT + i, cc] for i in range(HT)], NO, lo(c, 1, 2), hi(c, 1, 2), (0, NO), "d"))
        for c in range(FT):
            cc = slice(c * P, (c + 1) * P)
            jobs.append(("r0", [F[:, CT + i, cc] for i in range(QT)], N0, lo(c, 0, 4), hi(c, 4, 4), (1, N0 - 1), "u"))
        for c in range(FT):
            cc = slice(c * P, (c + 1) * P)
            jobs.append(("r2", [F[:, CT + QT + i, cc] for i in range(QT)], N2, lo(c, 2, 4), hi(c, 2, 4), (0, N2), "u"))
        NJ = len(jobs)
        block = x.enter_context(nc.Block())

        @block.sync
        def _(sp):
            sp.dma_start(chan[:], a["k_chan"]).then_inc(chan_loaded, 16)
            for name, s in (("r0", r0_loaded), ("odd", odd_loaded), ("r2", r2_loaded)):
                for q, f in enumerate(("cos", "sin")):
                    sp.dma_start(tab[name][q][:], a[f"k_{f}_{name}"].rearrange("(k p) f -> p k f", p=P)).then_inc(s, 16)

        @block.gpsimd
        def _(pool):
            nc.gpsimd.memset(wblk[:], 0.0).then_inc(zeroed, 1)
            for i in range(HT):
                pool.wait_ge(g_done, i + 1)
                nc.gpsimd.tensor_tensor(F[:, CT + HT + i, :], F[:, CT + i, :], F[:, CT + HT + i, :], ALU.subtract)\
                    .then_inc(d_done, 1)

        @block.vector
        def _(dve):
            for i in range(HT):
                nc.vector.tensor_tensor(G[:, i, :], F[:, CT + i, :], F[:, CT + HT + i, :], ALU.add).then_inc(g_done, 1)
            dve.wait_ge(M_done, 1)
            for q in two:
                nc.vector.tensor_copy(M[:, 1, q], r_ps[q][1][:].rearrange("p (c d) -> p c d", c=FT)).then_inc(M_copied, 1)
            dve.wait_ge(d_done, HT)
            dve.wait_ge(g_done, HT)
            for i in range(QT):
                nc.vector.tensor_tensor(F[:, CT + i, :], G[:, i, :], G[:, QT + i, :], ALU.add).then_inc(u_done, 1)
            for i in range(QT):
                nc.vector.tensor_tensor(F[:, CT + QT + i, :], G[:, i, :], G[:, QT + i, :], ALU.subtract).then_inc(u_done, 1)

            def copy_q(i):
                s, n = i % 2, jobs[i][2]
                dve.wait_ge(pq_done[1], i + 1)
                if i >= 2:
                    dve.wait_ge(r_done, i - 1)
                nc.vector.tensor_copy(PQ[1][s][:, 0:n], pq_ps[1][s][:, 0:n]).then_inc(pq_copied[1], 1)

            def combine(i):
                s, (_, _, n, direct, mirror, (m0, m1), _) = i % 2, jobs[i]
                dve.wait_ge(r_done, i + 1)
                dve.wait_ge(r2_copied, i + 1)
                nc.vector.tensor_tensor(direct, r_ps[0][s][:, 0:n], R2[s][:, 0:n], ALU.subtract)
                nc.vector.tensor_tensor(mirror, r_ps[0][s][:, m0:m1], R2[s][:, m0:m1], ALU.add).then_inc(mixed, 1)

            for i in range(NJ + 1):
                if i < NJ:
                    copy_q(i)
                if i >= 1:
                    combine(i - 1)

        @block.scalar
        def _(act):
            act.wait_ge(zeroed, 1)
            for b in two:
                src = a["w_fmix"][0].rearrange("(c b) i d -> b i c d", b=2)[b]
                act.dma_start(wblk[b * 64:(b + 1) * 64, :, b * 64:(b + 1) * 64], src).then_inc(chan_loaded, 16)
            act.wait_ge(M_done, 1)
            for q in two:
                nc.scalar.copy(M[:, 0, q], r_ps[q][0][:].rearrange("p (c d) -> p c d", c=FT)).then_inc(M_copied, 1)
            for i in range(NJ + 1):
                if i < NJ:
                    s, n = i % 2, jobs[i][2]
                    act.wait_ge(pq_done[0], i + 1)
                    if i >= 2:
                        act.wait_ge(r_done, i - 1)
                    nc.scalar.copy(PQ[0][s][:, 0:n], pq_ps[0][s][:, 0:n]).then_inc(pq_copied[0], 1)
                if i >= 1:
                    s, n = (i - 1) % 2, jobs[i - 1][2]
                    act.wait_ge(r_done, i)
                    if i >= 3:
                        act.wait_ge(mixed, i - 2)
                    nc.scalar.copy(R2[s][:, 0:n], r_ps[1][s][:, 0:n]).then_inc(r2_copied, 1)

        @block.tensor
        def _(pe):
            pe.wait_ge(chan_loaded, 48)
            for kind in two:
                for q in two:
                    for c in range(FT):
                        last = nc.tensor.matmul(r_ps[q][kind][:, c * P:(c + 1) * P], chan[:, kind, q, :], wblk[:, c, :],
                                                start=True, stop=True)
            last.then_inc(M_done, 1)

            def mix(i):
                s, kind, n, c = i % 2, 0 if i < FT else 1, jobs[i][2], i % FT
                if i == 0:
                    pe.wait_ge(M_copied, 4)
                if i >= 2:
                    pe.wait_ge(mixed, i - 1)
                for q in two:
                    pe.wait_ge(pq_copied[q], i + 1)
                    last = nc.tensor.matmul(r_ps[q][s][:, 0:n], M[:, kind, q, c, :], PQ[q][s][:, 0:n],
                                            start=True, stop=True)
                last.then_inc(r_done, 1)

            for i, (name, src, n, _, _, _, need) in enumerate(jobs):
                s = i % 2
                if i == 0:
                    pe.wait_ge(r0_loaded, 32)
                if name == "odd":
                    pe.wait_ge(odd_loaded, 32)
                if name == "r2":
                    pe.wait_ge(r2_loaded, 32)
                for q in two:
                    if i >= 2:
                        pe.wait_ge(pq_copied[q], i - 1)
                for k in range(len(src)):
                    if need == "d":
                        pe.wait_ge(d_done, k + 1)
                    if need == "u":
                        pe.wait_ge(u_done, k + 1 + (QT if name == "r2" else 0))
                    for q in two:
                        rhs = tab["r0"][q][:, k, 0:2 * n - 1:2] if name == "ctx" else tab[name][q][:, k, :]
                        last = nc.tensor.matmul(pq_ps[q][s][:, 0:n], src[k], rhs, start=(k == 0),
                                                stop=(k == len(src) - 1))
                        if k == len(src) - 1:
                            last.then_inc(pq_done[q], 1)
                if i >= 1:
                    mix(i - 1)
            mix(NJ - 1)


def context_attention(nc, a, t):
    with ExitStack() as x:
        sb = lambda name, shape, dt=F32: x.enter_context(nc.sbuf_tensor(name, shape, dt))
        sem = lambda name: t["sems"].append(x.enter_context(nc.semaphore(name))) or t["sems"][-1]
        HP, K0 = H // 2, PAST + LAT
        wt = sb("c_w_ukv", [P, H, NOPE + VH])
        kc, qc = sb("c_kT", [QK + 1, H, CTX]), sb("c_qT", [QK + 1, H, CTX])
        Vc = sb("c_values", [P, CT, H, VH + 1])
        nm, prob = sb("c_neg_max", [P, H, CT]), sb("c_probT", [P, H, CT, CTX])
        OTs, rinv = sb("c_outT", [VH + 1, H, CTX]), sb("c_row_inv", [P, 2, CT])
        bank = [x.enter_context(nc.psum_tensor(f"c_ps{b}", [P, 512], F32)) for b in range(8)]
        loaded, ropes, filled = sem("c_loaded"), sem("c_rope_rows"), sem("c_constants")
        k_done, k_copied, v_done, v_copied = sem("c_k_done"), sem("c_k_copied"), sem("c_v_done"), sem("c_v_copied")
        a_done, max_done, row_done, row_copied = sem("c_a"), sem("c_max"), sem("c_row"), sem("c_row_copied")
        s_done, exp_done, pv_done, o_copied = sem("c_s"), sem("c_exp"), sem("c_pv"), sem("c_o_copied")
        ot_done, inv_done, o_done = sem("c_ot"), sem("c_inv"), sem("c_o")
        block = x.enter_context(nc.Block())

        @block.sync
        def _(sp):
            sp.dma_start(wt[:], a["w_ukv"][0].rearrange("c (h d) -> c h d", h=H)).then_inc(loaded, 16)
            for i in range(CT):
                src = a["s_q"][i].rearrange("p h q -> p h q")
                sp.dma_start(qc[0:QK, :, i * P:(i + 1) * P], src).then_inc(loaded, 16)

        @block.tensor
        def _(pe):
            pe.wait_ge(loaded, 16 * (1 + CT))
            for h in range(H):
                last = nc.tensor.matmul(bank[h // 2][0:NOPE, (h % 2) * CTX:(h % 2 + 1) * CTX], wt[:, h, 0:NOPE],
                                        t["ckvT"][:, K0:K0 + CTX], start=True, stop=True)
                if h % 2:
                    last.then_inc(k_done, 1)
            for n in range(CT):
                nc.tensor.matmul(bank[HP + n][:, 0:H * VH], t["ckvT"][:, K0 + n * P:K0 + (n + 1) * P],
                                 wt[:, :, NOPE:], start=True, stop=True).then_inc(v_done, 1)
            pe.wait_ge(ropes, 1)
            for h in range(H):
                pe.wait_ge(k_copied, h // 2 + 1)
                if h >= 2:
                    pe.wait_ge(max_done, h - 1)
                for i in range(CT):
                    last = nc.tensor.matmul(bank[6 + h % 2][:, i * CTX:(i + 1) * CTX], qc[0:QK, h, i * P:(i + 1) * P],
                                            kc[0:QK, h, :], start=True, stop=True)
                last.then_inc(a_done, 1)
            for g in range(HP):
                pe.wait_ge(max_done, 2 * g + 2)
                pe.wait_ge(k_copied, g + 1)
                for q in range(2 * CT):
                    last = nc.tensor.matmul(bank[g][0:1, q * P:(q + 1) * P], nm[:, 2 * g + q // CT, q % CT:q % CT + 1],
                                            t["ident"][:], start=True, stop=True)
                last.then_inc(row_done, 1)
            for h in range(H):
                b = bank[4 + h % 2]
                pe.wait_ge(row_copied, h // 2 + 1)
                pe.wait_ge(v_copied, CT)
                pe.wait_ge(filled, 3)
                if h >= 2:
                    pe.wait_ge(exp_done, h - 1)
                for n in range(CT):
                    last = nc.tensor.matmul(b[:, n * CTX:(n + 1) * CTX], kc[:, h, n * P:(n + 1) * P], qc[:, h, :],
                                            start=True, stop=True)
                last.then_inc(s_done, 1)
            for h in range(H):
                pe.wait_ge(exp_done, h + 1)
                pe.wait_ge(row_copied, h // 2 + 1)
                for n in range(CT):
                    last = nc.tensor.matmul(bank[h // 2][0:VH + 1, (h % 2) * CTX:(h % 2 + 1) * CTX], Vc[:, n, h, :],
                                            prob[:, h, n, :], start=(n == 0), stop=(n == CT - 1))
                if h % 2:
                    last.then_inc(pv_done, 1)
            for g in range(HP):
                pe.wait_ge(o_copied, g + 1)
                if g >= 2:
                    pe.wait_ge(o_done, g - 1)
                for q in range(2 * CT):
                    h, i = 2 * g + q // CT, q % CT
                    last = nc.tensor.transpose(bank[6 + g % 2][:, q * (VH + 1):(q + 1) * (VH + 1)],
                                               OTs[:, h, i * P:(i + 1) * P], t["ident"][0:VH + 1, 0:VH + 1])
                last.then_inc(ot_done, 1)

        @block.scalar
        def _(act):
            for g in range(HP):
                act.wait_ge(k_done, g + 1)
                nc.scalar.copy(kc[0:NOPE, 2 * g:2 * g + 2, :], bank[g][0:NOPE, :]).then_inc(k_copied, 1)
            for g in range(HP):
                act.wait_ge(row_done, g + 1)
                nc.scalar.copy(qc[QK:QK + 1, 2 * g:2 * g + 2, :], bank[g][0:1, :]).then_inc(row_copied, 1)
            for h in range(H):
                act.wait_ge(s_done, h + 1)
                nc.scalar.activation(prob[:, h, :, :], bank[4 + h % 2][:], ACT.Exp, scale=SCALE).then_inc(exp_done, 1)
            for g in range(HP):
                act.wait_ge(pv_done, g + 1)
                nc.scalar.copy(OTs[:, 2 * g:2 * g + 2, :], bank[g][0:VH + 1, :]).then_inc(o_copied, 1)

        @block.vector
        def _(dve):
            rope = t["kpeT"][NOPE:QK, K0:K0 + CTX].unsqueeze(1).broadcast_to([ROPE, H, CTX])
            nc.vector.tensor_copy(kc[NOPE:QK, :, :], rope).then_inc(ropes, 1)
            nc.vector.memset(kc[QK:QK + 1, :, :], 1.0).then_inc(filled, 1)
            for n in range(CT):
                nc.vector.memset(Vc[:, n, :, VH:VH + 1], 1.0).then_inc(filled, 1)
            for n in range(CT):
                dve.wait_ge(v_done, n + 1)
                nc.vector.tensor_copy(Vc[:, n, :, 0:VH], bank[HP + n][:, 0:H * VH].rearrange("p (h d) -> p h d", h=H))\
                    .then_inc(v_copied, 1)
            for h in range(H):
                dve.wait_ge(a_done, h + 1)
                nc.vector.tensor_reduce(nm[:, h, :], bank[6 + h % 2][:].rearrange("p (t k) -> p t k", t=CT), AX.X,
                                        ALU.max, negate=True).then_inc(max_done, 1)
            for g in range(HP):
                dve.wait_ge(ot_done, g + 1)
                if g >= 1:
                    dve.wait_ge(o_done, g)
                OT = bank[6 + g % 2][:, 0:2 * CT * (VH + 1)].rearrange("p (h t d) -> p h t d", h=2, t=CT)
                nc.vector.reciprocal(rinv[:], OT[:, :, :, VH]).then_inc(inv_done, 1)
                dve.wait_ge(inv_done, g + 1)
                dst = t["O"][:, 0:CT, 2 * g * VH:2 * (g + 1) * VH].rearrange("p t (h d) -> p h t d", h=2)
                nc.vector.tensor_tensor(dst, OT[:, :, :, 0:VH],
                                        rinv[:].unsqueeze(3).broadcast_to([P, 2, CT, VH]), ALU.mult)\
                    .then_inc(o_done, 1)


def attention(nc, a, t):
    with ExitStack() as x:
        sb = lambda name, shape, dt=F32: x.enter_context(nc.sbuf_tensor(name, shape, dt))
        sem = lambda name: t["sems"].append(x.enter_context(nc.semaphore(name))) or t["sems"][-1]
        two = range(2)
        CH = 512
        KL = PAST + LAT
        NS, TG = KL // P, CH // P
        NC = KL // CH
        assert NS == TG * NC
        GH = LAT // CH
        G, S = 2 * GH, 2 * GH * NS
        AHEAD = 4
        RING, LAG, QRING = 4, 2, 4
        UV = 4
        UNITS = NC + NS // UV
        UNIT_STEP = {4 + 3 * u: u for u in range(UNITS)}
        assert max(UNIT_STEP) < (GH - 1) * NS - AHEAD and S % RING == 0
        NEG_ROW, COPY_ROW = NS - AHEAD + 1, NS - AHEAD + 2
        QSPLIT, T_STEP, O_STEP = 10, 5, 6
        w_h = sb("w_ukv_head", [P, NOPE + VH])
        khi = [sb(f"k_hi{s}", [QK + 1, KL], F32R) for s in two]
        klo = [sb(f"k_lo{s}", [QK, KL], F32R) for s in two]
        vhi = [sb(f"v_hi{s}", [P, NS, VH + 1], F32R) for s in two]
        vlo = [sb(f"v_lo{s}", [P, NS, VH + 1], F32R) for s in two]
        q_raw = sb("q_group", [QK, TG, P])
        qhi = [sb(f"q_hi{s}", [QK + 1, CH], F32R) for s in range(QRING)]
        qlo = [sb(f"q_lo{s}", [QK, CH], F32R) for s in range(QRING)]
        prob = [sb(f"probT{r}", [P, CH]) for r in range(RING)]
        phi = [sb(f"probT_hi{r}", [P, CH], F32R) for r in range(RING)]
        plo = [sb(f"probT_lo{r}", [P, CH], F32R) for r in range(RING)]
        mx, nm = sb("chunk_max", [P, TG, NC]), sb("neg_max", [P, TG])
        OTs, rinv = sb("outT", [VH + 1, CH]), sb("row_inv", [P, TG])
        wm = sb("w_mod_tile", [P, DK, P])
        ones, zeros = sb("a_ones", [P, NS]), sb("a_zeros", [P, NS])
        S_ps = [x.enter_context(nc.psum_tensor(f"S_ps{b}", [P, CH], F32)) for b in two]
        A_ps = [x.enter_context(nc.psum_tensor(f"A_ps{b}", [P, CH], F32)) for b in two]
        O_ps = x.enter_context(nc.psum_tensor("O_ps", [P, CH], F32))
        row_ps = x.enter_context(nc.psum_tensor("row_ps", [P, CH], F32))
        kv_ps = x.enter_context(nc.psum_tensor("kv_ps", [P, CH], F32))
        OT_ps = x.enter_context(nc.psum_tensor("OT_ps", [P, CH], F32))
        w_loaded, q_loaded, constants = sem("a_w_loaded"), sem("a_q_loaded"), sem("a_constants")
        unit_done, unit_hi, unit_split = sem("a_unit_done"), sem("a_unit_hi"), sem("a_unit_split")
        a_done, max_done, nm_done = sem("a_chunk"), sem("a_chunk_max"), sem("a_neg_max")
        row_done, row_copied = sem("a_row_done"), sem("a_row_copied")
        q_hi_done, q_split = sem("a_q_hi"), sem("a_q_split")
        s_done, exp_done, p_hi_done, p_lo_done = sem("a_scores"), sem("a_exp"), sem("a_p_hi"), sem("a_p_lo")
        pv_done, o_copied, ot_done = sem("a_pv"), sem("a_o_copied"), sem("a_ot")
        inv_done, o_done, passed = sem("a_inv"), sem("a_o"), sem("a_pool_passed")
        sp_passed = sem("a_sync_passed")
        mod_loaded, mod_done, mod_added = sem("a_mod_loaded"), sem("a_mod_done"), sem("a_mod_added")
        M0 = 2 * DK
        MOD_STEP, MOD_COL = 12, CH - 2
        assert H * GH == 6 * DK - M0 and MOD_COL >= TG * (VH + 1)
        PRIMED = RING
        A0 = NS + AHEAD
        block = x.enter_context(nc.Block())

        def done(j, s, per):
            return j * per + (PRIMED + s + 1)

        def group_done(j, g):
            return j * G + (g + 2)

        def chunk(s):
            return s // NS, s % NS // NC, s % NC

        def head_buffer(g):
            return g // GH % 2

        def pe_unit(pe, u, par, heads):
            if u == 0:
                pe.wait_ge(w_loaded, heads * 16 + 16)
            pe.wait_ge(unit_split, heads * UNITS + u + 1)
            if u < NC:
                nc.tensor.matmul(kv_ps[0:NOPE, :], w_h[:, 0:NOPE], t["ckvT"][:, u * CH:(u + 1) * CH],
                                 start=True, stop=True).then_inc(unit_done, 1)
            else:
                for i in range(UV):
                    n = (u - NC) * UV + i
                    last = nc.tensor.matmul(kv_ps[:, i * VH:(i + 1) * VH], t["ckvT"][:, n * P:(n + 1) * P],
                                            w_h[:, NOPE:], start=True, stop=True)
                last.then_inc(unit_done, 1)

        def dve_unit(dve, u, par, heads):
            dve.wait_ge(unit_done, heads * UNITS + u + 1)
            if u < NC:
                ps, cols = kv_ps[0:NOPE, :], slice(u * CH, (u + 1) * CH)
                hi, lo = khi[par][0:NOPE, cols], klo[par][0:NOPE, cols]
            else:
                tiles = slice((u - NC) * UV, (u - NC + 1) * UV)
                ps = kv_ps[:, 0:UV * VH].rearrange("p (n d) -> p n d", n=UV)
                hi, lo = vhi[par][:, tiles, 0:VH], vlo[par][:, tiles, 0:VH]
            split_hi(nc.vector, hi, ps).then_inc(unit_hi, 1)
            dve.wait_ge(unit_hi, heads * UNITS + u + 1)
            split_lo(nc.vector, lo, ps, hi).then_inc(unit_split, 1)

        def pe_chunk(pe, j, s):
            g, i, c = chunk(s)
            par = head_buffer(g)
            pe.wait_ge(max_done, done(j, s - 2, S))
            if c == 0:
                pe.wait_ge(q_split, j * G + (g + 1))
            if g % GH == 0 and i == 0:
                pe.wait_ge(unit_split, 1 + (j * 2 + g // GH) * UNITS + c + 1)
            nc.tensor.matmul(A_ps[s % 2][:], qhi[g % QRING][0:QK, i * P:(i + 1) * P], khi[par][0:QK, c * CH:(c + 1) * CH],
                             start=True, stop=True).then_inc(a_done, 1)

        def dve_chunk(dve, j, s):
            g, i, c = chunk(s)
            dve.wait_ge(a_done, j * S + s + 1)
            if i == 0 and c == 0 and g > 0:
                dve.wait_ge(nm_done, j * G + g)
            nc.vector.reduce_max(mx[:, i, c:c + 1], A_ps[s % 2][:], AX.X).then_inc(max_done, 1)
            if i == TG - 1 and c == NC - 1:
                dve.wait_ge(max_done, done(j, s, S))
                dve.wait_ge(row_done, group_done(j, g - 1))
                nc.vector.tensor_reduce(nm[:], mx[:], AX.X, ALU.max, negate=True).then_inc(nm_done, 1)

        def pe_row(pe, j, g):
            pe.wait_ge(nm_done, j * G + g + 1)
            pe.wait_ge(row_copied, group_done(j, g - 1))
            for i in range(TG):
                last = nc.tensor.matmul(row_ps[0:1, i * P:(i + 1) * P], nm[:, i:i + 1], t["ident"][:],
                                        start=True, stop=True)
            last.then_inc(row_done, 1)

        def act_row(act, j, g):
            act.wait_ge(row_done, group_done(j, g))
            nc.scalar.copy(qhi[g % QRING][QK:QK + 1, :], row_ps[0:1, :]).then_inc(row_copied, 1)

        def dve_q(dve, j, g):
            dve.wait_ge(q_loaded, (j * G + (g + 1)) * 16)
            raw = q_raw[:].rearrange("p t q -> p (t q)")
            split_hi(nc.vector, qhi[g % QRING][0:QK, :], raw).then_inc(q_hi_done, 1)
            dve.wait_ge(q_hi_done, j * G + g + 1)
            split_lo(nc.vector, qlo[g % QRING][:], raw, qhi[g % QRING][0:QK, :]).then_inc(q_split, 1)

        @block.sync
        def _(sync):
            sp = PlainWaits(sync, sp_passed)

            def load_w(h):
                sync.dma_start(w_h[:], a["w_ukv"][0][:, bass.ds(h * (NOPE + VH), NOPE + VH)]).then_inc(w_loaded, 16)

            def load_q(j, g, h):
                if g > 0:
                    sp.wait_ge(q_split, j * G + g)
                n = CT + (g % GH) * TG
                src = a["s_q"][n:n + TG, :, bass.ds(h, 1), :].rearrange("n p h q -> p (n h) q")
                sync.dma_start(q_raw[:], src).then_inc(q_loaded, 16)

            def load_mod(j, g):
                if g > 0 or not is_int(j) or j > 0:
                    sp.wait_ge(mod_done, j * G + g)
                src = a["w_mod"][0].rearrange("(k p) n -> p k n", p=P)[:, :, bass.ds((j * G + (M0 + g)) * P, P)]
                sync.dma_start(wm[:], src).then_inc(mod_loaded, 16)

            load_w(0)
            load_mod(0, 0)
            for g in two:
                load_q(0, g, 0)

            def pair(j, last=False):
                for hl in two:
                    sp.wait_ge(unit_done, (j * 2 + (hl + 1)) * UNITS)
                    load_w(H - 1 if last and hl == 1 else j * 2 + (hl + 1))
                    for g in range(hl * GH + 2, hl * GH + GH + 2):
                        load_q(j, g, min(2 * j + g // GH, H - 1) if is_int(j) else 2 * j + g // GH)
                        if not (last and g == G + 1):
                            load_mod(j, g - 1)

            with sp.Fori(0, H // 2 - 1) as j:
                pair(j)
            pair(H // 2 - 1, last=True)
            sp.wait_ge(q_loaded, 16 * (G * H // 2 + 2))
            sp.wait_ge(w_loaded, 16 * (H + 1))

        @block.tensor
        def _(pe):
            for ring in (s_done, pv_done):
                pe.sem_inc(ring, PRIMED)
            for once in (row_done, ot_done):
                pe.sem_inc(once, 1)
            for u in range(UNITS):
                pe_unit(pe, u, 0, 0)
            pe.wait_ge(constants, 12)
            for s in range(A0):
                pe_chunk(pe, 0, s)
            pe_row(pe, 0, 0)

            with pe.Fori(0, H // 2) as j:
                def scores(s):
                    g, n = s // NS, s % NS
                    q, par = g % QRING, head_buffer(g)
                    pe.wait_ge(exp_done, done(j, s - 2, S))
                    if n == 0:
                        pe.wait_ge(q_split, j * G + g + 1)
                        pe.wait_ge(row_copied, group_done(j, g))
                    keys = slice(n * P, (n + 1) * P)
                    ps = S_ps[s % 2][:]
                    nc.tensor.matmul(ps, khi[par][:, keys], qhi[q][:], start=True, stop=False)
                    nc.tensor.matmul(ps, khi[par][0:QK, keys], qlo[q][:], start=False, stop=False)
                    nc.tensor.matmul(ps, klo[par][:, keys], qhi[q][0:QK, :],
                                     start=False, stop=True).then_inc(s_done, 1)

                def products(s):
                    g, n = s // NS, s % NS
                    par = head_buffer(g)
                    pe.wait_ge(p_hi_done, done(j, s, S))
                    if n == 0:
                        pe.wait_ge(o_copied, group_done(j, g - 1))
                    if g % GH == 0 and n % UV == 0:
                        pe.wait_ge(unit_split, 1 + (j * 2 + g // GH) * UNITS + NC + n // UV + 1)
                    ps = O_ps[0:VH + 1, :]
                    nc.tensor.matmul(ps, vhi[par][:, n, :], phi[s % RING][:],
                                     start=(n == 0), stop=False)
                    nc.tensor.matmul(ps, vlo[par][:, n, :], phi[s % RING][:],
                                     start=False, stop=False)
                    pe.wait_ge(p_lo_done, done(j, s, S))
                    nc.tensor.matmul(ps, vhi[par][:, n, :], plo[s % RING][:],
                                     start=False, stop=(n == NS - 1)).then_inc(pv_done, 1)

                def out_transposed(g):
                    pe.wait_ge(o_copied, group_done(j, g))
                    pe.wait_ge(mod_added, j * G + g + 1)
                    pe.wait_ge(o_done, group_done(j, g - 1))
                    for i in range(TG):
                        last = nc.tensor.transpose(OT_ps[:, i * (VH + 1):(i + 1) * (VH + 1)],
                                                   OTs[:, i * P:(i + 1) * P], t["ident"][0:VH + 1, 0:VH + 1])
                    last.then_inc(ot_done, 1)

                for s in range(S):
                    g, n = s // NS, s % NS
                    hl, head_step = g // GH, s % (GH * NS)
                    scores(s)
                    pe_chunk(pe, j, s + A0)
                    if head_step in UNIT_STEP:
                        pe_unit(pe, UNIT_STEP[head_step], 1 - hl, j * 2 + (hl + 1))
                    if n == NEG_ROW:
                        pe_row(pe, j, g + 1)
                    if n == MOD_STEP:
                        pe.wait_ge(mod_loaded, (j * G + (g + 1)) * 16)
                        if g == 0:
                            pe.wait_ge(o_done, group_done(j, -1))
                        for k in range(DK):
                            last = nc.tensor.matmul(OT_ps[:, MOD_COL:], wm[:, k, :], t["silu_cols"][:, :, k],
                                                    start=(k == 0), stop=(k == DK - 1))
                        last.then_inc(mod_done, 1)
                    if s >= LAG:
                        products(s - LAG)
                    if n == T_STEP and g >= 1:
                        out_transposed(g - 1)
                for s in range(S - LAG, S):
                    products(s)
                out_transposed(G - 1)

        @block.scalar
        def _(act):
            act.sem_inc(exp_done, PRIMED)
            for once in (row_copied, o_copied):
                act.sem_inc(once, 1)
            act_row(act, 0, 0)
            with act.Fori(0, H // 2) as j:
                def out_copied(g):
                    act.wait_ge(pv_done, done(j, (g + 1) * NS - 1, S))
                    act.wait_ge(ot_done, group_done(j, g - 1))
                    nc.scalar.copy(OTs[:], O_ps[0:VH + 1, :]).then_inc(o_copied, 1)

                for s in range(S):
                    g, n = s // NS, s % NS
                    act.wait_ge(s_done, done(j, s, S))
                    act.wait_ge(p_lo_done, done(j, s - RING, S))
                    nc.scalar.activation(prob[s % RING][:], S_ps[s % 2][:], ACT.Exp, scale=SCALE).then_inc(exp_done, 1)
                    if n == LAG - 1 and g >= 1:
                        out_copied(g - 1)
                    if n == COPY_ROW:
                        act_row(act, j, g + 1)
                out_copied(G - 1)

        @block.vector
        def _(dve):
            for ring in (max_done, p_hi_done):
                dve.sem_inc(ring, PRIMED)
            for once in (unit_split, o_done):
                dve.sem_inc(once, 1)
            rope = t["kpeT"][NOPE:QK, 0:KL]
            nc.vector.memset(ones[:], 1.0).then_inc(constants, 1)
            nc.vector.memset(zeros[:], 0.0).then_inc(constants, 1)
            dve.wait_ge(constants, 2)
            for s in two:
                split_hi(nc.vector, khi[s][NOPE:QK, :], rope).then_inc(constants, 1)
                nc.vector.tensor_copy(khi[s][QK:QK + 1, :], ones[QK:QK + 1, 0:1].broadcast_to([1, KL]))\
                    .then_inc(constants, 1)
                nc.vector.tensor_copy(vhi[s][:, :, VH], ones[:]).then_inc(constants, 1)
                nc.vector.tensor_copy(vlo[s][:, :, VH], zeros[:]).then_inc(constants, 1)
            dve.wait_ge(constants, 10)
            for s in two:
                split_lo(nc.vector, klo[s][NOPE:QK, :], rope, khi[s][NOPE:QK, :]).then_inc(constants, 1)
            for u in range(UNITS):
                dve_unit(dve, u, 0, 0)
            for g in two:
                dve_q(dve, 0, g)
            for s in range(A0):
                dve_chunk(dve, 0, s)

            with dve.Fori(0, H // 2) as j:
                def out_scaled(g):
                    dve.wait_ge(ot_done, group_done(j, g))
                    OT = OT_ps[:, 0:TG * (VH + 1)].rearrange("p (t d) -> p t d", t=TG)
                    nc.vector.reciprocal(rinv[:], OT[:, :, VH]).then_inc(inv_done, 1)
                    dve.wait_ge(inv_done, j * G + g + 1)
                    n = CT + (g % GH) * TG
                    dst = t["O"][:, n:n + TG, bass.ds((j * 2 + g // GH) * VH, VH)]
                    nc.vector.tensor_tensor(dst, OT[:, :, 0:VH], rinv[:].unsqueeze(2).broadcast_to([P, TG, VH]), ALU.mult)\
                        .then_inc(o_done, 1)

                for s in range(S):
                    g, n = s // NS, s % NS
                    hl, head_step = g // GH, s % (GH * NS)
                    dve_chunk(dve, j, s + A0)
                    dve.wait_ge(exp_done, done(j, s, S))
                    dve.wait_ge(pv_done, done(j, s - RING, S))
                    split_hi(nc.vector, phi[s % RING][:], prob[s % RING][:]).then_inc(p_hi_done, 1)
                    if head_step in UNIT_STEP:
                        dve_unit(dve, UNIT_STEP[head_step], 1 - hl, j * 2 + (hl + 1))
                    if n == QSPLIT:
                        dve_q(dve, j, g + 2)
                    if n == O_STEP and g >= 1:
                        out_scaled(g - 1)
                    if n == MOD_STEP + 1:
                        dve.wait_ge(mod_done, j * G + g + 1)
                        dst = t["mods"][:, bass.ds(j * G + (M0 + g), 1), :].rearrange("p o k -> p (o k)")
                        bias = t["vec_cols"][:, bass.ds(j * G + (VEC_BIAS + M0 + g), 1)].to_broadcast([P, 2])
                        nc.vector.tensor_tensor(dst, OT_ps[:, MOD_COL:], bias, ALU.add).then_inc(mod_added, 1)
                out_scaled(G - 1)

        @block.gpsimd
        def _(pool):
            pool.sem_inc(p_lo_done, PRIMED)
            pool = PlainWaits(pool, passed)
            with pool.Fori(0, H // 2) as j:
                for s in range(S):
                    pool.wait_ge(pv_done, done(j, s - RING, S))
                    pool.wait_ge(p_hi_done, done(j, s, S))
                    split_lo(nc.gpsimd, plo[s % RING][:], prob[s % RING][:], phi[s % RING][:]).then_inc(p_lo_done, 1)


def mixing_out(nc, a, t):
    with ExitStack() as x:
        sb = lambda name, shape, dt=F32: x.enter_context(nc.sbuf_tensor(name, shape, dt))
        sem = lambda name: x.enter_context(nc.semaphore(name))
        ps = lambda name: x.enter_context(nc.psum_tensor(name, [P, 512], F32))
        two = range(2)
        FT, HD = FW // P, D // 2
        w_raw = [sb(f"w_out_raw{s}", [P, D]) for s in two]
        w_hi, w_lo = sb("w_out_hi", [P, DK, D], F32R), sb("w_out_lo", [P, DK, D], F32R)
        w_r = sb("w_router_sb", [P, DK, NE])
        gate = sb("gate1_rows", [P, 2, D])
        xt = [t["ckvT"][:, s * D:(s + 1) * D] for s in two]
        x2 = [t["kpeT"][:, s * D:(s + 1) * D] for s in two]
        o_st = sb("o_attn", [P, FW])
        f_hi = [sb(f"o_fmixT_hi{s}", [P, FT, P], F32R) for s in two]
        f_lo = [sb(f"o_fmixT_lo{s}", [P, FT, P], F32R) for s in two]
        aT_hi, aT_lo = sb("o_attnT_hi", [P, FT, P], F32R), sb("o_attnT_lo", [P, FT, P], F32R)
        gate_col, gate_row = sb("gate_cols", [P, 2, 2, DK]), sb("gate_rows", [4 * DK, P])
        junk = t["ckvT"][:, 2 * D:2 * D + D // 2].bitcast(BF16)
        row = [sb(f"row{s}", [P, ROWW]) for s in two]
        hT = sb("h2T", [P, DK, P])
        ex, se = [sb(f"aff_exp{s}", [P, NE]) for s in two], [sb(f"o_se{s}", [P, 1]) for s in two]
        ss, rs = [sb(f"o_ss{s}", [P, 1]) for s in two], [sb(f"o_rs{s}", [P, 1]) for s in two]
        ms, nm, ri = sb("o_ms", [P, 1]), sb("o_nm", [P, 1]), sb("o_ri", [P, 1])
        aT_ps, l_ps = ps("o_aT_ps"), ps("o_logit_ps")
        y_ps = [[ps(f"o_y_ps{s}{h}") for h in two] for s in two]
        xT_ps = [ps(f"o_xT_ps{h}") for h in two]
        rest_loaded, w_loaded = sem("o_rest_loaded"), [sem(f"o_w_loaded{s}") for s in two]
        whi_done, wlo_done = sem("o_w_hi"), sem("o_w_lo")
        x_loaded = [sem(f"o_x_loaded{s}") for s in two]
        gates_ready, gateT_done, gateT_copied = sem("o_gates"), sem("o_gateT"), sem("o_gateT_copied")
        gates_stored, gain_chain = sem("o_gates_stored"), sem("o_gain_chain")
        acc_stored, row_stored = [sem(f"o_acc_st{s}") for s in two], [sem(f"o_row_st{s}") for s in two]
        fhi_done, flo_done, o_staged = sem("o_f_hi"), sem("o_f_lo"), sem("o_o_staged")
        aT_done, ahi_done, alo_done, y_done = sem("o_aT"), sem("o_aT_hi"), sem("o_aT_lo"), sem("o_y")
        gated, added, ss_done, rs_done = sem("o_gated"), sem("o_added"), sem("o_ss_done"), sem("o_rs_done")
        xn_done, xT_done, hTa, hTv = sem("o_xn"), sem("o_xT"), sem("o_hTa"), sem("o_hTv")
        l_done, nm_done, ex_done, aff_done = sem("o_logits"), sem("o_nm_done"), sem("o_ex"), sem("o_aff")
        pchain, vchain, passed = sem("o_pool_chain"), sem("o_dve_chain"), sem("o_pool_waits_passed")
        mods, gs2, O, fmixT, AFF, ident = (t[k] for k in ("mods", "gs2", "O", "fmixT", "AFF", "ident"))
        SH = 3 * DK
        HK = DK // 2
        W_ORDER = [(i + FT) % DK for i in range(DK)]
        xp, xs = a["x_prompt"][0], a["x_sample"][0]
        block = x.enter_context(nc.Block())

        def kind(n):
            return 0 if is_int(n) and n < CT else 1

        def run(eng, step):
            run_steps(eng, step, 2, NT // 2 - 1, NT + 1)

        @block.sync
        def _(sp):
            w_v = a["w_out"][0].rearrange("(k p) n -> p k n", p=P)

            def step(n, s, j):
                if active(n, 0, NT - 1):
                    wait_slot(sp, added, n, 1, 2)
                    src = xp[n * P:(n + 1) * P, :] if kind(n) == 0 else xs[bass.ds((n - CT) * P, P), :]
                    sp.dma_start(xt[s], src).then_inc(x_loaded[s], 16)
                    if is_int(n) and n == 0:
                        for i, k in enumerate(W_ORDER):
                            if i >= 2:
                                sp.wait_ge(whi_done, i - 1)
                                sp.wait_ge(wlo_done, i - 1)
                            sp.dma_start(w_raw[i % 2][:], w_v[:, k, :]).then_inc(w_loaded[i % 2], 16)
                if active(n, 1, NT):
                    m, o = n - 1, 1 - s
                    sp.wait_ge(added, m + 1)
                    sp.dma_start(a["s_acc"][bass.ds(m * P, P), :], x2[o]).then_inc(acc_stored[o], 16)
                if active(n, 2, NT + 1):
                    m = n - 2
                    sp.wait_ge(aff_done, 2 * (m + 1))
                    sp.dma_start(a["s_rows"][bass.ds(m * P, P), :], row[s][:]).then_inc(row_stored[s], 16)

            run(sp, step)
            for s in two:
                sp.wait_ge(acc_stored[s], 16 * (NT // 2))
                sp.wait_ge(row_stored[s], 16 * (NT // 2))

        @block.gpsimd
        def _(pool):
            pool = PlainWaits(pool, passed)

            def stage(m, s):
                wait_slot(pool, y_done, m, 1, 2)
                split_hi(nc.gpsimd, f_hi[s][:], fmixT[:, :, bass.ds(m * P, P)]).then_inc(fhi_done, 1)
                wait_slot(pool, aT_done, m, 1, 1)
                nc.gpsimd.tensor_copy(o_st[:], at(O, m)).then_inc(o_staged, 1)

            stage(0, 0)

            def step(n, s, j):
                o = 1 - s
                if active(n, 1, NT):
                    m = n - 1
                    pool.wait_ge(gated, 2 * (m + 1))
                    pool.wait_ge(x_loaded[o], 16 * (j + s))
                    nc.gpsimd.tensor_tensor(x2[o], x2[o], xt[o], ALU.add).then_inc(added, 1)
                if active(n, 0, NT - 2):
                    stage(n + 1, o)
                if active(n, 1, NT):
                    pool.wait_ge(ss_done, m + 1)
                    c = Chain(pool, pchain, 1, m)
                    c.link(nc.gpsimd.tensor_scalar(ms[:], ss[o][:], 1.0 / D, EPS, ALU.mult, ALU.add))
                    nc.gpsimd.tensor_tensor(rs[o][:], ms[:], t["neg_half"][:], ALU.pow).then_inc(rs_done, 1)

            run(pool, step)

        @block.scalar
        def _(act):
            act.wait_ge(gateT_done, 1)
            nc.scalar.copy(gate_row[:], l_ps[0:4 * DK, 0:P]).then_inc(gateT_copied, 1)
            act.wait_ge(gateT_copied, 1)
            act.dma_start(a["s_gates"].rearrange("g k (j p) -> (g k j) p", p=P), gate_row[:]).then_inc(gates_stored, 16)
            act.dma_start(w_r[:], a["w_router"][0].rearrange("(k p) n -> p k n", p=P)).then_inc(rest_loaded, 16)
            for i, k in enumerate(W_ORDER):
                act.wait_ge(w_loaded[i % 2], 16 * (i // 2 + 1))
                nc.scalar.copy(w_hi[:, k, :], w_raw[i % 2][:]).then_inc(whi_done, 1)
                if i == FT - 1:
                    act.wait_ge(aT_done, 1)
                    nc.scalar.copy(aT_hi[:], aT_ps[:]).then_inc(ahi_done, 1)
                if i == 0:
                    act.wait_ge(gates_stored, 16)
                    act.dma_start(gate[:], a["s_gates"][0].partition_broadcast(P)).then_inc(rest_loaded, 16)

            def step(n, s, j):
                o = 1 - s
                if active(n, 1, NT - 1):
                    act.wait_ge(aT_done, n + 1)
                    wait_slot(act, y_done, n, 1, 1)
                    nc.scalar.copy(aT_hi[:], aT_ps[:]).then_inc(ahi_done, 1)
                if active(n, 2, NT + 1):
                    m = n - 2
                    act.wait_ge(xT_done, 2 * m + 1)
                    wait_slot(act, l_done, m, 1, 1)
                    for k in range(HK):
                        nc.scalar.activation(hT[:, k, :], xT_ps[0][:, k * P:(k + 1) * P], ACT.Identity,
                                             scale=gs2[:, k, kind(m):kind(m) + 1],
                                             bias=mods[:, SH + k, kind(m):kind(m) + 1]).then_inc(hTa, 1)
                if active(n, 1, NT):
                    m = n - 1
                    act.wait_ge(added, m + 1)
                    wait_slot(act, rs_done, m, 1, 2)
                    wait_slot(act, ss_done, m, 1, 1)
                    nc.scalar.activation(junk, x2[o], ACT.Square, accum_out=ss[o][:]).then_inc(ss_done, 1)
                if active(n, 2, NT + 1):
                    m = n - 2
                    act.wait_ge(nm_done, m + 1)
                    wait_slot(act, aff_done, m, 2, 2)
                    nc.scalar.activation(ex[s][:], l_ps[:, 0:NE], ACT.Exp, bias=nm[:], accum_out=se[s][:])\
                        .then_inc(ex_done, 1)

            run(act, step)

        @block.vector
        def _(dve):
            def f_rest(m, s):
                dve.wait_ge(fhi_done, m + 1)
                wait_slot(dve, y_done, m, 1, 2)
                split_lo(nc.vector, f_lo[s][:], fmixT[:, :, bass.ds(m * P, P)], f_hi[s][:]).then_inc(flo_done, 1)

            for g in two:
                for k in two:
                    nc.vector.tensor_copy(gate_col[:, g, k, :], mods[:, (2 + 3 * g) * DK:(3 + 3 * g) * DK, k])\
                        .then_inc(gates_ready, 1)
            scaled_gain(nc.vector, Chain(dve, gain_chain, 2, 0).link, gs2, mods, t["vec_cols"], 4, 3)
            f_rest(0, 0)
            for i, k in enumerate(W_ORDER):
                dve.wait_ge(whi_done, i + 1)
                split_lo(nc.vector, w_lo[:, k, :], w_raw[i % 2][:], w_hi[:, k, :]).then_inc(wlo_done, 1)
                if i == FT - 1:
                    dve.wait_ge(ahi_done, 1)
                    split_lo(nc.vector, aT_lo[:], aT_ps[:], aT_hi[:]).then_inc(alo_done, 1)
            dve.wait_ge(rest_loaded, 32)

            def step(n, s, j):
                o = 1 - s
                if active(n, 1, NT):
                    m = n - 1
                    dve.wait_ge(y_done, m + 1)
                    wait_slot(dve, acc_stored[o], j - 1 + s, 16, 1)
                    wait_slot(dve, xn_done, m, 1, 2)
                    for h in two:
                        nc.vector.tensor_tensor(x2[o][:, h * HD:(h + 1) * HD], y_ps[o][h][:],
                                                gate[:, kind(m), h * HD:(h + 1) * HD], ALU.mult).then_inc(gated, 1)
                if active(n, 2, NT + 1):
                    m = n - 2
                    dve.wait_ge(xT_done, 2 * m + 2)
                    wait_slot(dve, l_done, m, 1, 1)
                    for k in range(HK, DK):
                        nc.vector.tensor_scalar(hT[:, k, :], xT_ps[1][:, (k - HK) * P:(k - HK + 1) * P],
                                                gs2[:, k, kind(m):kind(m) + 1], mods[:, SH + k, kind(m):kind(m) + 1],
                                                ALU.mult, ALU.add).then_inc(hTv, 1)
                if active(n, 1, NT - 1):
                    dve.wait_ge(ahi_done, n + 1)
                    wait_slot(dve, y_done, n, 1, 1)
                    split_lo(nc.vector, aT_lo[:], aT_ps[:], aT_hi[:]).then_inc(alo_done, 1)
                if active(n, 0, NT - 2):
                    f_rest(n + 1, o)
                if active(n, 1, NT):
                    m = n - 1
                    dve.wait_ge(rs_done, m + 1)
                    wait_slot(dve, row_stored[o], j - 1 + s, 16, 1)
                    nc.vector.tensor_scalar(row[o][:, 0:D], x2[o], rs[o][:], None, ALU.mult).then_inc(xn_done, 1)
                if active(n, 2, NT + 1):
                    m = n - 2
                    dve.wait_ge(l_done, m + 1)
                    wait_slot(dve, ex_done, m, 1, 1)
                    nc.vector.tensor_reduce(nm[:], l_ps[:, 0:NE], AX.X, ALU.max, negate=True).then_inc(nm_done, 1)
                    dve.wait_ge(ex_done, m + 1)
                    Chain(dve, vchain, 1, m).link(nc.vector.reciprocal(ri[:], se[s][:]))
                    nc.vector.tensor_scalar(row[s][:, D:], ex[s][:], ri[:], None, ALU.mult).then_inc(aff_done, 1)
                    nc.vector.tensor_scalar(at(AFF, m), ex[s][:], ri[:], None, ALU.mult).then_inc(aff_done, 1)
                    dve.wait_ge(aff_done, 2 * (m + 1))

            run(dve, step)

        @block.tensor
        def _(pe):
            pe.wait_ge(gates_ready, 4)
            nc.tensor.transpose(l_ps[0:4 * DK, 0:P], gate_col[:].rearrange("p g k j -> p (g k j)"), ident[:])\
                .then_inc(gateT_done, 1)

            def product(s, k, st_hi, st_lo, tile0, first, last):
                if tile0:
                    pe.wait_ge(wlo_done, W_ORDER.index(k) + 1)
                for h in two:
                    cols = slice(h * HD, (h + 1) * HD)
                    nc.tensor.matmul(y_ps[s][h][:], st_hi, w_hi[:, k, cols], start=first, stop=False)
                    nc.tensor.matmul(y_ps[s][h][:], st_hi, w_lo[:, k, cols], start=False, stop=False)
                    ins = nc.tensor.matmul(y_ps[s][h][:], st_lo, w_hi[:, k, cols], start=False, stop=last)
                return ins

            def step(n, s, j):
                o, tile0 = 1 - s, is_int(n) and n == 0
                if active(n, 0, NT - 1):
                    pe.wait_ge(o_staged, n + 1)
                    wait_slot(pe, alo_done, n, 1, 1)
                    for k in range(FT):
                        last = nc.tensor.transpose(aT_ps[:, k * P:(k + 1) * P], o_st[:, k * P:(k + 1) * P], ident[:])
                    last.then_inc(aT_done, 1)
                    wait_slot(pe, gated, n, 2, 2)
                    pe.wait_ge(flo_done, n + 1)
                    for k in range(FT):
                        product(s, FT + k, f_hi[s][:, k, :], f_lo[s][:, k, :], tile0, k == 0, False)
                if active(n, 2, NT + 1):
                    m = n - 2
                    if is_int(m) and m == 0:
                        pe.wait_ge(rest_loaded, 32)
                        pe.wait_ge(gateT_copied, 1)
                    wait_slot(pe, ex_done, m, 1, 1)
                    for k in range(DK):
                        pe.wait_ge((hTa, hTv)[k // HK], m * HK + k % HK + 1)
                        last = nc.tensor.matmul(l_ps[:, 0:NE], hT[:, k, :], w_r[:, k, :], start=(k == 0),
                                                stop=(k == DK - 1))
                    last.then_inc(l_done, 1)
                if active(n, 0, NT - 1):
                    pe.wait_ge(alo_done, n + 1)
                    for k in range(FT):
                        last = product(s, k, aT_hi[:, k, :], aT_lo[:, k, :], tile0, False, k == FT - 1)
                    last.then_inc(y_done, 1)
                if active(n, 1, NT):
                    m = n - 1
                    pe.wait_ge(xn_done, m + 1)
                    for b in two:
                        wait_slot(pe, (hTa, hTv)[b], m, HK, 1)
                        for k in range(HK):
                            c0 = (b * HK + k) * P
                            last = nc.tensor.transpose(xT_ps[b][:, k * P:(k + 1) * P], row[o][:, c0:c0 + P], ident[:])
                        last.then_inc(xT_done, 1)

            run(pe, step)


def routing(nc, a, t):
    with ExitStack() as x:
        sb = lambda name, shape, dt=F32: x.enter_context(nc.sbuf_tensor(name, shape, dt))
        sem = lambda name: x.enter_context(nc.semaphore(name))
        ps = lambda name: x.enter_context(nc.psum_tensor(name, [P, 512], F32))
        two = range(2)
        BITS = 30
        UNROLL = 5
        NONE = 512.0
        tri_f, tri, ones = sb("tri_f", [P, P]), sb("tri", [P, P], BF16), sb("ones_bf", [P, P], BF16)
        iota_f, iota = sb("iota_f", [P, P]), sb("iota", [P, P], BF16)
        pay_f, pay = sb("pay_f", [P, NT, 2]), sb("pay", [P, NT, 2], BF16)
        bit, cur, cand = (sb(n, [P, 2, NE], U32) for n in ("bit", "cur", "cand"))
        keep = sb("keep", [P, 2, NE])
        ge, cnt = sb("reaches", [P, NT, NE], BF16), sb("counts", [P, 2, NE], BF16)
        mk = sb("above_at", [P, NT, 2, NE], BF16)
        run = sb("tiles_before", [P, NT, 2, NE], BF16)
        total = sb("total", [P, 2, NE], BF16)
        above = sb("n_above", [P, 2, NE])
        pe_, pg = sb("pos_at", [P, NT, NE]), sb("pos_above", [P, NT, NE])
        pos = sb("pos", [P, NT, NE])
        half = [sb(f"in_half{h}", [P, LT, NE]) for h in two]
        place, place_c = sb("place", [P, LT, NE], BF16), sb("place_ctx", [P, CT, NE], BF16)
        pay_h = sb("pay_halves", [P, NE, LT, 2, 2], BF16)
        hot = [sb(f"one_hot{s}", [P, LT, P], BF16) for s in two]
        hot_c = [sb(f"one_hot_ctx{s}", [P, CT, CAP_C], BF16) for s in two]
        ids = [sb(f"ids{s}", [P, 3, 2]) for s in two]
        n_ps, l_ps, c_ps = ps("count_ps"), ps("prefix_lat_ps"), ps("prefix_ctx_ps")
        id_ps = [ps(f"ids_ps{s}") for s in two]
        loaded, counted, totalled = sem("r_loaded"), sem("r_counted"), sem("r_totalled")
        v, pre_ready, pre_done = sem("r_dve"), sem("r_prefix_ready"), sem("r_prefix_done")
        hot_done, ids_done, ids_read, id_chain = sem("r_one_hot"), sem("r_ids"), sem("r_ids_read"), sem("r_ids_chain")
        setup = sem("r_setup")
        AFF, IDX, W = t["AFF"], t["IDX"], t["expert_weights"]
        groups = ((0, 0, CT), (1, CT, NT))
        PRIMED = 1
        block = x.enter_context(nc.Block())

        @block.sync
        def _(sp):
            sp.dma_start(tri_f[:], a["k_before"]).then_inc(loaded, 16)
            sp.dma_start(iota_f[:], a["k_slots"][0:P].partition_broadcast(P)).then_inc(loaded, 16)
            sp.dma_start(pay_f[:], a["k_tile_part"].rearrange("(n p) q -> p n q", p=P)).then_inc(loaded, 16)
            for i, name, f in W.first():
                if i >= W.RING:
                    sp.wait_ge(W.lo_done, i - W.RING + 1)
                W.load(sp.dma_start, i, name, f, 0)

        @block.scalar
        def _(act):
            for i, name, f in W.first():
                act.wait_ge(W.loaded[i % W.RING], (i // W.RING + 1) * 16)
                nc.scalar.copy(W.hi[name][f][:], W.raw[i % W.RING][:]).then_inc(W.hi_done, 1)

        @block.gpsimd
        def _(pool):
            pool.wait_ge(loaded, 48)
            nc.gpsimd.memset(ones[:], 1.0).then_inc(setup, 1)
            nc.gpsimd.tensor_copy(tri[:], tri_f[:]).then_inc(setup, 1)
            nc.gpsimd.tensor_copy(iota[:], iota_f[:]).then_inc(setup, 1)
            nc.gpsimd.tensor_copy(pay[:], pay_f[:]).then_inc(setup, 1)
            for i, name, f in W.first():
                pool.wait_ge(W.hi_done, i + 1)
                split_lo(nc.gpsimd, W.lo[name][f][:], W.raw[i % W.RING][:], W.hi[name][f][:]).then_inc(W.lo_done, 1)

        @block.vector
        def _(dve):
            dve.sem_inc(id_chain, PRIMED)
            nc.vector.memset(bit[:], 1 << (BITS - 1))
            Chain(dve, v, 1, 0).link(nc.vector.memset(cur[:], 0))
            PER = 5

            def narrow(b):
                c = Chain(dve, v, PER, b)
                c.base = b * PER + 1
                c.link(nc.vector.tensor_tensor(cand[:], cur[:], bit[:], ALU.bitwise_or))
                for k, n0, n1 in groups:
                    ins = nc.vector.tensor_tensor(
                        ge[:, n0:n1], AFF[:, n0:n1],
                        cand[:, k].bitcast(F32).unsqueeze(1).to_broadcast([P, n1 - n0, NE]), ALU.is_ge)
                c.link(ins)
                with nc.allow_low_precision(reason="counts up to 16 are exact in bfloat16"):
                    for k, n0, n1 in groups:
                        ins = nc.vector.tensor_reduce(cnt[:, k], ge[:, n0:n1].rearrange("p n e -> p e n"), AX.X, ALU.add)
                ins.then_inc(counted, 1)
                c.link(nc.vector.tensor_scalar(bit[:], bit[:], 1, None, ALU.logical_shift_right))
                dve.wait_ge(totalled, b + 1)
                for k, capacity in ((0, CAP_C), (1, CAP_L)):
                    ins = nc.vector.scalar_tensor_tensor(keep[:, k], n_ps[:, k * NE:(k + 1) * NE], float(capacity),
                                                         cand[:, k].bitcast(F32), ALU.is_ge, ALU.mult)
                c.link(ins)
                c.link(nc.vector.tensor_tensor(cur[:].bitcast(F32), cur[:].bitcast(F32), keep[:], ALU.max))

            with dve.Fori(0, BITS // UNROLL) as i:
                for b in range(UNROLL):
                    narrow(i * UNROLL + b)
            c = Chain(dve, v, 99, 0)
            c.base = BITS * PER + 1
            for k, n0, n1 in groups:
                thr = cur[:, k].bitcast(F32).unsqueeze(1).to_broadcast([P, n1 - n0, NE])
                nc.vector.tensor_tensor(mk[:, n0:n1, 0], AFF[:, n0:n1], thr, ALU.is_gt)
                nc.vector.tensor_tensor(mk[:, n0:n1, 1], AFF[:, n0:n1], thr, ALU.is_equal)
                ins = nc.vector.memset(run[:, n0], 0.0)
            c.link(ins)
            for k, n0, n1 in groups:
                for n in range(n0 + 1, n1):
                    c.link(nc.vector.tensor_tensor(run[:, n], run[:, n - 1], mk[:, n - 1], ALU.add))
                ins = nc.vector.tensor_tensor(total[:, k], run[:, n1 - 1, 0], mk[:, n1 - 1, 0], ALU.add)
            ins.then_inc(pre_ready, 1)
            dve.wait_ge(pre_done, 1)
            c.link(nc.vector.tensor_copy(above[:], n_ps[:, 0:2 * NE]))
            for k, n0, n1 in groups:
                src = (c_ps, l_ps)[k][:, 0:(n1 - n0) * 2 * NE].rearrange("p (n q e) -> p n q e", q=2, e=NE)
                nc.vector.tensor_tensor(pe_[:, n0:n1], src[:, :, 1], above[:, k].unsqueeze(1)
                                        .to_broadcast([P, n1 - n0, NE]), ALU.add)
                ins = nc.vector.tensor_scalar(pg[:, n0:n1], src[:, :, 0], -NONE, None, ALU.add)
            c.link(ins)
            c.link(nc.vector.tensor_scalar(pe_[:], pe_[:], -NONE, None, ALU.add))
            c.link(nc.vector.tensor_tensor(pe_[:], pe_[:], mk[:, :, 1], ALU.mult))
            c.link(nc.vector.tensor_tensor(pg[:], pg[:], mk[:, :, 0], ALU.mult))
            c.link(nc.vector.tensor_tensor(pg[:], pg[:], pe_[:], ALU.add))
            c.link(nc.vector.tensor_scalar(pos[:], pg[:], NONE, None, ALU.add))
            c.link(nc.vector.tensor_scalar(half[1][:], pos[:, CT:], float(P), None, ALU.is_ge))
            nc.vector.tensor_scalar(half[0][:], half[1][:], -1.0, 1.0, ALU.mult, ALU.add)
            c.link(nc.vector.scalar_tensor_tensor(place[:], half[1][:], -float(P), pos[:, CT:], ALU.mult, ALU.add))
            nc.vector.tensor_copy(place_c[:], pos[:, 0:CT])
            dve.wait_ge(setup, 4)
            for h in two:
                for q in two:
                    part = pay[:, CT:, q].unsqueeze(1).to_broadcast([P, NE, LT])
                    ins = nc.vector.tensor_tensor(pay_h[:, :, :, h, q], half[h][:].rearrange("p n e -> p e n"), part,
                                                  ALU.mult)
            c.link(ins)

            def index(e, s):
                dve.wait_ge(ids_done, PRIMED + e + 1)
                nc.vector.tensor_copy(ids[s][:, 0:2, :], id_ps[s][:, 0:4])
                nc.vector.tensor_copy(ids[s][0:CAP_C, 2, :], id_ps[s][0:CAP_C, 4:6]).then_inc(ids_read, 1)
                dve.wait_ge(ids_read, e + 1)
                for lo, hi, rows in ((0, 2, P), (2, 3, CAP_C)):
                    dst = IDX[0:rows, bass.ds(e, 1), lo:hi].rearrange("p e h -> p (e h)")
                    ins = nc.vector.scalar_tensor_tensor(dst, ids[s][0:rows, lo:hi, 0], float(P),
                                                         ids[s][0:rows, lo:hi, 1], ALU.mult, ALU.add)
                ins.then_inc(id_chain, 1)

            def one_hots(e, s):
                if not is_int(e) or e >= 2:
                    dve.wait_ge(ids_done, PRIMED + e - 1)
                for dst, src, n1, w in ((hot_c[s], place_c, CT, CAP_C), (hot[s], place, LT, P)):
                    ins = nc.vector.tensor_tensor(
                        dst[:], iota[:, 0:w].unsqueeze(1).to_broadcast([P, n1, w]),
                        src[:, :, bass.ds(e, 1)].to_broadcast([P, n1, w]), ALU.is_equal)
                ins.then_inc(hot_done, 1)

            def pair(j):
                one_hots(2 * j, 0)
                if not is_int(j):
                    index(2 * j - 1, 1)
                one_hots(2 * j + 1, 1)
                index(2 * j, 0)

            pair(0)
            with dve.Fori(1, NE // 2) as j:
                pair(j)
            index(NE - 1, 1)
            dve.wait_ge(id_chain, PRIMED + NE)

        @block.tensor
        def _(pe):
            pe.sem_inc(ids_done, PRIMED)
            pe.wait_ge(setup, 4)
            with pe.Fori(0, BITS // UNROLL) as i:
                for b in range(UNROLL):
                    pe.wait_ge(counted, i * UNROLL + (b + 1))
                    nc.tensor.matmul(n_ps[:, 0:2 * NE], ones[:], cnt[:].rearrange("p k e -> p (k e)"), start=True,
                                     stop=True).then_inc(totalled, 1)
            pe.wait_ge(pre_ready, 1)
            flat = lambda z, n0, n1: z[:, n0:n1].rearrange("p n q e -> p (n q e)")
            for k, n0, n1 in groups:
                w = (n1 - n0) * 2 * NE
                dst = (c_ps, l_ps)[k][:, 0:w]
                nc.tensor.matmul(dst, tri[:], flat(mk, n0, n1), start=True, stop=False)
                nc.tensor.matmul(dst, ones[:], flat(run, n0, n1), start=False, stop=True)
            nc.tensor.matmul(n_ps[:, 0:2 * NE], ones[:], total[:].rearrange("p k e -> p (k e)"), start=True, stop=True)\
                .then_inc(pre_done, 1)
            def ids_of(e, s):
                pe.wait_ge(hot_done, e + 1)
                if not is_int(e) or e >= 2:
                    pe.wait_ge(id_chain, PRIMED + e - 1)
                for n in range(LT):
                    halves = pay_h[:, bass.ds(e, 1), n].rearrange("p e h q -> p (e h q)")
                    nc.tensor.matmul(id_ps[s][:, 0:4], hot[s][:, n, :], halves, start=(n == 0), stop=(n == LT - 1))
                for n in range(CT):
                    last = nc.tensor.matmul(id_ps[s][0:CAP_C, 4:6], hot_c[s][:, n, :], pay[:, n, :],
                                            start=(n == 0), stop=(n == CT - 1))
                last.then_inc(ids_done, 1)

            for s in two:
                ids_of(s, s)
            with pe.Fori(1, NE // 2) as j:
                for s in two:
                    ids_of(2 * j + s, s)


class ExpertWeights:
    RING, NF = 6, DE // P
    HEAD = 2 * NF

    def __init__(self, nc, a, stack):
        sb = lambda name, dt: stack.enter_context(nc.sbuf_tensor(name, [P, DK, P], dt))
        sem = lambda name: stack.enter_context(nc.semaphore(name))
        self.a = a
        self.raw = [sb(f"w_piece{r}", F32) for r in range(self.RING)]
        names = ("w_e_gate", "w_e_up", "w_e_down")
        self.hi = {n: [sb(f"{n}_hi{f}", F32R) for f in range(self.NF)] for n in names}
        self.lo = {n: [sb(f"{n}_lo{f}", F32R) for f in range(self.NF)] for n in names}
        self.loaded = [sem(f"w_piece_loaded{r}") for r in range(self.RING)]
        self.hi_done, self.lo_done = sem("w_piece_hi"), sem("w_piece_lo")

    def first(self):
        return [(2 * f + q, n, f) for f in range(self.NF) for q, n in enumerate(("w_e_gate", "w_e_up"))]

    def per_step(self, last):
        return [(self.HEAD + 3 * f + q, n, f, q > 0) for f in range(self.NF)
                for q, n in enumerate(("w_e_down", "w_e_gate", "w_e_up")) if not (last and q)]

    def load(self, dma, i, name, f, e):
        w = self.a[name][0][e] if is_int(e) else self.a[name][0][bass.ds(e, 1)].rearrange("e r c -> (e r) c")
        src = w[f * P:(f + 1) * P, :].rearrange("p (k c) -> p k c", c=P) if name == "w_e_down" else \
            w[:, f * P:(f + 1) * P].rearrange("(k p) c -> p k c", p=P)
        dma(self.raw[i % self.RING][:], src).then_inc(self.loaded[i % self.RING], 16)


def experts(nc, a, t):
    with ExitStack() as x:
        sb = lambda name, shape, dt=F32: x.enter_context(nc.sbuf_tensor(name, shape, dt))
        sem = lambda name: x.enter_context(nc.semaphore(name))
        ps = lambda name: x.enter_context(nc.psum_tensor(name, [P, 512], F32))
        two = range(2)
        C = CAP_L + CAP_C
        parts = ((0, P, 1), (P, P, 1), (CAP_L, CAP_C, 0))
        NF, HD = DE // P, D // 2
        NU = 2 * len(parts)
        W = t["expert_weights"]
        PIECES = 3 * NF
        w_hi, w_lo, whi_done, wlo_done = W.hi, W.lo, W.hi_done, W.lo_done
        gate = sb("gate2_rows", [P, 2, D])
        idx = [[sb(f"idx{s}{i}", [P, 1], U32) for i in range(3)] for s in two]
        rows = [sb(f"rows{s}", [P, 3, ROWW]) for s in two]
        aff = [sb(f"slot_aff{s}", [P, 3]) for s in two]
        xm = [sb(f"modulated{b}", [P, C]) for b in two]
        x_hi, x_lo = sb("xsT_hi", [P, DK, C], F32R), sb("xsT_lo", [P, DK, C], F32R)
        act_g, hid = [sb(f"silu_gate{b}", [P, C]) for b in two], [sb(f"hidT{b}", [P, C]) for b in two]
        h_hi, h_lo = sb("hidT_hi", [P, NF, C], F32R), sb("hidT_lo", [P, NF, C], F32R)
        ys = [sb(f"ys{i}", [P, D]) for i in range(3)]
        xT_ps = [ps(f"e_xT_ps{b}") for b in two]
        g_ps, u_ps = [ps(f"e_g_ps{b}") for b in two], [ps(f"e_u_ps{b}") for b in two]
        y_ps = [ps(f"e_y_ps{b}") for b in two]
        gate_loaded = sem("e_gate2_loaded")
        gathered = [sem(f"e_gathered{s}") for s in two]
        idx_ready, aff_done = sem("e_idx"), sem("e_slot_aff")
        xT_done, modulated = sem("e_xT"), [sem(f"e_modulated{b}") for b in two]
        xhi_done, xlo_done = sem("e_x_hi"), sem("e_x_lo")
        gu_done, silu_done, hid_done = sem("e_gate_up"), sem("e_silu"), sem("e_hid")
        hhi_done, hlo_done, y_done = sem("e_hid_hi"), sem("e_hid_lo"), sem("e_y")
        ys_done, added = sem("e_ys"), sem("e_added")
        mods, gs2, IDX, ident = (t[k] for k in ("mods", "gs2", "IDX", "ident"))
        SH = 3 * DK
        block = x.enter_context(nc.Block())

        def wait_pos(eng, sem, value):
            if not is_int(value) or value > 0:
                eng.wait_ge(sem, value)

        def pairs(eng, step):
            for s in two:
                step(s, s, 0, False)
            with eng.Fori(1, NE // 2 - 1) as j:
                for s in two:
                    step(2 * j + s, s, j, False)
            for s in two:
                step(NE - 2 + s, s, NE // 2 - 1, s == 1)

        def piece(i, e, last):
            if last:
                f = (i - W.HEAD) // 3
                return PIECES * e + W.HEAD + f, W.HEAD + f
            return PIECES * e + i, i

        @block.sync
        def _(sync):
            sp = PlainWaits(sync, x.enter_context(nc.semaphore("e_sync_waits_passed")))
            sp_dma = sync.dma_start
            sp_dma(gate[:], a["s_gates"][1].partition_broadcast(P)).then_inc(gate_loaded, 16)

            sp.wait_ge(gathered[0], 48)

            def load(e, s, j, last):
                for i, name, f, ahead in W.per_step(last):
                    n, ring = piece(i, e, last)
                    sp.wait_ge(whi_done, n - W.RING + 1)
                    sp.wait_ge(wlo_done, n - W.RING + 1)
                    W.load(sp_dma, ring, name, f, e + 1 if ahead else e)

            pairs(sync, load)

        @block.gpsimd
        def _(pool):
            passed = x.enter_context(nc.semaphore("e_pool_waits_passed"))
            pool = PlainWaits(pool, passed)

            def gather(e, s, j):
                pool.wait_ge(idx_ready, e + 1)
                wait_slot(pool, xT_done, e, DK, 2)
                wait_slot(pool, aff_done, e, 1, 2)
                for i, (_, n, _) in enumerate(parts):
                    nc.gpsimd.indirect_dma_start(
                        out=rows[s][0:n, i, :], out_offset=None, in_=a["s_rows"],
                        in_offset=bass.IndirectOffsetOnAxis(ap=idx[s][i][0:n, :], axis=0)).then_inc(gathered[s], 16)

            def scatter(e, s, j):
                pool.wait_ge(added, 48 * e)
                for i, (_, n, _) in enumerate(parts):
                    pool.wait_ge(ys_done, 6 * e + 2 * (i + 1))
                    nc.gpsimd.indirect_dma_start(
                        out=a["s_acc"], out_offset=bass.IndirectOffsetOnAxis(ap=idx[s][i][0:n, :], axis=0),
                        in_=ys[i][0:n, :], in_offset=None, compute_op=ALU.add).then_inc(added, 16)

            gather(0, 0, 0)
            gather(1, 1, 0)
            scatter(0, 0, 0)
            with pool.Fori(1, NE // 2) as j:
                gather(2 * j, 0, j)
                scatter(2 * j - 1, 1, j)
                gather(2 * j + 1, 1, j)
                scatter(2 * j, 0, j)
            scatter(NE - 1, 1, 0)
            pool.wait_ge(added, 48 * NE)

        def act_piece(act, i, name, f, ring, r):
            act.wait_ge(W.loaded[ring % W.RING], (ring // W.RING + 1 + r) * 16)
            nc.scalar.copy(w_hi[name][f][:], W.raw[ring % W.RING][:]).then_inc(whi_done, 1)

        def dve_piece(dve, i, name, f, ring):
            dve.wait_ge(whi_done, i + 1)
            split_lo(nc.vector, w_lo[name][f][:], W.raw[ring % W.RING][:], w_hi[name][f][:]).then_inc(wlo_done, 1)

        @block.scalar
        def _(act):
            def modulate(e, u):
                k = 2 * u
                act.wait_ge(xT_done, DK * e + k + 1)
                wait_pos(act, gu_done, NF * e)
                wait_pos(act, xlo_done, DK * e + k - 1)
                for lo, hi, kind in ((0, CAP_L, 1), (CAP_L, C, 0)):
                    ins = nc.scalar.activation(xm[0][:, lo:hi], xT_ps[0][:, lo:hi], ACT.Identity,
                                               scale=gs2[:, k, kind:kind + 1], bias=mods[:, SH + k, kind:kind + 1])
                ins.then_inc(modulated[0], 1)
                for b in two:
                    act.wait_ge(modulated[b], (DK // 2) * e + u + 1)
                    nc.scalar.copy(x_hi[:, k + b, :], xm[b][:]).then_inc(xhi_done, 1)

            def step(e, s, j, last):
                for i, name, f, ahead in W.per_step(last):
                    n, ring = piece(i, e, last)
                    if ahead:
                        act.wait_ge(gu_done, NF * e + f + 1)
                    elif f == 0:
                        wait_pos(act, y_done, NU * e)
                    act_piece(act, n, name, f, ring, 2 * e)
                    if not ahead:
                        act.wait_ge(gu_done, NF * e + f + 1)
                        wait_pos(act, hid_done, NF * e + f - 1)
                        nc.scalar.activation(act_g[f % 2][:], g_ps[f % 2][:, 0:C], ACT.Silu).then_inc(silu_done, 1)
                        act.wait_ge(hid_done, NF * e + f + 1)
                        nc.scalar.copy(h_hi[:, f, :], hid[f % 2][:]).then_inc(hhi_done, 1)
                if not last:
                    for u in range(DK // 2):
                        modulate(e + 1, u)

            for u in range(DK // 2):
                modulate(0, u)
            pairs(act, step)

        @block.vector
        def _(dve):
            dve.wait_ge(gate_loaded, 16)

            def stage_idx(e, s):
                for i, (_, n, _) in enumerate(parts):
                    src = IDX[0:n, bass.ds(e, 1), i:i + 1].rearrange("p e i -> p (e i)")
                    ins = nc.vector.tensor_copy(idx[s][i][0:n, :], src)
                ins.then_inc(idx_ready, 1)

            def modulate(e, u):
                k = 2 * u + 1
                dve.wait_ge(xT_done, DK * e + k + 1)
                wait_pos(dve, xhi_done, DK * e + k - 1)
                wait_pos(dve, xlo_done, DK * e + k - 1)
                for lo, hi, kind in ((0, CAP_L, 1), (CAP_L, C, 0)):
                    ins = nc.vector.tensor_scalar(xm[1][:, lo:hi], xT_ps[1][:, lo:hi], gs2[:, k, kind:kind + 1],
                                                  mods[:, SH + k, kind:kind + 1], ALU.mult, ALU.add)
                ins.then_inc(modulated[1], 1)
                dve.wait_ge(modulated[1], (DK // 2) * e + u + 1)
                for b in two:
                    dve.wait_ge(xhi_done, DK * e + k + b)
                    split_lo(nc.vector, x_lo[:, 2 * u + b, :], xm[b][:], x_hi[:, 2 * u + b, :]).then_inc(xlo_done, 1)

            def step(e, s, j, last):
                for i, name, f, ahead in W.per_step(last):
                    n, ring = piece(i, e, last)
                    dve_piece(dve, n, name, f, ring)
                    if ahead:
                        continue
                    if f == 0 and not last:
                        wait_pos(dve, added, 48 * e)
                        stage_idx(e + 1, 1 - s)
                    dve.wait_ge(silu_done, NF * e + f + 1)
                    wait_pos(dve, hlo_done, NF * e + f - 1)
                    nc.vector.tensor_tensor(hid[f % 2][:], act_g[f % 2][:], u_ps[f % 2][:, 0:C], ALU.mult)\
                        .then_inc(hid_done, 1)
                    dve.wait_ge(hhi_done, NF * e + f + 1)
                    split_lo(nc.vector, h_lo[:, f, :], hid[f % 2][:], h_hi[:, f, :]).then_inc(hlo_done, 1)
                dve.wait_ge(gathered[s], 48 * (j + 1))
                for i, (_, n, _) in enumerate(parts):
                    ins = nc.vector.tensor_copy(aff[s][0:n, i:i + 1], rows[s][0:n, i, bass.ds(D + e, 1)])
                ins.then_inc(aff_done, 1)
                dve.wait_ge(aff_done, e + 1)
                wait_slot(dve, added, e, 48, 1)
                for u in range(NU):
                    i, h = u // 2, u % 2
                    _, n, kind = parts[i]
                    dve.wait_ge(y_done, NU * e + u + 1)
                    nc.vector.scalar_tensor_tensor(ys[i][0:n, h * HD:(h + 1) * HD], y_ps[h][0:n, :],
                                                   aff[s][0:n, i:i + 1], gate[0:n, kind, h * HD:(h + 1) * HD],
                                                   ALU.mult, ALU.mult).then_inc(ys_done, 1)
                    if u < DK // 2 and not last:
                        modulate(e + 1, u)

            stage_idx(0, 0)
            for u in range(DK // 2):
                modulate(0, u)
            pairs(dve, step)

        @block.tensor
        def _(pe):
            def transpose(e, s, rounds, k):
                b = k % 2
                if k == 0:
                    pe.wait_ge(gathered[s], 48 * rounds)
                wait_pos(pe, modulated[b], (DK // 2) * e + k // 2)
                for i, (c0, n, _) in enumerate(parts):
                    last = nc.tensor.transpose(xT_ps[b][:, c0:c0 + n], rows[s][0:n, i, k * P:(k + 1) * P],
                                               ident[0:n, 0:n])
                last.then_inc(xT_done, 1)

            def three(dst, st_hi, st_lo, mv_hi, mv_lo, first, last):
                nc.tensor.matmul(dst, st_hi, mv_hi, start=first, stop=False)
                nc.tensor.matmul(dst, st_hi, mv_lo, start=False, stop=False)
                return nc.tensor.matmul(dst, st_lo, mv_hi, start=False, stop=last)

            def step(e, s, j, is_last):
                for f in range(NF):
                    wait_pos(pe, hid_done, NF * e + f - 1)
                    pe.wait_ge(wlo_done, PIECES * e + 3 * f - 1 if not is_int(e) or e > 0 else 2 * f + 2)
                    for name, dst in (("w_e_gate", g_ps), ("w_e_up", u_ps)):
                        for k in range(DK):
                            if f == 0 and name == "w_e_gate":
                                pe.wait_ge(xlo_done, DK * e + k + 1)
                            last = three(dst[f % 2][:, 0:C], w_hi[name][f][:, k, :], w_lo[name][f][:, k, :],
                                         x_hi[:, k, :], x_lo[:, k, :], k == 0, k == DK - 1)
                    last.then_inc(gu_done, 1)
                for u in range(NU):
                    i, h = u // 2, u % 2
                    c0, n, _ = parts[i]
                    wait_pos(pe, ys_done, NU * e + u - 1)
                    for f in range(NF):
                        if u == 0:
                            pe.wait_ge(hlo_done, NF * e + f + 1)
                            pe.wait_ge(wlo_done, PIECES * e + W.HEAD + (1 if is_last else 3) * f + 1)
                        cols = slice(h * DK // 2, (h + 1) * DK // 2)
                        last = three(y_ps[h][0:n, :], h_hi[:, f, c0:c0 + n], h_lo[:, f, c0:c0 + n],
                                     w_hi["w_e_down"][f][:, cols, :], w_lo["w_e_down"][f][:, cols, :],
                                     f == 0, f == NF - 1)
                    last.then_inc(y_done, 1)
                    if u < DK // 2 and not is_last:
                        for k in (2 * u, 2 * u + 1):
                            transpose(e + 1, 1 - s, j + 1 + s, k)

            for k in range(DK):
                transpose(0, 0, 1, k)
            pairs(pe, step)


def final_norm(nc, a, t):
    with ExitStack() as x:
        sb = lambda name, shape, dt=F32: x.enter_context(nc.sbuf_tensor(name, shape, dt))
        sem = lambda name: x.enter_context(nc.semaphore(name))
        NS = 6
        fg = sb("final_g_rows", [P, D])
        xt = [sb(f"z{s}", [P, D]) for s in range(NS)]
        sq = [sb(f"z_sq{s}", [P, D]) for s in range(2)]
        yt = [sb(f"y{s}", [P, D]) for s in range(NS)]
        ss, rs = [sb(f"z_ss{s}", [P, 1]) for s in range(NS)], [sb(f"z_rs{s}", [P, 1]) for s in range(NS)]
        ms = [sb(f"z_ms{s}", [P, 1]) for s in range(NS)]
        g_loaded = sem("z_g_loaded")
        loaded, stored = [sem(f"z_loaded{s}") for s in range(NS)], [sem(f"z_stored{s}") for s in range(NS)]
        ss_done, ms_done, rs_done, y_done = sem("z_ss"), sem("z_ms"), sem("z_rs"), sem("z_y")
        passed = sem("z_pool_waits_passed")
        yp, ysm = a["y_prompt"][0], a["y_sample"][0]
        block = x.enter_context(nc.Block())

        def tiles(eng, step):
            for s in range(NS):
                step(s, s, 0)
            with eng.Fori(1, NT // NS) as r:
                for s in range(NS):
                    step(r * NS + s, s, r)

        @block.sync
        def _(sp):
            sp.dma_start(fg[:], a["final_g"].partition_broadcast(P)).then_inc(g_loaded, 16)

            def step(n, s, r):
                wait_slot(sp, y_done, n, 1, NS)
                sp.dma_start(xt[s][:], a["s_acc"][bass.ds(n * P, P), :]).then_inc(loaded[s], 16)

            tiles(sp, step)

        @block.scalar
        def _(act):
            def square(n, s, r):
                act.wait_ge(loaded[s], 16 * (r + 1))
                wait_slot(act, ms_done, n, 1, NS)
                wait_slot(act, ss_done, n, 1, 2)
                nc.scalar.activation(sq[s % 2][:], xt[s][:], ACT.Square, accum_out=ss[s][:]).then_inc(ss_done, 1)

            def store(n, s, r):
                act.wait_ge(y_done, n + 1)
                dst = yp[n * P:(n + 1) * P, :] if is_int(n) and n < CT else ysm[bass.ds((n - CT) * P, P), :]
                act.dma_start(dst, yt[s][:]).then_inc(stored[s], 16)

            for s in range(NS):
                square(s, s, 0)
            for s in range(NS):
                store(s, s, 0)
            with act.Fori(1, NT // NS) as r:
                for s in range(NS):
                    square(r * NS + s, s, r)
                for s in range(NS):
                    store(r * NS + s, s, r)
            for s in range(NS):
                act.wait_ge(stored[s], 16 * (NT // NS))

        @block.gpsimd
        def _(pool):
            pool = PlainWaits(pool, passed)

            def step(n, s, r):
                pool.wait_ge(ss_done, n + 1)
                nc.gpsimd.tensor_scalar(ms[s][:], ss[s][:], 1.0 / D, EPS, ALU.mult, ALU.add).then_inc(ms_done, 1)
                pool.wait_ge(ms_done, n + 1)
                wait_slot(pool, y_done, n, 1, NS)
                nc.gpsimd.tensor_tensor(rs[s][:], ms[s][:], t["neg_half"][:], ALU.pow).then_inc(rs_done, 1)

            tiles(pool, step)

        @block.vector
        def _(dve):
            dve.wait_ge(g_loaded, 16)

            def step(n, s, r):
                dve.wait_ge(rs_done, n + 1)
                wait_slot(dve, stored[s], r, 16, 1)
                nc.vector.scalar_tensor_tensor(yt[s][:], xt[s][:], rs[s][:], fg[:], ALU.mult, ALU.mult)\
                    .then_inc(y_done, 1)

            tiles(dve, step)


_INS = ['x_prompt', 'x_sample', 'cache_ckv', 'cache_kpe', 'c', 'c_ctx', 'w_mod', 'b_mod', 'norm1_g', 'w_in',
        'q_norm_g', 'w_uq', 'kv_norm_g', 'w_ukv', 'w_fmix', 'w_out', 'norm2_g', 'w_router', 'w_e_gate',
        'w_e_up', 'w_e_down', 'final_g']
_OUTS = [('y_prompt', (1, CTX, D)), ('y_sample', (1, LAT, D)), ('state_ckv', (1, 1, CTX, KVL)),
         ('state_kpe', (1, 1, CTX, ROPE))]
_SCRATCH = [('s_gates', (2, 2, D)), ('s_state', (NTOK, KVL + ROPE)), ('s_q', (NT, QK, H, P)),
            ('s_acc', (NTOK, D)), ('s_rows', (NTOK, ROWW))]


def constants():
    f32 = np.float32
    k = {'k_ident': np.eye(P, dtype=f32)}
    nf = ROPE // 4
    inv = (f32(10000.0) ** (-np.arange(nf, dtype=f32) / f32(nf))).astype(f32)
    rows = np.repeat(np.arange(LAT // 64, dtype=f32), 64)
    cols = np.tile(np.arange(64, dtype=f32), LAT // 64)
    ang = np.concatenate([rows[:, None] * inv, cols[:, None] * inv], axis=-1).astype(f32)
    ang = np.concatenate([np.zeros((CTX, 2 * nf), f32), ang]).astype(np.float64)
    cos, sin = np.cos(ang).astype(f32), np.sin(ang).astype(f32)
    k['k_rope_cos'] = np.concatenate([cos, cos], axis=1)
    k['k_rope_sin'] = np.concatenate([-sin, sin], axis=1)
    def dft(t, f):
        ang = 2 * np.pi * ((np.arange(t)[:, None] * np.asarray(f)[None, :]) % LAT) / LAT
        return np.cos(ang).astype(f32), np.sin(ang).astype(f32)

    k['k_cos_odd'], k['k_sin_odd'] = dft(LAT // 2, np.arange(1, LAT // 2, 2))
    k['k_cos_r0'], k['k_sin_r0'] = dft(LAT // 4, np.arange(0, LAT // 2 + 1, 4))
    k['k_cos_r2'], k['k_sin_r2'] = dft(LAT // 4, np.arange(2, LAT // 2, 4))
    g = 64
    ang = 2 * np.pi * ((np.arange(g)[:, None] * np.arange(g)[None, :]) % g) / g
    blk = np.zeros((P, 2, 2, P))
    for kind, n in enumerate((CTX, LAT)):
        for q, m in enumerate((np.cos(ang), np.sin(ang))):
            for b in range(2):
                blk[b * g:(b + 1) * g, kind, q, b * g:(b + 1) * g] = m / np.sqrt(float(n) * g)
    k['k_chan'] = blk.astype(f32)
    k['k_before'] = np.triu(np.ones((P, P), f32), 1)
    k['k_slots'] = np.arange(CAP_L, dtype=f32)
    k['k_tile_part'] = np.stack([np.arange(NTOK) // P, np.arange(NTOK) % P], axis=1).astype(f32)
    return k


def kernel(**inputs):
    import concourse.bacc as _bacc
    from concourse.bass_utils import run_bass_kernel_spmd as _run

    nc = _bacc.Bacc("TRN2", target_bir_lowering=False, num_devices=1)
    arrays, aps = {}, {}
    host = {name: np.ascontiguousarray(inputs[name]) for name in _INS}
    host.update(constants())
    for name, v in host.items():
        arrays[f"in_{name}"] = v
        aps[name] = nc.dram_tensor(f"in_{name}", v.shape, mybir.dt.from_np(v.dtype), kind="ExternalInput").ap()
    for name, shape in _OUTS:
        aps[name] = nc.dram_tensor(f"out_{name}", shape, F32, kind="ExternalOutput").ap()
    for name, shape in _SCRATCH:
        aps[name] = nc.dram_tensor(name, shape, F32, kind="Internal").ap()
    program(nc, aps)
    r = _run(nc, [arrays], core_ids=[0])
    return tuple(r.results[0][f"out_{name}"] for name, _ in _OUTS)
```
